# Optimizing a Trainium2 kernel written in Bass

```python
import math, functools
import jax, jax.numpy as jnp
from jax import lax
import numpy as np

D_MODEL = 1024
BATCH = 1
SEQ = 512
DEPTH = 2
DEC_BATCH = 8
DEC_SEQ = 8
PAST_LEN = 4096
PAGE_SIZE = 128

HEAD_DIM = 64
RET_WIDTH = D_MODEL // 4
NSA_WIDTH = D_MODEL // 2
GDN_WIDTH = D_MODEL - RET_WIDTH - NSA_WIDTH
MIX_WIDTH = RET_WIDTH + NSA_WIDTH + GDN_WIDTH
RET_HEADS = RET_WIDTH // HEAD_DIM
NSA_HEADS = NSA_WIDTH // HEAD_DIM
NSA_KV_HEADS = 2
NSA_GROUP = NSA_HEADS // NSA_KV_HEADS
GDN_HEADS = GDN_WIDTH // HEAD_DIM
CMP_BLOCK = 32
CMP_STRIDE = 16
SEL_BLOCK = 64
N_SELECT = 16
WINDOW = 512
RET_CHUNK = 64
GDN_CHUNK = 64
CONV_WIDTH = 4
SEL_QBLK = 32
WIN_QBLK = 128
ROPE_THETA = 10000.0
EPS = 1e-6
N_CACHE_SLOTS = 4

PROJ_SPLITS = (
    ('ret_q', RET_WIDTH), ('ret_k', RET_WIDTH), ('ret_v', RET_WIDTH), ('ret_g', RET_WIDTH),
    ('nsa_q', NSA_WIDTH), ('nsa_kv', 6 * NSA_KV_HEADS * HEAD_DIM), ('nsa_gate', 3 * NSA_HEADS), ('nsa_g', NSA_WIDTH),
    ('gdn_qkv', 3 * GDN_WIDTH), ('gdn_beta', GDN_HEADS), ('gdn_a', GDN_HEADS), ('gdn_g', GDN_WIDTH),
)
PROJ_WIDTH = sum(w for _, w in PROJ_SPLITS)

kernel_name = 'hymba_retention_nsa_gdn_step'

def _split_proj(u):
    offs = [int(o) for o in np.cumsum([w for _, w in PROJ_SPLITS])[:-1]]
    return dict(zip([n for n, _ in PROJ_SPLITS], jnp.split(u, offs, axis=-1)))

def _rmsnorm(x, g):
    xf = x.astype(jnp.float32)
    y = xf * lax.rsqrt(jnp.mean(xf * xf, axis=-1, keepdims=True) + EPS)
    return (y * g.astype(jnp.float32)).astype(x.dtype)

def _head_layernorm(o, g):
    B, T = o.shape[:2]
    of = o.astype(jnp.float32)
    mu = jnp.mean(of, axis=-1, keepdims=True)
    var = jnp.mean(jnp.square(of - mu), axis=-1, keepdims=True)
    return ((of - mu) * lax.rsqrt(var + EPS)).reshape(B, T, -1) * g.astype(jnp.float32)

def _head_rmsnorm(o, g):
    B, T = o.shape[:2]
    of = o.astype(jnp.float32)
    y = of * lax.rsqrt(jnp.mean(of * of, axis=-1, keepdims=True) + EPS) * g.astype(jnp.float32)
    return y.reshape(B, T, -1)

def _l2norm(x):
    return x * lax.rsqrt(jnp.sum(x * x, axis=-1, keepdims=True) + EPS)

def _rope(x, pos):
    half = HEAD_DIM // 2
    inv = ROPE_THETA ** (-jnp.arange(half, dtype=jnp.float32) / half)
    ang = pos.astype(jnp.float32)[:, None] * inv[None, :]
    cos = jnp.cos(ang)[:, None, :]
    sin = jnp.sin(ang)[:, None, :]
    xf = x.astype(jnp.float32)
    x1, x2 = xf[..., :half], xf[..., half:]
    return jnp.concatenate([x1 * cos - x2 * sin, x2 * cos + x1 * sin], axis=-1).astype(x.dtype)

def _masked_softmax(s, mask):
    s = jnp.where(mask, s, -jnp.inf)
    m = jnp.max(s, axis=-1, keepdims=True)
    m = jnp.where(jnp.isfinite(m), m, 0.0)
    p = jnp.exp(s - m)
    return p / jnp.maximum(jnp.sum(p, axis=-1, keepdims=True), 1e-30)

def _retention(q, k, v, S0):
    B, T, H, D = q.shape
    c = math.gcd(T, RET_CHUNK)
    n = T // c
    lg = jnp.log1p(-jnp.exp2(-5.0 - jnp.arange(H, dtype=jnp.float32)))
    ii = jnp.arange(c, dtype=jnp.float32)
    rel = ii[:, None] - ii[None, :]
    dm = jnp.exp(jnp.where(rel[None] >= 0, rel[None] * lg[:, None, None], -jnp.inf))
    q_dec = jnp.exp((ii + 1.0)[:, None] * lg[None, :])
    k_dec = jnp.exp((c - 1.0 - ii)[:, None] * lg[None, :])
    s_dec = jnp.exp(c * lg)
    ch = lambda a: a.astype(jnp.float32).reshape(B, n, c, H, D).swapaxes(0, 1)

    def step(S, inp):
        qc, kc, vc = inp
        att = jnp.einsum('bihd,bjhd->bhij', qc, kc) * dm
        o = jnp.einsum('bhij,bjhe->bihe', att, vc) + jnp.einsum('bihd,bhde->bihe', qc, S) * q_dec[None, :, :, None]
        S = S * s_dec[None, :, None, None] + jnp.einsum('bjhd,bjhe->bhde', kc * k_dec[None, :, :, None], vc)
        return S, o

    S, o = lax.scan(step, S0.astype(jnp.float32), (ch(q), ch(k), ch(v)))
    return o.swapaxes(0, 1).reshape(B, T, H, D), S

def _gdn_chunked(q, k, v, beta, g, S0):
    B, T, H, D = q.shape
    c = math.gcd(T, GDN_CHUNK)
    n = T // c
    ch = lambda a: a.reshape(B, n, c, *a.shape[2:]).swapaxes(0, 1)
    ii = jnp.arange(c)
    tri = ii[:, None] >= ii[None, :]
    strict = ii[:, None] > ii[None, :]
    eye = jnp.eye(c, dtype=jnp.float32)

    def step(S, inp):
        qc, kc, vc, bc, gc = inp
        G = jnp.cumsum(gc, axis=1)
        Gh = jnp.swapaxes(G, 1, 2)
        L = jnp.exp(jnp.where(tri, Gh[..., :, None] - Gh[..., None, :], -jnp.inf))
        kb = kc * bc[..., None]
        A = eye + jnp.where(strict, jnp.einsum('bihd,bjhd->bhij', kb, kc) * L, 0.0)
        Tinv = lax.linalg.triangular_solve(A, jnp.broadcast_to(eye, A.shape), left_side=True, lower=True)
        u = jnp.einsum('bhij,bjhe->bihe', Tinv, vc * bc[..., None])
        w = jnp.einsum('bhij,bjhd->bihd', Tinv, kb * jnp.exp(G)[..., None])
        v_new = u - jnp.einsum('bihd,bhde->bihe', w, S)
        o = (jnp.einsum('bihd,bhde->bihe', qc * jnp.exp(G)[..., None], S)
             + jnp.einsum('bhij,bjhe->bihe', jnp.einsum('bihd,bjhd->bhij', qc, kc) * L, v_new))
        G_last = G[:, -1]
        S = (S * jnp.exp(G_last)[..., None, None]
             + jnp.einsum('bjhd,bjhe->bhde', kc * jnp.exp(G_last[:, None] - G)[..., None], v_new))
        return S, o

    S, o = lax.scan(step, S0.astype(jnp.float32), (ch(q), ch(k), ch(v), ch(beta), ch(g)))
    return o.swapaxes(0, 1).reshape(B, T, H, D), S

def _gated_delta(qkv_raw, beta_raw, a_raw, conv_buf, S0, conv_w, a_log, dt_bias):
    B, T, C = qkv_raw.shape
    xcat = jnp.concatenate([conv_buf.astype(qkv_raw.dtype), qkv_raw], axis=1)
    y = lax.conv_general_dilated(xcat, conv_w[:, None, :].astype(xcat.dtype), (1,), 'VALID',
                                 dimension_numbers=('NWC', 'WIO', 'NWC'), feature_group_count=C)
    y = jax.nn.silu(y.astype(jnp.float32))
    q, k, v = [a.reshape(B, T, GDN_HEADS, HEAD_DIM) for a in jnp.split(y, 3, axis=-1)]
    q = _l2norm(q) * (HEAD_DIM ** -0.5)
    k = _l2norm(k)
    beta = jax.nn.sigmoid(beta_raw.astype(jnp.float32))
    g = -jnp.exp(a_log.astype(jnp.float32)) * jax.nn.softplus(a_raw.astype(jnp.float32) + dt_bias.astype(jnp.float32))
    o, S = _gdn_chunked(q, k, v, beta, g, S0)
    return o, S, xcat[:, -(CONV_WIDTH - 1):]

def _compress(rows, w1, b1, w2):
    B, L, G, D = rows.shape
    n_seg = L // CMP_STRIDE
    r = CMP_BLOCK // CMP_STRIDE
    n_cmp = n_seg - r + 1
    seg = rows[:, :n_seg * CMP_STRIDE].reshape(B, n_seg, CMP_STRIDE, G, D)
    h = b1
    for i in range(r):
        h = h + jnp.einsum('bnsgd,sde->bnge', seg[:, i:i + n_cmp], w1[i * CMP_STRIDE:(i + 1) * CMP_STRIDE])
    return jnp.einsum('bnge,ef->bngf', jax.nn.silu(h), w2)

def _nsa_compressed(q, qpos, k_c, v_c):
    B, T, H, D = q.shape
    nc = k_c.shape[1]
    qg = q.reshape(B, T, NSA_KV_HEADS, NSA_GROUP, D)
    s = jnp.einsum('btgrd,bngd->btgrn', qg, k_c).astype(jnp.float32) * (HEAD_DIM ** -0.5)
    end = jnp.arange(nc) * CMP_STRIDE + (CMP_BLOCK - 1)
    mask = (end[None, :] <= qpos[:, None])[None, :, None, None, :]
    p = _masked_softmax(s, mask)
    o = jnp.einsum('btgrn,bngd->btgrd', p.astype(v_c.dtype), v_c).reshape(B, T, H, D)
    return o, jnp.sum(p, axis=3)

def _nsa_select(imp, qpos, n_blk):
    nc = imp.shape[-1]
    ci = jnp.arange(nc)[:, None] * CMP_STRIDE
    sj = jnp.arange(n_blk)[None, :] * SEL_BLOCK
    overlap = ((ci < sj + SEL_BLOCK) & (ci + CMP_BLOCK > sj)).astype(jnp.float32)
    score = jnp.einsum('btgn,nj->btgj', imp, overlap)
    jt = (qpos // SEL_BLOCK)[:, None]
    jj = jnp.arange(n_blk)[None, :]
    valid = jj <= jt
    forced = valid & ((jj == 0) | (jj == jt) | (jj == jt - 1))
    score = jnp.where(forced[None, :, None, :], jnp.inf, jnp.where(valid[None, :, None, :], score, -jnp.inf))
    _, idx = lax.top_k(score, min(N_SELECT, n_blk))
    return idx

def _block_positions(idx):
    return idx[..., None] * SEL_BLOCK + jnp.arange(SEL_BLOCK)

def _nsa_sel_attend(q, qpos, kg, vg, kpos):
    B, T, H, D = q.shape
    G = NSA_KV_HEADS
    kg = kg.reshape(B, T, G, -1, D)
    vg = vg.reshape(B, T, G, -1, D)
    kpos = kpos.reshape(B, T, G, -1)
    qg = q.reshape(B, T, G, NSA_GROUP, D)
    s = jnp.einsum('btgrd,btgld->btgrl', qg, kg).astype(jnp.float32) * (HEAD_DIM ** -0.5)
    mask = (kpos <= qpos[None, :, None, None])[:, :, :, None, :]
    p = _masked_softmax(s, mask)
    return jnp.einsum('btgrl,btgld->btgrd', p.astype(vg.dtype), vg).reshape(B, T, H, D)

def _window_attend(q, qpos, k, v, kpos):
    B, Tq, H, D = q.shape
    qg = q.reshape(B, Tq, NSA_KV_HEADS, NSA_GROUP, D)
    s = jnp.einsum('btgrd,blgd->btgrl', qg, k).astype(jnp.float32) * (HEAD_DIM ** -0.5)
    dist = qpos[:, None] - kpos[None, :]
    mask = ((dist >= 0) & (dist < WINDOW) & (kpos[None, :] >= 0))[None, :, None, None, :]
    p = _masked_softmax(s, mask)
    return jnp.einsum('btgrl,blgd->btgrd', p.astype(v.dtype), v).reshape(B, Tq, H, D)

def _nsa_prompt(q, q_rot, rows, win_rows, pos, *, cmp):
    B, T, H, D = q.shape
    G = NSA_KV_HEADS
    w1, b1, w2 = cmp
    k_c = _compress(rows[:, :, 0], w1[0], b1[0], w2[0])
    v_c = _compress(rows[:, :, 1], w1[1], b1[1], w2[1])
    o_cmp, imp = _nsa_compressed(q, pos, k_c, v_c)
    idx = _nsa_select(imp, pos, -(-T // SEL_BLOCK))
    cq = math.gcd(T, SEL_QBLK)
    nq = T // cq
    chunk = lambda a: a.reshape(B, nq, cq, *a.shape[2:]).swapaxes(0, 1)
    bi = jnp.arange(B)[:, None, None, None, None]
    gi = jnp.arange(G)[None, None, :, None, None]

    def sel_chunk(inp):
        qc, pc, ic = inp
        kpos = _block_positions(ic)
        r = jnp.minimum(kpos, T - 1)
        kg = rows[bi, r, 2, gi]
        vg = rows[bi, r, 3, gi]
        return _nsa_sel_attend(qc, pc, kg, vg, kpos)

    o_sel = lax.map(sel_chunk, (chunk(q_rot), pos.reshape(nq, cq), chunk(idx)))
    o_sel = o_sel.swapaxes(0, 1).reshape(B, T, H, D)
    cw = math.gcd(T, WIN_QBLK)
    nb = T // cw
    pad = ((0, 0), (WINDOW, 0), (0, 0), (0, 0))
    kpad = jnp.pad(win_rows[:, :, 0], pad)
    vpad = jnp.pad(win_rows[:, :, 1], pad)

    def win_chunk(inp):
        b, qc = inp
        s0 = b * cw
        kc = lax.dynamic_slice_in_dim(kpad, s0, WINDOW + cw, axis=1)
        vc = lax.dynamic_slice_in_dim(vpad, s0, WINDOW + cw, axis=1)
        kpos = s0 - WINDOW + jnp.arange(WINDOW + cw)
        return _window_attend(qc, s0 + jnp.arange(cw), kc, vc, kpos)

    qb = q_rot.reshape(B, nb, cw, H, D).swapaxes(0, 1)
    o_win = lax.map(win_chunk, (jnp.arange(nb), qb)).swapaxes(0, 1).reshape(B, T, H, D)
    return o_cmp, o_sel, o_win, win_rows[:, T - min(WINDOW, T):]

def _nsa_sample(q, q_rot, rows, win_rows, pos, *, cmp, cache, layer, page_table, win_buf):
    B, T, H, D = q.shape
    G = NSA_KV_HEADS
    w1, b1, w2 = cmp
    past_len = page_table.shape[1] * PAGE_SIZE
    past = cache[layer, page_table, :, :2]
    past = past.reshape(B, past_len, 2, G, D).astype(rows.dtype)
    cmp_rows = jnp.concatenate([past, rows[:, :, :2]], axis=1)
    k_c = _compress(cmp_rows[:, :, 0], w1[0], b1[0], w2[0])
    v_c = _compress(cmp_rows[:, :, 1], w1[1], b1[1], w2[1])
    o_cmp, imp = _nsa_compressed(q, pos, k_c, v_c)
    L = past_len + T
    idx = _nsa_select(imp, pos, -(-L // SEL_BLOCK))
    kpos = _block_positions(idx)
    bi = jnp.arange(B)[:, None, None, None, None]
    gi = jnp.arange(G)[None, None, :, None, None]
    pp = jnp.minimum(kpos, past_len - 1)
    phys = page_table[bi, pp // PAGE_SIZE]
    off = pp % PAGE_SIZE
    k_past = cache[layer, phys, off, 2, gi].astype(rows.dtype)
    v_past = cache[layer, phys, off, 3, gi].astype(rows.dtype)
    nr = jnp.clip(kpos - past_len, 0, T - 1)
    is_new = (kpos >= past_len)[..., None]
    kg = jnp.where(is_new, rows[bi, nr, 2, gi], k_past)
    vg = jnp.where(is_new, rows[bi, nr, 3, gi], v_past)
    o_sel = _nsa_sel_attend(q_rot, pos, kg, vg, kpos)
    wb = win_buf.shape[1]
    keys = jnp.concatenate([win_buf.astype(win_rows.dtype), win_rows], axis=1)
    kpos_w = past_len - wb + jnp.arange(wb + T)
    o_win = _window_attend(q_rot, pos, keys[:, :, 0], keys[:, :, 1], kpos_w)
    return o_cmp, o_sel, o_win, keys[:, -wb:]

def _layer(x, pos, lp, nsa_fn, ret_state, gdn_state, conv_buf):
    B, T, _ = x.shape
    h = _rmsnorm(x, lp['norm_pre'])
    pr = _split_proj(h @ lp['w_in'])
    heads = lambda a: a.reshape(B, T, -1, HEAD_DIM)
    rq = _rope(heads(pr['ret_q']), pos)
    rk = _rope(heads(pr['ret_k']), pos) * (HEAD_DIM ** -0.5)
    ro, ret_new = _retention(rq, rk, heads(pr['ret_v']), ret_state)
    ro = _head_layernorm(ro, lp['ret_gn']) * jax.nn.silu(pr['ret_g'].astype(jnp.float32))
    q = heads(pr['nsa_q'])
    kv = pr['nsa_kv'].reshape(B, T, 6, NSA_KV_HEADS, HEAD_DIM)
    rows = jnp.stack([kv[:, :, 0], kv[:, :, 1], _rope(kv[:, :, 2], pos), kv[:, :, 3]], axis=2)
    win_rows = jnp.stack([_rope(kv[:, :, 4], pos), kv[:, :, 5]], axis=2)
    o_cmp, o_sel, o_win, win_new = nsa_fn(q, _rope(q, pos), rows, win_rows, pos)
    gate = jax.nn.sigmoid(pr['nsa_gate'].astype(jnp.float32)).reshape(B, T, 3, NSA_HEADS, 1)
    no = gate[:, :, 0] * o_cmp + gate[:, :, 1] * o_sel + gate[:, :, 2] * o_win
    no = no.reshape(B, T, NSA_WIDTH) * jax.nn.silu(pr['nsa_g'].astype(jnp.float32))
    go, gdn_new, conv_new = _gated_delta(pr['gdn_qkv'], pr['gdn_beta'], pr['gdn_a'], conv_buf, gdn_state,
                                         lp['gdn_conv'], lp['gdn_a_log'], lp['gdn_dt_bias'])
    go = _head_rmsnorm(go, lp['gdn_norm']) * jax.nn.silu(pr['gdn_g'].astype(jnp.float32))
    mix = jnp.concatenate([ro, no, go], axis=-1).astype(x.dtype)
    y = x + _rmsnorm(mix @ lp['w_out'], lp['norm_post'])
    return y, (rows, win_new, ret_new, gdn_new, conv_new)

def setup_inputs(seed: int = 0) -> dict:
    key = jax.random.key(seed)
    ks = jax.random.split(key, 24)
    n_pages = PAST_LEN // PAGE_SIZE
    n_used = DEC_BATCH * n_pages
    n_phys = (5 * n_used + 3) // 4
    win_buf = min(WINDOW, PAST_LEN)
    nrm = lambda k, shape, s: jax.random.normal(k, shape, jnp.float32) * s
    dt = jnp.exp(jax.random.uniform(ks[16], (DEPTH, GDN_HEADS), jnp.float32, math.log(1e-3), math.log(1e-1)))
    return {
        'x_prompt': nrm(ks[0], (BATCH, SEQ, D_MODEL), 1.0),
        'x_sample': nrm(ks[1], (DEC_BATCH, DEC_SEQ, D_MODEL), 1.0),
        'cache_nsa_kv': nrm(ks[2], (DEPTH, n_phys, PAGE_SIZE, N_CACHE_SLOTS, NSA_KV_HEADS, HEAD_DIM), 1.0),
        'page_table': jax.random.permutation(ks[3], n_phys)[:n_used].reshape(DEC_BATCH, n_pages).astype(jnp.int32),
        'state_nsa_win': nrm(ks[4], (DEPTH, DEC_BATCH, win_buf, 2, NSA_KV_HEADS, HEAD_DIM), 1.0),
        'state_ret': nrm(ks[5], (DEPTH, DEC_BATCH, RET_HEADS, HEAD_DIM, HEAD_DIM), 0.5),
        'state_gdn': nrm(ks[6], (DEPTH, DEC_BATCH, GDN_HEADS, HEAD_DIM, HEAD_DIM), 0.1),
        'state_gdn_conv': nrm(ks[7], (DEPTH, DEC_BATCH, CONV_WIDTH - 1, 3 * GDN_WIDTH), 1.0),
        'w_in': nrm(ks[8], (DEPTH, D_MODEL, PROJ_WIDTH), D_MODEL ** -0.5),
        'w_out': nrm(ks[9], (DEPTH, MIX_WIDTH, D_MODEL), MIX_WIDTH ** -0.5),
        'norm_pre': 1.0 + nrm(ks[10], (DEPTH, D_MODEL), 0.02),
        'norm_post': 1.0 + nrm(ks[11], (DEPTH, D_MODEL), 0.02),
        'ret_gn': 1.0 + nrm(ks[12], (DEPTH, RET_WIDTH), 0.02),
        'gdn_norm': 1.0 + nrm(ks[13], (DEPTH, HEAD_DIM), 0.02),
        'gdn_conv': nrm(ks[14], (DEPTH, CONV_WIDTH, 3 * GDN_WIDTH), CONV_WIDTH ** -0.5),
        'gdn_a_log': jnp.log(jax.random.uniform(ks[15], (DEPTH, GDN_HEADS), jnp.float32, 1.0, 16.0)),
        'gdn_dt_bias': dt + jnp.log(-jnp.expm1(-dt)),
        'cmp_w1': nrm(ks[17], (DEPTH, 2, CMP_BLOCK, HEAD_DIM, HEAD_DIM), (CMP_BLOCK * HEAD_DIM) ** -0.5),
        'cmp_b1': nrm(ks[18], (DEPTH, 2, HEAD_DIM), 0.02),
        'cmp_w2': nrm(ks[19], (DEPTH, 2, HEAD_DIM, HEAD_DIM), HEAD_DIM ** -0.5),
    }

def reference(x_prompt, x_sample, cache_nsa_kv, page_table, state_nsa_win, state_ret, state_gdn, state_gdn_conv,
              w_in, w_out, norm_pre, norm_post, ret_gn, gdn_norm, gdn_conv, gdn_a_log, gdn_dt_bias,
              cmp_w1, cmp_b1, cmp_w2):
    Bp, T, _ = x_prompt.shape
    Bs, Ts, _ = x_sample.shape
    past_len = page_table.shape[1] * PAGE_SIZE
    pos_p = jnp.arange(T, dtype=jnp.int32)
    pos_s = past_len + jnp.arange(Ts, dtype=jnp.int32)
    yp, ys = x_prompt, x_sample
    st_p, st_s = [], []
    for l in range(DEPTH):
        lp = {'w_in': w_in[l], 'w_out': w_out[l], 'norm_pre': norm_pre[l], 'norm_post': norm_post[l],
              'ret_gn': ret_gn[l], 'gdn_norm': gdn_norm[l], 'gdn_conv': gdn_conv[l],
              'gdn_a_log': gdn_a_log[l], 'gdn_dt_bias': gdn_dt_bias[l]}
        cmp = (cmp_w1[l], cmp_b1[l], cmp_w2[l])
        yp, sp = _layer(yp, pos_p, lp, functools.partial(_nsa_prompt, cmp=cmp),
                        jnp.zeros((Bp, RET_HEADS, HEAD_DIM, HEAD_DIM), jnp.float32),
                        jnp.zeros((Bp, GDN_HEADS, HEAD_DIM, HEAD_DIM), jnp.float32),
                        jnp.zeros((Bp, CONV_WIDTH - 1, 3 * GDN_WIDTH), x_prompt.dtype))
        ys, ss = _layer(ys, pos_s, lp,
                        functools.partial(_nsa_sample, cmp=cmp, cache=cache_nsa_kv, layer=l,
                                          page_table=page_table, win_buf=state_nsa_win[l]),
                        state_ret[l], state_gdn[l], state_gdn_conv[l])
        st_p.append(sp)
        st_s.append(ss)
    stk = lambda sts, i: jnp.stack([s[i] for s in sts])
    return (yp, ys, stk(st_p, 0), stk(st_s, 0), stk(st_p, 1), stk(st_s, 1), stk(st_p, 2), stk(st_s, 2),
            stk(st_p, 3), stk(st_s, 3), stk(st_p, 4), stk(st_s, 4))


_drawn_inputs = setup_inputs


def setup_inputs(seed=0):
    import zlib

    import numpy as np

    out = dict(_drawn_inputs(seed))
    spreads = {}
    factors = {'ret_gn': 12.797, 'gdn_norm': 13.052, 'cmp_b1': 37.23, 'cache_nsa_kv': 5.13}
    for name, (base, spread) in spreads.items():
        noise = np.random.default_rng([zlib.crc32(name.encode()), seed]).standard_normal(out[name].shape)
        drawn = base * np.exp(spread * noise) if base else spread * noise
        out[name] = __import__('jax').numpy.asarray(drawn.astype(out[name].dtype))
    for name, factor in factors.items():
        out[name] = (out[name] * factor).astype(out[name].dtype)
    return out
```

```python
import concourse.bass as bass
from concourse import mybir
from contextlib import ExitStack, contextmanager
import numpy as np

F32 = mybir.dt.float32
BF16 = mybir.dt.bfloat16
I32 = mybir.dt.int32
ALU = mybir.AluOpType
ACT = mybir.ActivationFunctionType
AX = mybir.AxisListType

D = 1024
SEQ = 512
DEPTH = 2
NB, NT = 8, 8
PAST = 4096
PAGE = 128
HD = 64
H4 = 4
NH, G, R = 8, 2, 4
WIN = 512
NPHYS = 320
NPAGE = PAST // PAGE
P = 128
KD = D // P
NTILE = 5
ROWS = [P, P, P, P, NB * NT]
CONV = 4
CW = 768
EPS = 1e-6
NEG = -1e30
SCALE = HD ** -0.5
RQ, RK, RV, RG = 0, 256, 512, 768
NQ, NKV, NGATE, NG = 1024, 1536, 2304, 2328
GQKV, GB, GA, GG = 2840, 3608, 3612, 3616
PROJ = 3872
SEL_BLOCK = 64
NSEL = 16
NBLK = PAST // SEL_BLOCK + 1
PAIRS = 2
GT = PAST // (P * PAIRS)
SEG = 16
NSEG = PAST // SEG
NSEGP = SEQ // SEG
NCP = NSEGP - 1
COLS = NH * NT
NKEYG = 2 * GT + 1



def constants():
    c = {}
    i = np.arange(P)
    c['ident'] = np.eye(P)
    half = HD // 2
    inv = (np.float32(10000.0) ** (-np.arange(half, dtype=np.float32) / np.float32(half))).astype(np.float32)
    pos = np.zeros((P, NTILE), np.float32)
    for t in range(4):
        pos[:, t] = t * P + i
    pos[:, 4] = PAST + i % NT
    ang = (pos[:, :, None] * inv[None, None, :]).astype(np.float32).astype(np.float64)
    c['cos'] = np.cos(ang)
    c['sin'] = np.sin(ang)
    blk = [np.ones((P, P)), np.zeros((P, P))]
    j = i[:, None]
    k = i[None, :]
    blk[1][:64, :64] = (j[:64] // NT == k[:, :64] // NT)
    c['same'] = np.stack(blk, 1)
    c['tri'] = np.stack([b * (j <= k) for b in blk], 1)
    c['neg'] = (1 - c['tri']) * NEG
    lev = np.zeros((P, 7, P))
    for s in range(7):
        w = 1 << s
        lev[:, s] = (j // (2 * w) == k // (2 * w)) & (j % (2 * w) < w) & (k % (2 * w) >= w)
    c['level'] = lev
    c['pair'] = (j // HD == k // HD).astype(np.float64)
    lg = np.log1p(-np.exp2(-5.0 - np.arange(H4)))
    rel = (k - j).astype(np.float64)
    for n, b in enumerate(blk):
        c[f'dm{n}'] = np.stack([np.where(b * (j <= k) > 0, np.exp(np.maximum(rel, 0) * g), 0) * SCALE for g in lg], 1)
    step = [i, i % NT]
    last = [P, NT]
    c['qdec'] = np.stack([np.exp((s[:, None] + 1) * lg[None]) for s in step], 1)
    c['kdec'] = np.stack([np.exp((n - 1 - s[:, None]) * lg[None]) * SCALE for s, n in zip(step, last)], 1)
    sd = np.zeros((P, 2, 2))
    for n in range(2):
        for hp in range(2):
            sd[:, n, hp] = np.exp(last[n] * lg[2 * hp + i // HD])
    c['sdec'] = sd
    own = np.zeros((P, NB, 64))
    for b in range(NB):
        own[:, b] = (np.arange(64)[None] // NT == b)
    c['own'] = own
    c['ownrow'] = (i[:, None] // NT == np.arange(NB)[None, :])
    ci = (np.arange(2 * P) * SEG)[:, None]
    sj = (np.arange(NBLK) * SEL_BLOCK)[None, :]
    ov = ((ci < sj + SEL_BLOCK) & (ci + 2 * SEG > sj)).astype(np.float64)
    ov[255] = 0
    c['overlap'] = np.stack([ov[:P], ov[P:]], 1)
    force = np.zeros((P, NBLK))
    force[:, [0, NBLK - 2, NBLK - 1]] = -NEG
    c['force'] = force
    return {n: np.ascontiguousarray(a, np.float32).reshape(P, -1) for n, a in c.items()}


def bf_constants():
    c = {}
    i = np.arange(P)
    c['identb'] = np.eye(P)
    c['causal'] = np.where(i[None] <= i[:, None], 0, NEG)
    cm = np.zeros((P, 4, 32))
    for t in range(4):
        cm[:, t] = np.where((np.arange(32) * SEG + 2 * SEG - 1)[None] <= (t * P + i)[:, None], 0, NEG)
    c['cmask'] = cm
    be = np.zeros((P, GT, P))
    for t in range(GT):
        be[:, t] = (i[:, None] == 4 * t + i[None] // 32)
    c['blockof'] = be
    stepc = (np.arange(COLS) % NT)[None]
    c['newmask'] = np.where(i[:, None] <= stepc, 0, NEG)
    c['winmask'] = np.where(i[:, None] > stepc, 0, NEG)
    c['padmask'] = np.where(i[:, None] < P - 1, 0, NEG) + 0 * stepc
    return {n: np.ascontiguousarray(a, np.float32).reshape(P, -1) for n, a in c.items()}


def layout(c):
    at, out = 0, {}
    for n, a in c.items():
        out[n] = (at, a.shape[1])
        at += a.shape[1]
    return out, at



class Steps:

    def __init__(self, sem, names):
        self.sem, self.names, self.at = sem, list(names), {n: i + 1 for i, n in enumerate(names)}
        assert len(self.at) == len(self.names)
        self.next = 0

    def done(self, eng, name, ins):
        assert self.next < len(self.names) and self.names[self.next] == name, (name, self.names[self.next:self.next + 2])
        self.next += 1
        return ins.then_inc(self.sem, 1)

    def link(self, eng, name, ins):
        self.done(eng, name, ins)
        eng.wait_ge(self.sem, self.next)

    def wait(self, eng, name):
        eng.wait_ge(self.sem, self.at[name])


def b_(ap, axis, shape):
    return ap.unsqueeze(axis).broadcast_to(shape)


def build(nc, A, O):
    es = ExitStack()

    used = []

    def sb(scope, name, shape, dt=F32):
        used.append(name)
        name = name if used.count(name) == 1 else f"{name}_{used.count(name)}"
        return scope.enter_context(nc.sbuf_tensor(name, shape, dt))

    @contextmanager
    def stage(sems):
        with ExitStack() as st:
            got = [st.enter_context(nc.semaphore(n)) for n in sems]
            with nc.Block() as block:
                yield block, got
            for s in got:
                nc.gpsimd.sem_clear(s)
            nc.all_engine_barrier()

    cl, cn = layout(constants())
    bl, bn = layout(bf_constants())

    with es:
        X = sb(es, "X", [P, NTILE, D])
        MIX = sb(es, "MIX", [P, NTILE, D])
        CF = sb(es, "CF", [P, cn])
        CB = sb(es, "CB", [P, bn], BF16)
        US = sb(es, "US", [P, PROJ])
        QRS = sb(es, "QRS", [P, 2, NH * HD])
        ones = sb(es, "ones", [P, P])
        W1 = sb(es, "W1", [P, 2, SEG // PAIRS, P])
        W2 = sb(es, "W2", [HD, 2, G, P])
        B1 = sb(es, "B1", [HD, 2])
        eps = sb(es, "eps", [P, 1])

        def cf(n, shape=None):
            o, w = cl[n]
            ap = CF[:, o:o + w]
            if shape:
                ap = ap.rearrange("p (a b) -> p a b", b=shape)
            return ap

        def cb(n, shape=None):
            o, w = bl[n]
            ap = CB[:, o:o + w]
            if shape:
                ap = ap.rearrange("p (a b) -> p a b", b=shape)
            return ap

        ident = cf('ident')
        bank = [es.enter_context(nc.psum_tensor(f"bank{i}", [P, 512], F32)) for i in range(8)]

        def bk(i, a=None):
            ap = bank[i][:, :]
            return ap if a is None else ap.rearrange("p (a b) -> p a b", a=a)

        with stage(["loaded", "filled"]) as (block, (loaded, filled)):
            @block.sync
            def _(sp):
                sp.dma_start(CF[:, :], A['cf']).then_inc(loaded, 16)
                sp.dma_start(CB[:, :], A['cb']).then_inc(loaded, 16)
                sp.dma_start(X[:, 0:4, :], A['x_prompt'][0].rearrange("(t p) d -> p t d", p=P)).then_inc(loaded, 16)
                sp.dma_start(X[0:64, 4, :], A['x_sample'].rearrange("b t d -> (b t) d")).then_inc(loaded, 16)
                sp.wait_ge(loaded, 64)

            @block.vector
            def _(dve):
                nc.vector.memset(ones[:, :], 1.0).then_inc(filled, 1)
                nc.vector.memset(eps[:, :], EPS).then_inc(filled, 1)
                dve.wait_ge(filled, 2)

        with nc.Fori(0, DEPTH) as l:
            layer(nc, A, O, l, sb, stage, dict(X=X, MIX=MIX, US=US, QRS=QRS, ones=ones, eps=eps, cf=cf, cb=cb,
                                               ident=ident, bk=bk, nc=nc, W1=W1, W2=W2, B1=B1))

        with stage(["written"]) as (block, (written,)):
            @block.sync
            def _(sp):
                sp.dma_start(O['y_prompt'][0].rearrange("(t p) d -> p t d", p=P), X[:, 0:4, :]).then_inc(written, 16)
                sp.dma_start(O['y_sample'].rearrange("b t d -> (b t) d"), X[0:64, 4, :]).then_inc(written, 16)
                sp.wait_ge(written, 32)


def layer(nc, A, O, l, sb, stage, v):
    with ExitStack() as scope:
        UP = sb(scope, "UP", [P, 4, PROJ])
        U = [UP[:, t, :] for t in range(4)] + [v['US'][0:64, :]]
        project(nc, A, l, sb, stage, v, U)
        with ExitStack() as s2:
            Y = [u[:, GQKV:GQKV + CW] for u in U]
            g_log = sb(s2, "g_log", [P, NTILE, H4])
            with ExitStack() as s3:
                pointwise(nc, A, O, l, s3, sb, stage, v, U, Y, g_log)
            with ExitStack() as s3:
                retention(nc, A, O, l, s3, sb, stage, v, U)
            with ExitStack() as s3:
                delta(nc, A, O, l, s3, sb, stage, v, U, Y, g_log)
        with ExitStack() as s2:
            prompt_attention(nc, A, O, l, s2, sb, stage, v, U)
    with ExitStack() as scope:
        sample_attention(nc, A, O, l, scope, sb, stage, v)
    with ExitStack() as scope:
        out_project(nc, A, l, scope, sb, stage, v)


def project(nc, A, l, sb, stage, v, U):
    X, ident = v['X'], v['ident']
    chunks = [(c, min(c + 512, PROJ)) for c in range(0, PROJ, 512)]
    NC = len(chunks)
    with ExitStack() as scope:
        hT = sb(scope, "hT", [P, KD, 4 * P + 64])
        W = sb(scope, "W", [P, 2, KD, 512])
        ss = sb(scope, "ss", [P, NTILE])
        xn = sb(scope, "xn", [P, D])
        gpre = sb(scope, "gpre", [P, KD])
        with stage(["w0", "w1", "gain", "act_s", "dve_s", "pe_s", "e_act", "e_dve", "chunk_done", "proj_done"]) as \
                (block, (w0, w1, gain, act_s, dve_s, pe_s, e_act, e_dve, chunk_done, proj_done)):
            wsem = [w0, w1]
            act = Steps(act_s, [f"{n}{t}" for t in range(NTILE) for n in ("sq", "rt")])
            dve = Steps(dve_s, [f"{n}{t}" for t in range(NTILE) for n in ("rs", "xn", "h0", "h1")])
            pe = Steps(pe_s, [f"T{t}" for t in range(NTILE)])
            wv = A['w_in'][l].rearrange("(k p) c -> p k c", p=P)

            @block.sync
            def _(e):
                e.dma_start(gpre[:, :], A['norm_pre'][l].rearrange("(k p) -> p k", p=P),
                            allow_slow_non_contiguous=True).then_inc(gain, 16)
                for c, (a, b) in enumerate(chunks):
                    if c >= 2:
                        e.wait_ge(chunk_done, c - 1)
                    e.dma_start(W[:, c % 2, :, 0:b - a], wv[:, :, a:b]).then_inc(wsem[c % 2], 16)

            def evacuate(e, u):
                c, t = divmod(u, NTILE)
                a, b = chunks[c]
                e.wait_ge(proj_done, u + 1)
                return U[t][:, a:b], v['bk'](4 + u % 4)[0:ROWS[t], 0:b - a]

            @block.scalar
            def _(e):
                for t in range(NTILE):
                    n = ROWS[t]
                    if t:
                        dve.wait(e, f"xn{t-1}")
                        pe.wait(e, f"T{t-1}")
                    act.link(e, f"sq{t}", nc.scalar.activation(xn[0:n, :], X[0:n, t, :], ACT.Square, accum_out=ss[0:n, t:t + 1]))
                    act.link(e, f"rt{t}", nc.scalar.activation(ss[0:n, t:t + 1], ss[0:n, t:t + 1], ACT.Sqrt,
                                                               scale=1.0 / D, bias=v['eps'][0:n, :]))
                for u in range(0, NC * NTILE, 2):
                    o, i = evacuate(e, u)
                    nc.scalar.activation(o, i, ACT.Copy).then_inc(e_act, 1)

            @block.vector
            def _(e):
                e.wait_ge(gain, 16)
                for t in range(NTILE):
                    n = ROWS[t]
                    act.wait(e, f"rt{t}")
                    dve.link(e, f"rs{t}", nc.vector.reciprocal(ss[0:n, t:t + 1], ss[0:n, t:t + 1]))
                    dve.link(e, f"xn{t}", nc.vector.tensor_scalar(xn[0:n, :], X[0:n, t, :], ss[0:n, t:t + 1], None, ALU.mult))
                    pe.wait(e, f"T{t}")
                    for h in range(2):
                        dve.done(e, f"h{h}{t}", nc.vector.tensor_tensor(
                            hT[:, 4 * h:4 * h + 4, t * P:t * P + n], v['bk'](2 * (t % 2) + h, 4)[:, :, 0:n],
                            b_(gpre[:, 4 * h:4 * h + 4], 2, [P, 4, n]), ALU.mult))
                for u in range(1, NC * NTILE, 2):
                    o, i = evacuate(e, u)
                    nc.vector.tensor_copy(o, i).then_inc(e_dve, 1)

            @block.tensor
            def _(e):
                for t in range(NTILE):
                    n = ROWS[t]
                    dve.wait(e, f"xn{t}")
                    if t >= 2:
                        dve.wait(e, f"h1{t-2}")
                    for k in range(KD):
                        mm = nc.tensor.transpose(v['bk'](2 * (t % 2) + k // 4, 4)[:, k % 4, 0:n],
                                                 xn[0:n, k * P:(k + 1) * P], ident[0:n, 0:n])
                    pe.done(e, f"T{t}", mm)
                dve.wait(e, f"h1{NTILE-1}")
                u = 0
                for c, (a, b) in enumerate(chunks):
                    e.wait_ge(wsem[c % 2], 16 * (c // 2 + 1))
                    for t in range(NTILE):
                        if u >= 4:
                            e.wait_ge(e_dve if (u - 4) % 2 else e_act, (u - 4) // 2 + 1)
                        for k in range(KD):
                            mm = nc.tensor.matmul(v['bk'](4 + u % 4)[0:ROWS[t], 0:b - a], hT[:, k, t * P:t * P + ROWS[t]],
                                                  W[:, c % 2, k, 0:b - a], start=(k == 0), stop=(k == KD - 1))
                        mm.then_inc(proj_done, 1)
                        u += 1
                    nc.tensor.matmul(v['bk'](0)[0:1, 0:1], ident[:, 0:1], ident[:, 0:1], start=True, stop=True).then_inc(chunk_done, 1)


def pointwise(nc, A, O, l, scope, sb, stage, v, U, Y, g_log):
    cw = sb(scope, "cw", [P, CONV, CW])
    XS = sb(scope, "XS", [P, CONV - 1, CW])
    QR = sb(scope, "QR", [P, 2, 512])
    ta = sb(scope, "ta", [P, CW])
    tb = sb(scope, "tb", [P, CW])
    alog = sb(scope, "alog", [P, H4])
    dtb = sb(scope, "dtb", [P, H4])
    sp_ = sb(scope, "sp_", [P, 3, H4])
    nrm = sb(scope, "nrm", [P, 8])
    zero = sb(scope, "zero", [CONV - 1, CW])
    cos, sin = v['cf']('cos', 32), v['cf']('sin', 32)
    names = []
    for t in range(NTILE):
        for r in ("rq", "nq", "kv"):
            names += [f"{r}{x}{t}" for x in ("ab12" if r != "nq" else "ab12c")]
        names += [f"{x}{t}" for x in ("a1", "mx", "sg", "gl", "c0", "c1", "c1a", "c2", "c2a", "c3", "c3a", "s2", "ss",
                                      "rc", "q8", "nm")]
    with stage(["dve_s", "act_s", "par", "raw", "shift", "rot", "outs"]) as (block, (dve_s, act_s, par, raw, shift, rot, outs)):
        dve = Steps(dve_s, ["zero", "al"] + names)
        act = Steps(act_s, ["al"] + [f"{x}{t}" for t in range(NTILE) for x in ("rg", "ng", "gg", "gt", "bt", "ab", "ex", "ln", "ys", "sq")])
        XP, XC = A['conv_p'], A['conv_s']

        @block.sync
        def _(e):
            e.dma_start(cw[:, :, :].rearrange("p a b -> p (a b)"),
                        A['gdn_conv'][l].rearrange("a b -> (a b)").partition_broadcast(P)).then_inc(par, 16)
            e.dma_start(alog[:, :], A['gdn_a_log'][l].partition_broadcast(P)).then_inc(par, 16)
            e.dma_start(dtb[:, :], A['gdn_dt_bias'][l].partition_broadcast(P)).then_inc(par, 16)
            dve.wait(e, "zero")
            e.dma_start(XP[0:3, :], zero[:, :]).then_inc(raw, 16)
            for t in range(4):
                e.dma_start(XP[3 + t * P:3 + (t + 1) * P, :], U[t][:, GQKV:GQKV + CW]).then_inc(raw, 16)
            e.dma_start(XC[:, 0:3, :], A['state_gdn_conv'][l]).then_inc(raw, 16)
            e.dma_start(XC[:, 3:3 + NT, :], U[4][:, GQKV:GQKV + CW]).then_inc(raw, 16)
            e.wait_ge(raw, 7 * 16)
            e.dma_start(O['conv_prompt'][l, 0], XP[SEQ:SEQ + 3, :]).then_inc(outs, 16)
            e.dma_start(O['conv_sample'][l], XC[:, NT:NT + 3, :]).then_inc(outs, 16)
            nout = 2
            for t in range(NTILE):
                if t:
                    dve.wait(e, f"c3a{t-1}")
                for k in range(1, 4):
                    src = XP[3 - k + t * P:3 - k + (t + 1) * P, :] if t < 4 else XC[:, 3 - k:3 - k + NT, :]
                    e.dma_start(XS[0:ROWS[t], k - 1, :], src).then_inc(shift, 16)
                dve.wait(e, f"kv2{t}")
                n = ROWS[t]
                if t < 4:
                    kvo = O['kv_prompt'][l, 0].rearrange("s a g d -> s (a g d)")[t * P:(t + 1) * P]
                    wno = O['win_prompt'][l, 0].rearrange("s a g d -> s (a g d)")[t * P:(t + 1) * P]
                    e.dma_start(A['q_rot'][t * P:(t + 1) * P, :], QR[:, :, :].rearrange("p i c -> p (i c)")).then_inc(rot, 16)
                else:
                    kvo = O['kv_sample'][l].rearrange("b s a g d -> (b s) (a g d)")
                    wno = O['win_sample'][l].rearrange("b s a g d -> b s (a g d)")[:, WIN - NT:WIN, :]
                e.dma_start(kvo, U[t][:, NKV:NKV + 512]).then_inc(outs, 16)
                e.dma_start(wno, U[t][:, NKV + 512:NKV + 768]).then_inc(outs, 16)
                nout += 2
            e.dma_start(O['win_sample'][l].rearrange("b s a g d -> b s (a g d)")[:, 0:WIN - NT, :],
                        A['state_nsa_win'][l].rearrange("b s a g d -> b s (a g d)")[:, NT:WIN, :]).then_inc(outs, 16)
            e.wait_ge(outs, 16 * (nout + 1))
            e.wait_ge(rot, 64)

        @block.scalar
        def _(e):
            e.wait_ge(par, 48)
            act.link(e, "al", nc.scalar.activation(alog[:, :], alog[:, :], ACT.Exp))
            for t in range(NTILE):
                u, n = U[t], ROWS[t]
                for nm, a, w, f in (("rg", RG, 256, ACT.Silu), ("ng", NG, 512, ACT.Silu), ("gg", GG, 256, ACT.Silu),
                                    ("gt", NGATE, 24, ACT.Sigmoid), ("bt", GB, H4, ACT.Sigmoid)):
                    act.done(e, f"{nm}{t}", nc.scalar.activation(u[:, a:a + w], u[:, a:a + w], f))
                dve.wait(e, f"a1{t}")
                act.link(e, f"ab{t}", nc.scalar.activation(sp_[0:n, 1, :], sp_[0:n, 0, :], ACT.Abs))
                act.link(e, f"ex{t}", nc.scalar.activation(sp_[0:n, 1, :], sp_[0:n, 1, :], ACT.Exp, scale=-1.0))
                act.link(e, f"ln{t}", nc.scalar.activation(sp_[0:n, 1, :], sp_[0:n, 1, :], ACT.Ln, bias=1.0))
                dve.wait(e, f"c3a{t}")
                act.link(e, f"ys{t}", nc.scalar.activation(Y[t], Y[t], ACT.Silu))
                dve.wait(e, f"ss{t}")
                act.link(e, f"sq{t}", nc.scalar.activation(nrm[0:n, :], nrm[0:n, :], ACT.Sqrt, bias=v['eps'][0:n, :]))

        @block.vector
        def _(e):
            dve.link(e, "zero", nc.vector.memset(zero[:, :], 0.0))
            act.wait(e, "al")
            dve.link(e, "al", nc.vector.tensor_scalar(alog[:, :], alog[:, :], -1.0, None, ALU.mult))
            for t in range(NTILE):
                u, n = U[t], ROWS[t]
                co, si = cos[0:n, t, :], sin[0:n, t, :]

                def rope(nm, src, dst, s, w):
                    m = w // 32
                    A1 = ta[0:n, 0:s * w].rearrange("p (s m c) -> p s m c", s=s, m=m)
                    B1 = tb[0:n, 0:s * w].rearrange("p (s m c) -> p s m c", s=s, m=m)
                    sv = src.rearrange("p s (m c) -> p s m c", c=32)
                    bc = [n, s, m, 32]
                    dve.link(e, f"{nm}a{t}", nc.vector.tensor_tensor(A1, sv, co.unsqueeze(1).unsqueeze(1).broadcast_to(bc), ALU.mult))
                    dve.link(e, f"{nm}b{t}", nc.vector.tensor_tensor(B1, sv, si.unsqueeze(1).unsqueeze(1).broadcast_to(bc), ALU.mult))
                    dve.link(e, f"{nm}1{t}", nc.vector.tensor_tensor(dst[:, :, :, 0:32], A1[:, :, 0::2, :], B1[:, :, 1::2, :], ALU.subtract))
                    dve.link(e, f"{nm}2{t}", nc.vector.tensor_tensor(dst[:, :, :, 32:64], A1[:, :, 1::2, :], B1[:, :, 0::2, :], ALU.add))

                rqv = u[:, RQ:RQ + 512].unsqueeze(1)
                rope("rq", rqv, rqv.rearrange("p s (h c) -> p s h c", c=HD), 1, 512)
                if 0 < t < 4:
                    e.wait_ge(rot, 16 * t)
                q_to = (QR if t < 4 else v['QRS'])[0:n, :, :].rearrange("p i (r g c) -> p i g r c", r=R, g=G)
                qv = u[:, NQ:NQ + 512].rearrange("p (g w) -> p g w", g=G)
                rope("nq", qv, q_to[:, 1], 2, 256)
                dve.link(e, f"nqc{t}", nc.vector.tensor_copy(q_to[:, 0], qv.rearrange("p g (r c) -> p g r c", r=R)))
                kv = u[:, NKV + 256:NKV + 768].rearrange("p (s w) -> p s w", s=2)[:, :, 0:128]
                rope("kv", kv, kv.rearrange("p s (h c) -> p s h c", c=HD), 2, 128)
                dve.link(e, f"a1{t}", nc.vector.tensor_tensor(sp_[0:n, 0, :], u[:, GA:GA + H4], dtb[0:n, :], ALU.add))
                dve.link(e, f"mx{t}", nc.vector.tensor_scalar(sp_[0:n, 2, :], sp_[0:n, 0, :], 0.0, None, ALU.max))
                act.wait(e, f"ln{t}")
                dve.link(e, f"sg{t}", nc.vector.tensor_tensor(sp_[0:n, 2, :], sp_[0:n, 2, :], sp_[0:n, 1, :], ALU.add))
                dve.link(e, f"gl{t}", nc.vector.tensor_tensor(g_log[0:n, t, :], sp_[0:n, 2, :], alog[0:n, :], ALU.mult))
                y = Y[t]
                e.wait_ge(shift, 48 * (t + 1))
                dve.link(e, f"c0{t}", nc.vector.tensor_tensor(y, y, cw[0:n, 3, :], ALU.mult))
                for k in range(1, 4):
                    dve.link(e, f"c{k}{t}", nc.vector.tensor_tensor(ta[0:n, :], XS[0:n, k - 1, :], cw[0:n, 3 - k, :], ALU.mult))
                    dve.link(e, f"c{k}a{t}", nc.vector.tensor_tensor(y, y, ta[0:n, :], ALU.add))
                act.wait(e, f"ys{t}")
                qk = Y[t][:, 0:512].rearrange("p (h c) -> p h c", c=HD)
                tq = ta[0:n, 0:512].rearrange("p (h c) -> p h c", c=HD)
                dve.link(e, f"s2{t}", nc.vector.tensor_tensor(tq, qk, qk, ALU.mult))
                dve.link(e, f"ss{t}", nc.vector.tensor_reduce(nrm[0:n, :], tq, AX.X, ALU.add))
                act.wait(e, f"sq{t}")
                dve.link(e, f"rc{t}", nc.vector.reciprocal(nrm[0:n, :], nrm[0:n, :]))
                dve.link(e, f"q8{t}", nc.vector.tensor_scalar(nrm[0:n, 0:4], nrm[0:n, 0:4], SCALE, None, ALU.mult))
                dve.link(e, f"nm{t}", nc.vector.tensor_tensor(qk, qk, b_(nrm[0:n, :], 2, [n, 8, HD]), ALU.mult))


def load_states(e, S, src, loaded, l):
    for b in range(NB):
        for h in range(H4):
            hp, o = h // 2, (h % 2) * HD
            e.dma_start(S[o:o + HD, b, hp, o:o + HD], src[l, b, h]).then_inc(loaded, 16)
    return 32 * 16


def retention(nc, A, O, l, scope, sb, stage, v, U):
    QK = sb(scope, "QK", [P, 4, P])
    ATT = sb(scope, "ATT", [P, H4, P])
    KDc = sb(scope, "KDc", [P, 256])
    S = sb(scope, "S", [P, 2, P])
    SS = sb(scope, "SS", [P, NB, 2, P])
    QM = sb(scope, "QM", [P, 2, NB, 64])
    VM = sb(scope, "VM", [P, NB, 256])
    T1 = sb(scope, "T1", [P, 512])
    Ot = sb(scope, "Ot", [P, 256])
    st = sb(scope, "st", [P, 4, H4])
    gn = sb(scope, "gn", [P, 256])
    bk, cf, ident, MIX = v['bk'], v['cf'], v['ident'], v['MIX']
    dn = ["z1", "z2"]
    for t in range(NTILE):
        dn += [f"{x}{t}" for x in ("qk", "att0", "att1", "kd")]
        dn += [f"qm{hp}" for hp in range(2)] + ["vm"] if t == 4 else []
        dn += [f"{x}{t}" for x in ("qs", "o")]
        dn += [f"{x}{t}" for x in ("m", "m2", "ce", "sq", "va", "rc", "n1", "n2", "n3")]
        dn += [f"{x}{t}" for x in ("sm", "s0", "s1")] if t < 4 else [f"ss{i}{j}" for i in range(4) for j in "ms"]
    pn = [f"{x}{t}" for t in range(NTILE) for x in ("T", "a", "qs", "av", "su")]
    with stage(["dve_s", "act_s", "pe_s", "loaded", "gl", "outs"]) as (block, (dve_s, act_s, pe_s, loaded, gl, outs)):
        dve = Steps(dve_s, dn)
        act = Steps(act_s, [f"sq{t}" for t in range(NTILE)])
        pe = Steps(pe_s, pn)

        @block.sync
        def _(e):
            e.dma_start(gn[:, :], A['ret_gn'][l].partition_broadcast(P)).then_inc(gl, 16)
            dve.wait(e, "z2")
            load_states(e, SS, A['state_ret'], loaded, l)
            dve.wait(e, "s13")
            for h in range(H4):
                hp, o = h // 2, (h % 2) * HD
                e.dma_start(O['ret_prompt'][l, 0, h], S[o:o + HD, hp, o:o + HD]).then_inc(outs, 16)
            dve.wait(e, "ss3s")
            for b in range(NB):
                for h in range(H4):
                    hp, o = h // 2, (h % 2) * HD
                    e.dma_start(O['ret_sample'][l, b, h], SS[o:o + HD, b, hp, o:o + HD]).then_inc(outs, 16)
            e.wait_ge(outs, 36 * 16)

        @block.scalar
        def _(e):
            for t in range(NTILE):
                dve.wait(e, f"va{t}")
                act.done(e, f"sq{t}", nc.scalar.activation(st[0:ROWS[t], 2, :], st[0:ROWS[t], 2, :], ACT.Sqrt,
                                                           scale=1.0 / HD, bias=v['eps'][0:ROWS[t], :]))

        @block.tensor
        def _(e):
            for t in range(NTILE):
                u, n, k = U[t], ROWS[t], int(t == 4)
                if t:
                    dve.wait(e, f"qk{t-1}")
                for i in range(4):
                    mm = nc.tensor.transpose(bk(0, 4)[:, i, 0:n], u[:, i * P:(i + 1) * P], ident[0:n, 0:n])
                pe.done(e, f"T{t}", mm)
                dve.wait(e, f"qk{t}")
                for h in range(H4):
                    o = (h % 2) * HD
                    mm = nc.tensor.matmul(bk(1 + 4 * (h % 2), 4)[0:n, h // 2, 0:n], QK[o:o + HD, 2 + h // 2, 0:n], QK[o:o + HD, h // 2, 0:n],
                                          start=True, stop=True)
                pe.done(e, f"a{t}", mm)
                if t < 4:
                    if t:
                        dve.wait(e, f"s1{t-1}")
                    else:
                        dve.wait(e, "z1")
                    for hp in range(2):
                        mm = nc.tensor.matmul(bk(2, 4)[0:n, hp, :], QK[:, hp, 0:n], S[:, hp, :], start=True, stop=True)
                else:
                    dve.wait(e, "qm1")
                    e.wait_ge(loaded, 32 * 16)
                    for hp in range(2):
                        for b in range(NB):
                            mm = nc.tensor.matmul(bk(2, 4)[0:n, hp, :], QM[:, hp, b, :], SS[:, b, hp, :],
                                                  start=(b == 0), stop=(b == NB - 1))
                pe.done(e, f"qs{t}", mm)
                dve.wait(e, f"att1{t}")
                for h in range(H4):
                    mm = nc.tensor.matmul(bk(3)[0:n, h * HD:(h + 1) * HD], ATT[0:n, h, 0:n], u[:, RV + h * HD:RV + (h + 1) * HD],
                                          start=True, stop=True)
                pe.done(e, f"av{t}", mm)
                dve.wait(e, f"kd{t}" if t < 4 else "vm")
                if t < 4:
                    for hp in range(2):
                        mm = nc.tensor.matmul(bk(4, 4)[:, hp, :], KDc[0:n, hp * P:(hp + 1) * P], u[:, RV + hp * P:RV + (hp + 1) * P],
                                              start=True, stop=True)
                else:
                    for i in range(4):
                        hp, q = divmod(i, 2)
                        mm = nc.tensor.matmul(bk(4 + i), KDc[0:n, hp * P:(hp + 1) * P], VM[0:n, 4 * q:4 * q + 4, hp * P:(hp + 1) * P],
                                              start=True, stop=True)
                pe.done(e, f"su{t}", mm)

        @block.vector
        def _(e):
            dve.link(e, "z1", nc.vector.memset(S[:, :, :], 0.0))
            dve.link(e, "z2", nc.vector.memset(SS[:, :, :, :], 0.0))
            e.wait_ge(gl, 16)
            pair = cf('pair')
            for t in range(NTILE):
                u, n, k = U[t], ROWS[t], int(t == 4)
                pe.wait(e, f"T{t}")
                dve.link(e, f"qk{t}", nc.vector.tensor_copy(QK[:, :, 0:n], bk(0, 4)[:, :, 0:n]))
                pe.wait(e, f"a{t}")
                for o in range(2):
                    dve.link(e, f"att{o}{t}", nc.vector.tensor_tensor(ATT[0:n, o::2, 0:n], bk(1 + 4 * o, 4)[0:n, 0:2, 0:n],
                                                                       cf(f'dm{k}', P)[0:n, o::2, 0:n], ALU.mult))
                h3 = lambda ap: ap.rearrange("p (h c) -> p h c", c=HD)
                dve.link(e, f"kd{t}", nc.vector.tensor_tensor(h3(KDc[0:n, :]), h3(u[:, RK:RK + 256]),
                                                               b_(cf('kdec', 4)[0:n, k, :], 2, [n, H4, HD]), ALU.mult))
                if t == 4:
                    for hp in range(2):
                        dve.link(e, f"qm{hp}", nc.vector.tensor_tensor(QM[:, hp, :, :], b_(QK[:, hp, 0:64], 1, [P, NB, 64]), cf('own', 64), ALU.mult))
                    dve.link(e, "vm", nc.vector.tensor_tensor(VM[0:n, :, :], b_(u[:, RV:RV + 256], 1, [n, NB, 256]),
                                                               b_(cf('ownrow')[0:n, :], 2, [n, NB, 256]), ALU.mult))
                pe.wait(e, f"qs{t}")
                dve.link(e, f"qs{t}", nc.vector.tensor_tensor(h3(T1[0:n, 0:256]), h3(bk(2)[0:n, 0:256]),
                                                               b_(cf('qdec', 4)[0:n, k, :], 2, [n, H4, HD]), ALU.mult))
                pe.wait(e, f"av{t}")
                dve.link(e, f"o{t}", nc.vector.tensor_tensor(Ot[0:n, :], bk(3)[0:n, 0:256], T1[0:n, 0:256], ALU.add))
                o3 = h3(Ot[0:n, :])
                dve.link(e, f"m{t}", nc.vector.tensor_reduce(st[0:n, 0, :], o3, AX.X, ALU.add))
                dve.link(e, f"m2{t}", nc.vector.tensor_scalar(st[0:n, 1, :], st[0:n, 0, :], 1.0 / HD, None, ALU.mult))
                dve.link(e, f"ce{t}", nc.vector.tensor_tensor(o3, o3, b_(st[0:n, 1, :], 2, [n, H4, HD]), ALU.subtract))
                dve.link(e, f"sq{t}", nc.vector.tensor_tensor(T1[0:n, 0:256], Ot[0:n, :], Ot[0:n, :], ALU.mult))
                dve.link(e, f"va{t}", nc.vector.tensor_reduce(st[0:n, 2, :], h3(T1[0:n, 0:256]), AX.X, ALU.add))
                act.wait(e, f"sq{t}")
                dve.link(e, f"rc{t}", nc.vector.reciprocal(st[0:n, 3, :], st[0:n, 2, :]))
                dve.link(e, f"n1{t}", nc.vector.tensor_tensor(o3, o3, b_(st[0:n, 3, :], 2, [n, H4, HD]), ALU.mult))
                dve.link(e, f"n2{t}", nc.vector.tensor_tensor(Ot[0:n, :], Ot[0:n, :], gn[0:n, :], ALU.mult))
                dve.link(e, f"n3{t}", nc.vector.tensor_tensor(MIX[0:n, t, 0:256], Ot[0:n, :], u[:, RG:RG + 256], ALU.mult))
                pe.wait(e, f"su{t}")
                if t < 4:
                    dve.link(e, f"sm{t}", nc.vector.tensor_tensor(T1[:, 0:256].rearrange("p (a b) -> p a b", a=2), bk(4, 4)[:, 0:2, :],
                                                                   b_(pair, 1, [P, 2, P]), ALU.mult))
                    for hp in range(2):
                        dve.link(e, f"s{hp}{t}", nc.vector.scalar_tensor_tensor(
                            S[:, hp, :], S[:, hp, :], cf('sdec', 2)[:, 0, hp:hp + 1], T1[:, hp * P:(hp + 1) * P], ALU.mult, ALU.add))
                else:
                    for i in range(4):
                        hp, q = divmod(i, 2)
                        t3 = T1[:, :].rearrange("p (a b) -> p a b", a=4)
                        dve.link(e, f"ss{i}m", nc.vector.tensor_tensor(t3, bk(4 + i, 4), b_(pair, 1, [P, 4, P]), ALU.mult))
                        sv = SS[:, 4 * q:4 * q + 4, hp, :]
                        dve.link(e, f"ss{i}s", nc.vector.scalar_tensor_tensor(sv, sv, cf('sdec', 2)[:, 1, hp:hp + 1], t3, ALU.mult, ALU.add))


def delta(nc, A, O, l, scope, sb, stage, v, U, Y, g_log):
    QKT = sb(scope, "QKT", [P, 6, P])
    kb = sb(scope, "kb", [P, 256])
    vb = sb(scope, "vb", [P, 256])
    kd = sb(scope, "kd", [P, 256])
    work = sb(scope, "work", [P, 4, H4, P])
    gb, NTt, NTs, M1 = (work[:, i, :, :] for i in range(4))
    VM = work[:, :, :, :].rearrange("p a h c -> p (a h c)").rearrange("p (b c) -> p b c", b=NB)
    LT = sb(scope, "LT", [P, H4, P])
    ATT = sb(scope, "ATT", [P, H4, P])
    T = sb(scope, "T", [P, H4, P])
    TT = sb(scope, "TT", [P, H4, P])
    gs = sb(scope, "gs", [P, 7, H4])
    SL = sb(scope, "SL", [P, H4, NB])
    SLp = sb(scope, "SLp", [P, 2, NB])
    S = sb(scope, "S", [P, 2, P])
    SS = sb(scope, "SS", [P, NB, 2, P])
    QM = sb(scope, "QM", [P, 4, NB, 64])
    VN = sb(scope, "VN", [P, 256])
    T1 = sb(scope, "T1", [P, 512])
    Ot = sb(scope, "Ot", [P, 256])
    st = sb(scope, "st", [P, 4, H4])
    gn = sb(scope, "gn", [P, HD])
    bk, cf, ident, MIX = v['bk'], v['cf'], v['ident'], v['MIX']
    LV = [7, 7, 7, 7, 3]
    dn, pn, an = ["z1", "z2"], [], []
    for t in range(NTILE):
        dn += [f"{x}{t}" for x in ("kb", "vb", "gb", "g0", "g1", "g3", "gd", "lt", "tr", "tr2", "nt0", "nt1", "att0", "att1", "be", "kd", "i0", "i1")]
        dn += [f"{x}{t}.{s}" for s in range(LV[t]) for x in ("ns", "t", "tt")]
        dn += [f"qm{i}" for i in range(4)] if t == 4 else []
        dn += [f"{x}{t}" for x in ("ks", "r", "vn", "qs", "o")]
        dn += [f"{x}{t}" for x in ("sq", "va", "rc", "n1", "n2", "n3", "sp0", "sp1")]
        dn += [f"{x}{t}" for x in ("sm", "s0", "s1")] if t < 4 else ["vm"] + [f"ss{i}{j}" for i in range(4) for j in "nms"]
        pn += [f"{x}{t}" for x in ("g", "gr", "T", "kk", "qk")] + [f"{x}{t}.{s}" for s in range(LV[t]) for x in ("a", "b", "c")]
        pn += [f"{x}{t}" for x in ("ks", "vn", "qs", "av", "su")]
        an += [f"{x}{t}" for x in ("eg", "el", "sl", "L0", "L1", "L2", "L3")] + [f"m{t}.{s}" for s in range(LV[t])] + [f"rt{t}"]
    with stage(["dve_s", "act_s", "pe_s", "loaded", "gl", "outs"]) as (block, (dve_s, act_s, pe_s, loaded, gl, outs)):
        dve, act, pe = Steps(dve_s, dn), Steps(act_s, an), Steps(pe_s, pn)

        @block.sync
        def _(e):
            e.dma_start(gn[:, :], A['gdn_norm'][l].partition_broadcast(P)).then_inc(gl, 16)
            dve.wait(e, "z2")
            load_states(e, SS, A['state_gdn'], loaded, l)
            dve.wait(e, "s13")
            for h in range(H4):
                hp, o = h // 2, (h % 2) * HD
                e.dma_start(O['gdn_prompt'][l, 0, h], S[o:o + HD, hp, o:o + HD]).then_inc(outs, 16)
            dve.wait(e, "ss3s")
            for b in range(NB):
                for h in range(H4):
                    hp, o = h // 2, (h % 2) * HD
                    e.dma_start(O['gdn_sample'][l, b, h], SS[o:o + HD, b, hp, o:o + HD]).then_inc(outs, 16)
            e.wait_ge(outs, 36 * 16)

        @block.scalar
        def _(e):
            for t in range(NTILE):
                n, k = ROWS[t], int(t == 4)
                dve.wait(e, f"gd{t}")
                act.done(e, f"eg{t}", nc.scalar.activation(gs[0:n, 2, :], gs[0:n, 0, :], ACT.Exp))
                act.done(e, f"el{t}", nc.scalar.activation(gs[0:n, 4, :], gs[0:n, 5, :], ACT.Exp))
                pe.wait(e, f"gr{t}")
                if t:
                    dve.wait(e, f"sp1{t-1}")
                src = bk(1, 4)[:, :, P - 1:P] if t < 4 else bk(1, 4)[:, :, NT - 1:64:NT]
                act.done(e, f"sl{t}", nc.scalar.activation(SL[:, :, 0:1] if t < 4 else SL[:, :, :], src, ACT.Exp))
                dve.wait(e, f"lt{t}")
                for h in range(H4):
                    act.done(e, f"L{h}{t}", nc.scalar.activation(LT[0:n, h, 0:n], LT[0:n, h, 0:n], ACT.Exp, bias=gs[0:n, 1, h:h + 1]))
                for s in range(LV[t]):
                    pe.wait(e, f"a{t}.{s}")
                    if s or t:
                        pe.wait(e, f"c{t}.{s-1}" if s else f"c{t-1}.{LV[t-1]-1}")
                    act.done(e, f"m{t}.{s}", nc.scalar.activation(M1[0:n, :, 0:n], bk(4, 4)[0:n, :, 0:n], ACT.Copy))
                dve.wait(e, f"va{t}")
                act.done(e, f"rt{t}", nc.scalar.activation(st[0:n, 2, :], st[0:n, 2, :], ACT.Sqrt, scale=1.0 / HD, bias=v['eps'][0:n, :]))

        @block.tensor
        def _(e):
            for t in range(NTILE):
                n, k = ROWS[t], int(t == 4)
                y = Y[t]
                tri, same = cf('tri', P)[0:n, k, 0:n], cf('same', P)[0:n, k, 0:n]
                dve.wait(e, f"gb{t}")
                nc.tensor.matmul(bk(0)[0:n, 0:4], tri, g_log[0:n, t, :], start=True, stop=True)
                pe.done(e, f"g{t}", nc.tensor.matmul(bk(0)[0:n, 4:8], same, g_log[0:n, t, :], start=True, stop=True))
                for h in range(H4):
                    mm = nc.tensor.matmul(bk(1, 4)[:, h, 0:n], gb[0:n, h, :], tri, start=True, stop=True)
                pe.done(e, f"gr{t}", mm)
                for i in range(6):
                    src = y[:, i * P:(i + 1) * P] if i < 4 else kb[0:n, (i - 4) * P:(i - 3) * P]
                    mm = nc.tensor.transpose(bk(2 + i // 4, 4)[:, i % 4, 0:n], src, ident[0:n, 0:n])
                pe.done(e, f"T{t}", mm)
                dve.wait(e, f"tr2{t}")
                for nm, b, c in (("kk", 2, 4), ("qk", 4, 0)):
                    for h in range(H4):
                        o = (h % 2) * HD
                        mm = nc.tensor.matmul(bk(b + h % 2, 4)[0:n, h // 2, 0:n], QKT[o:o + HD, 2 + h // 2, 0:n], QKT[o:o + HD, c + h // 2, 0:n],
                                              start=True, stop=True)
                    pe.done(e, f"{nm}{t}", mm)
                dve.wait(e, f"i1{t}")
                for s in range(LV[t]):
                    dve.wait(e, f"ns{t}.{s}")
                    for h in range(H4):
                        mm = nc.tensor.matmul(bk(4, 4)[0:n, h, 0:n], NTs[0:n, h, 0:n], T[0:n, h, 0:n], start=True, stop=True)
                    pe.done(e, f"a{t}.{s}", mm)
                    act.wait(e, f"m{t}.{s}")
                    for h in range(H4):
                        mm = nc.tensor.matmul(bk(5, 4)[0:n, h, 0:n], TT[0:n, h, 0:n], M1[0:n, h, 0:n], start=True, stop=True)
                    pe.done(e, f"b{t}.{s}", mm)
                    for h in range(H4):
                        mm = nc.tensor.matmul(bk(6, 4)[0:n, h, 0:n], M1[0:n, h, 0:n], TT[0:n, h, 0:n], start=True, stop=True)
                    pe.done(e, f"c{t}.{s}", mm)
                    dve.wait(e, f"tt{t}.{s}")
                if t < 4:
                    dve.wait(e, f"s1{t-1}" if t else "z1")
                    for hp in range(2):
                        mm = nc.tensor.matmul(bk(0, 4)[0:n, hp, :], QKT[:, 2 + hp, 0:n], S[:, hp, :], start=True, stop=True)
                else:
                    dve.wait(e, "qm3")
                    e.wait_ge(loaded, 32 * 16)
                    for hp in range(2):
                        for b in range(NB):
                            mm = nc.tensor.matmul(bk(0, 4)[0:n, hp, :], QM[:, 2 + hp, b, :], SS[:, b, hp, :], start=(b == 0), stop=(b == NB - 1))
                pe.done(e, f"ks{t}", mm)
                dve.wait(e, f"r{t}")
                for h in range(H4):
                    mm = nc.tensor.matmul(bk(1)[0:n, h * HD:(h + 1) * HD], TT[0:n, h, 0:n], T1[0:n, 256 + h * HD:256 + (h + 1) * HD],
                                          start=True, stop=True)
                pe.done(e, f"vn{t}", mm)
                for hp in range(2):
                    if t < 4:
                        mm = nc.tensor.matmul(bk(2, 4)[0:n, hp, :], QKT[:, hp, 0:n], S[:, hp, :], start=True, stop=True)
                    else:
                        for b in range(NB):
                            mm = nc.tensor.matmul(bk(2, 4)[0:n, hp, :], QM[:, hp, b, :], SS[:, b, hp, :], start=(b == 0), stop=(b == NB - 1))
                pe.done(e, f"qs{t}", mm)
                dve.wait(e, f"vn{t}")
                for h in range(H4):
                    mm = nc.tensor.matmul(bk(3)[0:n, h * HD:(h + 1) * HD], ATT[0:n, h, 0:n], VN[0:n, h * HD:(h + 1) * HD], start=True, stop=True)
                pe.done(e, f"av{t}", mm)
                if t < 4:
                    for hp in range(2):
                        mm = nc.tensor.matmul(bk(4, 4)[:, hp, :], kd[0:n, hp * P:(hp + 1) * P], VN[0:n, hp * P:(hp + 1) * P], start=True, stop=True)
                else:
                    dve.wait(e, "vm")
                    for i in range(4):
                        hp, q = divmod(i, 2)
                        mm = nc.tensor.matmul(bk(4 + i), kd[0:n, hp * P:(hp + 1) * P], VM[0:n, 4 * q:4 * q + 4, hp * P:(hp + 1) * P],
                                              start=True, stop=True)
                pe.done(e, f"su{t}", mm)
                dve.wait(e, f"s1{t}" if t < 4 else "ss3s")

        @block.vector
        def _(e):
            dve.link(e, "z1", nc.vector.memset(S[:, :, :], 0.0))
            dve.link(e, "z2", nc.vector.memset(SS[:, :, :, :], 0.0))
            e.wait_ge(gl, 16)
            pair = cf('pair')
            h3 = lambda ap: ap.rearrange("p (h c) -> p h c", c=HD)
            for t in range(NTILE):
                u, n, k = U[t], ROWS[t], int(t == 4)
                y = Y[t]
                hb = lambda ap: b_(ap, 2, [n, H4, HD])
                if t:
                    pe.wait(e, f"su{t-1}")
                dve.link(e, f"kb{t}", nc.vector.tensor_tensor(h3(kb[0:n, :]), h3(y[:, 256:512]), hb(u[:, GB:GB + H4]), ALU.mult))
                dve.link(e, f"vb{t}", nc.vector.tensor_tensor(h3(vb[0:n, :]), h3(y[:, 512:768]), hb(u[:, GB:GB + H4]), ALU.mult))
                dve.link(e, f"gb{t}", nc.vector.tensor_copy(gb[0:n, :, :], b_(g_log[0:n, t, :], 2, [n, H4, P])))
                pe.wait(e, f"g{t}")
                dve.link(e, f"g0{t}", nc.vector.tensor_copy(gs[0:n, 0, :], bk(0)[0:n, 0:4]))
                dve.link(e, f"g1{t}", nc.vector.tensor_scalar(gs[0:n, 1, :], bk(0)[0:n, 0:4], -1.0, None, ALU.mult))
                dve.link(e, f"g3{t}", nc.vector.tensor_copy(gs[0:n, 3, :], bk(0)[0:n, 4:8]))
                dve.link(e, f"gd{t}", nc.vector.tensor_tensor(gs[0:n, 5, :], gs[0:n, 3, :], gs[0:n, 0, :], ALU.subtract))
                act.wait(e, f"sl{t}")
                dve.link(e, f"lt{t}", nc.vector.tensor_tensor(LT[0:n, :, 0:n], bk(1, 4)[0:n, :, 0:n],
                                                               b_(cf('neg', P)[0:n, k, 0:n], 1, [n, H4, n]), ALU.add))
                pe.wait(e, f"T{t}")
                dve.link(e, f"tr{t}", nc.vector.tensor_copy(QKT[:, 0:4, 0:n], bk(2, 4)[:, :, 0:n]))
                dve.link(e, f"tr2{t}", nc.vector.tensor_copy(QKT[:, 4:6, 0:n], bk(3, 4)[:, 0:2, 0:n]))
                pe.wait(e, f"kk{t}")
                act.wait(e, f"L3{t}")
                for o in range(2):
                    dve.link(e, f"nt{o}{t}", nc.vector.tensor_tensor(NTt[0:n, o::2, 0:n], bk(2 + o, 4)[0:n, 0:2, 0:n], LT[0:n, o::2, 0:n], ALU.mult))
                pe.wait(e, f"qk{t}")
                for o in range(2):
                    dve.link(e, f"att{o}{t}", nc.vector.tensor_tensor(ATT[0:n, o::2, 0:n], bk(4 + o, 4)[0:n, 0:2, 0:n], LT[0:n, o::2, 0:n], ALU.mult))
                dve.link(e, f"be{t}", nc.vector.tensor_tensor(gs[0:n, 6, :], gs[0:n, 2, :], u[:, GB:GB + H4], ALU.mult))
                dve.link(e, f"kd{t}", nc.vector.tensor_tensor(h3(kd[0:n, :]), h3(y[:, 256:512]), hb(gs[0:n, 4, :]), ALU.mult))
                dve.link(e, f"i0{t}", nc.vector.tensor_copy(T[0:n, :, 0:n], b_(ident[0:n, 0:n], 1, [n, H4, n])))
                dve.link(e, f"i1{t}", nc.vector.tensor_copy(TT[0:n, :, 0:n], b_(ident[0:n, 0:n], 1, [n, H4, n])))
                for s in range(LV[t]):
                    dve.link(e, f"ns{t}.{s}", nc.vector.tensor_tensor(NTs[0:n, :, 0:n], NTt[0:n, :, 0:n],
                                                                       b_(cf('level', P)[0:n, s, 0:n], 1, [n, H4, n]), ALU.mult))
                    pe.wait(e, f"b{t}.{s}")
                    dve.link(e, f"t{t}.{s}", nc.vector.tensor_tensor(T[0:n, :, 0:n], T[0:n, :, 0:n], bk(5, 4)[0:n, :, 0:n], ALU.subtract))
                    pe.wait(e, f"c{t}.{s}")
                    dve.link(e, f"tt{t}.{s}", nc.vector.tensor_tensor(TT[0:n, :, 0:n], TT[0:n, :, 0:n], bk(6, 4)[0:n, :, 0:n], ALU.subtract))
                if t == 4:
                    for i in range(4):
                        dve.link(e, f"qm{i}", nc.vector.tensor_tensor(QM[:, i, :, :], b_(QKT[:, i, 0:64], 1, [P, NB, 64]), cf('own', 64), ALU.mult))
                pe.wait(e, f"ks{t}")
                dve.link(e, f"ks{t}", nc.vector.tensor_tensor(h3(T1[0:n, 0:256]), h3(bk(0)[0:n, 0:256]), hb(gs[0:n, 6, :]), ALU.mult))
                dve.link(e, f"r{t}", nc.vector.tensor_tensor(T1[0:n, 256:512], vb[0:n, :], T1[0:n, 0:256], ALU.subtract))
                pe.wait(e, f"vn{t}")
                dve.link(e, f"vn{t}", nc.vector.tensor_copy(VN[0:n, :], bk(1)[0:n, 0:256]))
                pe.wait(e, f"qs{t}")
                dve.link(e, f"qs{t}", nc.vector.tensor_tensor(h3(T1[0:n, 0:256]), h3(bk(2)[0:n, 0:256]), hb(gs[0:n, 2, :]), ALU.mult))
                pe.wait(e, f"av{t}")
                dve.link(e, f"o{t}", nc.vector.tensor_tensor(Ot[0:n, :], bk(3)[0:n, 0:256], T1[0:n, 0:256], ALU.add))
                dve.link(e, f"sq{t}", nc.vector.tensor_tensor(T1[0:n, 0:256], Ot[0:n, :], Ot[0:n, :], ALU.mult))
                dve.link(e, f"va{t}", nc.vector.tensor_reduce(st[0:n, 2, :], h3(T1[0:n, 0:256]), AX.X, ALU.add))
                act.wait(e, f"rt{t}")
                dve.link(e, f"rc{t}", nc.vector.reciprocal(st[0:n, 3, :], st[0:n, 2, :]))
                dve.link(e, f"n1{t}", nc.vector.tensor_tensor(h3(Ot[0:n, :]), h3(Ot[0:n, :]), hb(st[0:n, 3, :]), ALU.mult))
                dve.link(e, f"n2{t}", nc.vector.tensor_tensor(h3(Ot[0:n, :]), h3(Ot[0:n, :]), b_(gn[0:n, :], 1, [n, H4, HD]), ALU.mult))
                dve.link(e, f"n3{t}", nc.vector.tensor_tensor(MIX[0:n, t, 768:1024], Ot[0:n, :], u[:, GG:GG + 256], ALU.mult))
                act.wait(e, f"sl{t}")
                w = 1 if t < 4 else NB
                dve.link(e, f"sp0{t}", nc.vector.tensor_copy(SLp[0:64, :, 0:w], SL[0:64, 0::2, 0:w]))
                dve.link(e, f"sp1{t}", nc.vector.tensor_copy(SLp[64:P, :, 0:w], SL[64:P, 1::2, 0:w]))
                if t < 4:
                    pe.wait(e, f"su{t}")
                    dve.link(e, f"sm{t}", nc.vector.tensor_tensor(T1[:, 0:256].rearrange("p (a b) -> p a b", a=2), bk(4, 4)[:, 0:2, :],
                                                                   b_(pair, 1, [P, 2, P]), ALU.mult))
                    for hp in range(2):
                        dve.link(e, f"s{hp}{t}", nc.vector.scalar_tensor_tensor(
                            S[:, hp, :], S[:, hp, :], SLp[:, hp, 0:1], T1[:, hp * P:(hp + 1) * P], ALU.mult, ALU.add))
                else:
                    dve.link(e, "vm", nc.vector.tensor_tensor(VM[0:n, :, :], b_(VN[0:n, :], 1, [n, NB, 256]),
                                                               b_(cf('ownrow')[0:n, :], 2, [n, NB, 256]), ALU.mult))
                    pe.wait(e, f"su{t}")
                    for i in range(4):
                        hp, q = divmod(i, 2)
                        t3 = T1[:, :].rearrange("p (a b) -> p a b", a=4)
                        sv = SS[:, 4 * q:4 * q + 4, hp, :]
                        dve.link(e, f"ss{i}n", nc.vector.tensor_tensor(sv, sv, b_(SLp[:, hp, 4 * q:4 * q + 4], 2, [P, 4, P]), ALU.mult))
                        dve.link(e, f"ss{i}m", nc.vector.tensor_tensor(t3, bk(4 + i, 4), b_(pair, 1, [P, 4, P]), ALU.mult))
                        dve.link(e, f"ss{i}s", nc.vector.tensor_tensor(sv, sv, t3, ALU.add))


class Compress:

    RING = 4

    def __init__(self, v, tiles, PC, RP, HT, HS, KC, VC):
        self.v, self.nt, self.PC, self.RP, self.HT, self.HS, self.KC, self.VC = v, tiles, PC, RP, HT, HS, KC, VC
        self.ns = tiles * P * PAIRS // SEG
        self.nc = -(-self.ns // P)
        self.pool_names = [f"R{i}" for i in range(tiles)]
        self.pe_names = [f"T{i}" for i in range(tiles)] + [f"{x}{kv}" for kv in range(2) for x in ("H", "J", "C")]
        self.act_names = [f"X{i}" for i in range(0, tiles, 2)] + [f"{x}{kv}" for kv in range(2) for x in ("HT", "HS")]
        self.dve_names = [f"X{i}" for i in range(1, tiles, 2)] + [f"C{kv}" for kv in range(2)]

    def pool(self, e, pool, pe):
        for i in range(self.nt):
            if i >= self.RING:
                pe.wait(e, f"T{i-self.RING}")
            pool.done(e, f"R{i}", nc_(self.v).gpsimd.tensor_copy(
                self.RP[:, i % self.RING, :, :, :].rearrange("p h r d -> p r h d"),
                self.PC[:, i, :, :].rearrange("p r (h d) -> p r h d", d=HD)))

    def copied(self, e, act, dve, i):
        (dve if i % 2 else act).wait(e, f"X{i}")

    def pe(self, e, pool, pe, act, dve):
        v, ident = self.v, self.v['ident']
        for i in range(self.nt):
            pool.wait(e, f"R{i}")
            if i >= 2:
                self.copied(e, act, dve, i - 2)
            for h in range(2 * G):
                mm = nc_(v).tensor.transpose(v['bk'](6 + i % 2, 4)[:, h, :], self.RP[:, i % self.RING, h, :, :].rearrange("p r d -> p (r d)"), ident)
            pe.done(e, f"T{i}", mm)
        for i in range(self.nt - 2, self.nt):
            self.copied(e, act, dve, i)
        ns = self.ns
        for kv in range(2):
            b0, b1 = 2 * kv, 2 * kv + 1
            seg = self.PC[:, :, :, :].rearrange("p i r c -> p i (r c)").rearrange(
                "p i (h n s) -> p h i n s", h=2 * G, s=SEG // PAIRS)[:, kv * G:(kv + 1) * G]
            out = v['bk'](b0)[:, 0:G * ns].rearrange("p (g i n) -> p g i n", g=G, i=self.nt)
            for s in range(SEG // PAIRS):
                mm = nc_(v).tensor.matmul(out, v['W1'][:, kv, s, :], seg[:, :, :, :, s], start=(s == 0), stop=(s == SEG // PAIRS - 1))
            pe.done(e, f"H{kv}", mm)
            act.wait(e, f"HT{kv}")
            ht = self.HT[:, 0:G * ns].rearrange("p (g n) -> p g n", g=G)
            out = v['bk'](b1)[0:HD, 0:G * (ns - 1)].rearrange("p (g n) -> p g n", g=G)
            nc_(v).tensor.matmul(out, ident[:, 0:HD], ht[:, :, 0:ns - 1], start=True, stop=False)
            pe.done(e, f"J{kv}", nc_(v).tensor.matmul(out, ident[:, HD:P], ht[:, :, 1:ns], start=False, stop=True))
            act.wait(e, f"HS{kv}")
            hs = self.HS
            if kv == 0:
                for g in range(G):
                    mm = nc_(v).tensor.matmul(v['bk'](b0)[:, 0:ns], v['W2'][:, kv, g, :], hs[:, g, 0:ns], start=(g == 0), stop=(g == G - 1))
            else:
                for c in range(self.nc):
                    for g in range(G):
                        mm = nc_(v).tensor.matmul(v['bk'](b0)[0:min(P, ns), c * P + g * HD:c * P + (g + 1) * HD],
                                                  hs[:, g, c * P:min(ns, (c + 1) * P)], v['W2'][:, kv, 0, 0:HD], start=True, stop=True)
            pe.done(e, f"C{kv}", mm)

    def x_copy(self, i):
        return self.PC[:, i, :, :].rearrange("p r (h c) -> p (r h) c", c=P), self.v['bk'](6 + i % 2, 4)

    def act(self, e, pe, act, dve):
        v, ns = self.v, self.ns
        for i in range(0, self.nt, 2):
            pe.wait(e, f"T{i}")
            dst, s = self.x_copy(i)
            act.done(e, f"X{i}", nc_(v).scalar.activation(dst, s, ACT.Copy))
        for kv in range(2):
            pe.wait(e, f"H{kv}")
            if kv:
                pe.wait(e, "J0")
            act.done(e, f"HT{kv}", nc_(v).scalar.activation(self.HT[:, 0:G * ns], v['bk'](2 * kv)[:, 0:G * ns], ACT.Copy))
            pe.wait(e, f"J{kv}")
            if kv:
                pe.wait(e, "C0")
            act.done(e, f"HS{kv}", nc_(v).scalar.activation(self.HS[:, :, 0:ns - 1],
                                                           v['bk'](2 * kv + 1)[0:HD, 0:G * (ns - 1)].rearrange("p (g n) -> p g n", g=G),
                                                           ACT.Silu, bias=v['B1'][:, kv:kv + 1]))

    def dve(self, e, pe, act, dve):
        v, ns = self.v, self.ns
        for i in range(1, self.nt, 2):
            pe.wait(e, f"T{i}")
            dst, s = self.x_copy(i)
            dve.done(e, f"X{i}", nc_(v).vector.tensor_copy(dst, s))
        pe.wait(e, "C0")
        dve.done(e, "C0", nc_(v).vector.tensor_copy(self.KC[:, 0:ns], v['bk'](0)[:, 0:ns]))
        pe.wait(e, "C1")
        m = min(P, ns)
        dve.link(e, "C1", nc_(v).vector.tensor_copy(self.VC[0:m, 0:self.nc, :], v['bk'](2, 4)[0:m, 0:self.nc, :]))


def nc_(v):
    return v['nc']


def prompt_attention(nc, A, O, l, scope, sb, stage, v, U):
    bk, cf, cb, ident, MIX = v['bk'], v['cf'], v['cb'], v['ident'], v['MIX']
    QT = sb(scope, "QT", [P, 2, R, SEQ])
    KT = sb(scope, "KT", [P, 2, SEQ])
    KC = sb(scope, "KCp", [P, 32])
    VC = sb(scope, "VCp", [P, 1, P])
    early = scope.enter_context(ExitStack())
    QRP = sb(early, "QRP", [P, 4, 2, 512])
    PG = sb(early, "PG", [P, 2, PAIRS, 256])
    RP = sb(early, "RPp", [P, 4, 2 * G, PAIRS, HD])
    HT = sb(early, "HTp", [P, 64])
    HS = sb(early, "HSp", [HD, G, 32])
    W1, W2, B1 = v['W1'], v['W2'], v['B1']
    with stage(["dve_s", "act_s", "pe_s", "pool_s", "weights", "rows"]) as (block, (dve_s, act_s, pe_s, pool_s, weights, rows)):
        cp = Compress(v, 2, PG, RP, HT, HS, KC, VC)
        pool = Steps(pool_s, cp.pool_names)
        pe = Steps(pe_s, cp.pe_names + [f"{x}{t}" for t in range(4) for x in ("Tq", "Tr", "Tk")])
        act = Steps(act_s, cp.act_names + [f"Tr{t}" for t in range(4)])
        dve = Steps(dve_s, ["z0", "z1"] + cp.dve_names + [f"{x}{t}" for t in range(4) for x in ("Tq", "Tk")])

        @block.sync
        def _(e):
            for i in range(2):
                e.dma_start(PG[:, i, :, :], O['kv_prompt'][l, 0].rearrange("(t p r) a g d -> t p r (a g d)", p=P, r=PAIRS)[i, :, :, 0:256]).then_inc(rows, 16)
            e.dma_start(QRP[:, :, :, :].rearrange("p t i c -> p t (i c)"), A['q_rot'].rearrange("(t p) c -> p t c", p=P)).then_inc(rows, 16)
            dve.wait(e, "z0")
            for kv in range(2):
                for half in range(2):
                    for r in range(PAIRS):
                        e.dma_start(W1[r * HD:(r + 1) * HD, kv, :, half * HD:(half + 1) * HD],
                                    A['cmp_w1'][l, kv].rearrange("(h s r) d e -> h r d s e", h=2, r=PAIRS)[half, r]).then_inc(weights, 16)
                for g in range(G):
                    e.dma_start(W2[:, kv, g, g * HD:(g + 1) * HD], A['cmp_w2'][l, kv]).then_inc(weights, 16)
            e.dma_start(B1[:, :], A['cmp_b1'][l].rearrange("k e -> e k"), allow_slow_non_contiguous=True).then_inc(weights, 16)

        @block.tensor
        def _(e):
            e.wait_ge(weights, 13 * 16)
            e.wait_ge(rows, 48)
            cp.pe(e, pool, pe, act, dve)
            dve.wait(e, "C1")
            for t in range(4):
                if t:
                    dve.wait(e, f"Tq{t-1}")
                for r in range(R):
                    mm = nc.tensor.transpose(bk(0, 4)[:, r, :], QRP[:, t, 0, r * P:(r + 1) * P], ident)
                pe.done(e, f"Tq{t}", mm)
                if t:
                    act.wait(e, f"Tr{t-1}")
                for r in range(R):
                    mm = nc.tensor.transpose(bk(1, 4)[:, r, :], QRP[:, t, 1, r * P:(r + 1) * P], ident)
                pe.done(e, f"Tr{t}", mm)
                if t:
                    dve.wait(e, f"Tk{t-1}")
                for i in range(2):
                    mm = nc.tensor.transpose(bk(2, 4)[:, i, :], U[t][:, NKV + 256 * (i + 1):NKV + 256 * (i + 1) + P], ident)
                pe.done(e, f"Tk{t}", mm)

        @block.gpsimd
        def _(e):
            e.wait_ge(rows, 48)
            cp.pool(e, pool, pe)

        @block.scalar
        def _(e):
            e.wait_ge(weights, 13 * 16)
            dve.wait(e, "z1")
            cp.act(e, pe, act, dve)
            for t in range(4):
                pe.wait(e, f"Tr{t}")
                act.done(e, f"Tr{t}", nc.scalar.activation(QT[:, 1, :, t * P:(t + 1) * P], bk(1, 4), ACT.Copy))

        @block.vector
        def _(e):
            dve.link(e, "z0", nc.vector.memset(W2[:, :, :, :], 0.0))
            dve.link(e, "z1", nc.vector.memset(HS[:, :, :], 0.0))
            cp.dve(e, pe, act, dve)
            for t in range(4):
                pe.wait(e, f"Tq{t}")
                dve.done(e, f"Tq{t}", nc.vector.tensor_copy(QT[:, 0, :, t * P:(t + 1) * P], bk(0, 4)))
                pe.wait(e, f"Tk{t}")
                dve.done(e, f"Tk{t}", nc.vector.tensor_copy(KT[:, :, t * P:(t + 1) * P], bk(2, 4)[:, 0:2, :]))

    early.close()
    Pr = sb(scope, "Pr", [P, 2, SEQ])
    PT = sb(scope, "PT", [P, 2, 4, P])
    mx = sb(scope, "mx", [P, 2, 2])
    SUM = sb(scope, "SUM", [P, 2, NH])
    fac = sb(scope, "fac", [P, NH])
    T1 = sb(scope, "T1", [P, 512])
    NO = sb(scope, "NO", [P, 512])
    units = [(qt, br, h) for qt in range(4) for br in range(3) for h in range(NH)]
    NU = len(units)
    with stage(["score", "shift", "exped", "turned", "copied", "used", "link_s", "merged"]) as \
            (block, (score, shift, exped, turned, copied, used, link_s, merged)):

        def keys(u):
            qt, br, h = units[u]
            return NCP if br == 0 else (qt + 1) * P

        @block.tensor
        def _(e):
            def scores(u):
                qt, br, h = units[u]
                g, r, n = h // R, h % R, keys(u)
                if u >= 2:
                    e.wait_ge(exped, u - 1)
                kt = KC[g * HD:(g + 1) * HD, 0:n] if br == 0 else KT[g * HD:(g + 1) * HD, br - 1, 0:n]
                nc.tensor.matmul(bk(u % 2)[:, 0:n], QT[g * HD:(g + 1) * HD, min(br, 1), r, qt * P:(qt + 1) * P], kt, start=True, stop=False)
                m = cb('cmask', 32)[:, qt, 0:n] if br == 0 else cb('causal')
                nc.tensor.matmul(bk(u % 2)[:, 0 if br == 0 else qt * P:n], cb('identb'), m, start=False, stop=True).then_inc(score, 1)

            def turn(u):
                n = keys(u)
                e.wait_ge(exped, u + 1)
                if u >= 2:
                    e.wait_ge(copied, u - 1)
                for j in range(-(-n // P)):
                    m = min(P, n - j * P)
                    mm = nc.tensor.transpose(bk(2 + u % 2, 4)[0:m, j, :], Pr[:, u % 2, j * P:j * P + m], ident)
                mm.then_inc(turned, 1)

            def values(u):
                qt, br, h = units[u]
                g, n, q = h // R, keys(u), u // NH
                e.wait_ge(copied, u + 1)
                if h == 0 and q >= 2:
                    e.wait_ge(merged, q - 1)
                for j in range(-(-n // P)):
                    m = min(P, n - j * P)
                    vv = VC[0:m, 0, g * HD:(g + 1) * HD] if br == 0 else U[j][:, NKV + P + 256 * br + g * HD:NKV + P + 256 * br + (g + 1) * HD]
                    mm = nc.tensor.matmul(bk(4 + q % 2)[:, h * HD:(h + 1) * HD], PT[0:m, u % 2, j, :], vv, start=(j == 0), stop=(j == -(-n // P) - 1))
                mm.then_inc(used, 1)

            for u in range(NU + 2):
                if u < NU:
                    scores(u)
                if 0 < u <= NU:
                    turn(u - 1)
                if u >= 2:
                    values(u - 2)

        @block.scalar
        def _(e):
            for u in range(NU):
                qt, br, h = units[u]
                n = keys(u)
                e.wait_ge(shift, u + 1)
                if u >= 2:
                    e.wait_ge(turned, u - 1)
                nc.scalar.activation(Pr[:, u % 2, 0:n], bk(u % 2)[:, 0:n], ACT.Exp, scale=SCALE, bias=mx[:, u % 2, 1:2],
                                     accum_out=SUM[:, (u // NH) % 2, h:h + 1]).then_inc(exped, 1)

        @block.vector
        def _(e):
            links = [0]

            def link(ins):
                links[0] += 1
                ins.then_inc(link_s, 1)
                e.wait_ge(link_s, links[0])

            def biggest(u):
                n = keys(u)
                e.wait_ge(score, u + 1)
                link(nc.vector.tensor_reduce(mx[:, u % 2, 0:1], bk(u % 2)[:, 0:n], AX.X, ALU.max))
                nc.vector.tensor_scalar(mx[:, u % 2, 1:2], mx[:, u % 2, 0:1], -1e20, -SCALE, ALU.max, ALU.mult).then_inc(shift, 1)

            def copy(u):
                n = keys(u)
                m, k = (n, 1) if n < P else (P, n // P)
                e.wait_ge(turned, u + 1)
                if u >= 2:
                    e.wait_ge(used, u - 1)
                nc.vector.tensor_copy(PT[0:m, u % 2, 0:k, :], bk(2 + u % 2, 4)[0:m, 0:k, :]).then_inc(copied, 1)

            def merge(u):
                qt, br, h = units[u]
                q = u // NH
                hb = lambda ap: ap.rearrange("p (h c) -> p h c", c=HD)
                e.wait_ge(used, u + 1)
                e.wait_ge(exped, u + 1)
                link(nc.vector.tensor_scalar(fac[:, :], SUM[:, q % 2, :], 1e-30, None, ALU.max))
                link(nc.vector.reciprocal(fac[:, :], fac[:, :]))
                link(nc.vector.tensor_tensor(fac[:, :], fac[:, :], U[qt][:, NGATE + br * NH:NGATE + (br + 1) * NH], ALU.mult))
                dst = NO if br == 0 else T1
                links[0] += 1
                nc.vector.tensor_tensor(hb(dst[:, :]), hb(bk(4 + q % 2)), b_(fac[:, :], 2, [P, NH, HD]), ALU.mult).then_inc(link_s, 1)
                e.wait_ge(link_s, links[0])
                if br:
                    link(nc.vector.tensor_tensor(NO[:, :], NO[:, :], T1[:, :], ALU.add))
                if br == 2:
                    link(nc.vector.tensor_tensor(MIX[:, qt, 256:768], NO[:, :], U[qt][:, NG:NG + 512], ALU.mult))
                nc.vector.engine_nop().then_inc(merged, 1)

            for u in range(NU + 2):
                if u < NU:
                    biggest(u)
                if 0 < u <= NU:
                    copy(u - 1)
                if u >= 2 and (u - 2) % NH == NH - 1:
                    merge(u - 2)


def sample_attention(nc, A, O, l, scope, sb, stage, v):
    bk, cf, cb, ident, MIX, US = v['bk'], v['cf'], v['cb'], v['ident'], v['MIX'], v['US']
    PC = sb(scope, "PC", [P, GT, PAIRS, 256])
    PS = sb(scope, "PS", [P, GT, PAIRS, 256])
    PSg = PS[:, :, :, :].rearrange("p i r c -> p (i r) c")
    HT = sb(scope, "HT", [P, 512])
    HS = sb(scope, "HS", [HD, G, NSEG])
    KC = sb(scope, "KC", [P, NSEG])
    VC = sb(scope, "VC", [P, 2, P])
    PW = sb(scope, "PW", [P, 4, 256])
    PB = sb(scope, "PB", [P, 2 + 5 + NKEYG, COLS])
    QBD = sb(scope, "QBD", [P, 2, NB, COLS])
    QB = sb(scope, "QB", [P, 2, COLS])
    KNT = sb(scope, "KNT", [P, 2, NB * NT])
    KN = sb(scope, "KN", [P, 2, P])
    VN = sb(scope, "VNn", [P, 2, P])
    OT = sb(scope, "OT", [P, 3, R, NB, NT])
    RP = sb(scope, "RP", [P, 4, 2 * G, PAIRS, HD])
    MX = sb(scope, "MX", [P, 6, COLS])
    sm = sb(scope, "sm", [P, 5, COLS])
    PR = sb(scope, "PR", [P, 2, 2, COLS])
    m1 = sb(scope, "m1", [COLS, 1])
    nd = sb(scope, "nd", [COLS, COLS])
    top = sb(scope, "top", [16, 3, NBLK + 1])
    t8 = sb(scope, "t8", [16, 2, 8])
    BT = sb(scope, "BT", [HD, COLS], BF16)
    ids = sb(scope, "ids", [1, (NB + 1) * NPAGE], I32)

    def load_pages(e, dst, c, row, sem):
        for pg in range(NPAGE):
            page = e.value_load(ids[0:1, bass.ds(row * NPAGE + pg, 1)], min_val=0, max_val=NPHYS - 1)
            o = (pg % 2) * HD
            e.dma_start(dst[o:o + HD, pg // 2, :, :],
                        A['cache_nsa_kv'][l, page].rearrange("(p r) a g d -> p r (a g d)", r=PAIRS)[:, :, c:c + 256]).then_inc(sem, 16)

    with stage(["dve_s", "pe_s", "kv", "idl", "first"]) as (block, (dve_s, pe_s, kv, idl, first)):
        dve = Steps(dve_s, ["z0", "z1", "z2", "z3"] + [f"q{i}{g}" for i in range(2) for g in range(G)] + ["k"])
        pe = Steps(pe_s, ["q0", "q1", "k"])

        @block.sync
        def _(e):
            e.dma_start(ids[0:1, 0:NB * NPAGE], A['page_table'].rearrange("b n -> (b n)").unsqueeze(0)).then_inc(idl, 16)
            e.dma_start(ids[0:1, NB * NPAGE:], A['page_table'][0:1, :]).then_inc(idl, 16)
            e.dma_start(A['new_kv'].rearrange("b t c -> (b t) c"), US[0:64, NKV:NKV + CW]).then_inc(kv, 16)
            e.wait_ge(idl, 32)
            load_pages(e, PC, 0, 0, first)
            e.wait_ge(first, NPAGE * 16)
            e.wait_ge(kv, 16)

        @block.tensor
        def _(e):
            for i in range(2):
                for r in range(R):
                    mm = nc.tensor.transpose(bk(i, 8)[:, r, 0:64], v['QRS'][0:64, i, r * P:(r + 1) * P], ident[0:64, 0:64])
                pe.done(e, f"q{i}", mm)
            for i in range(2):
                mm = nc.tensor.transpose(bk(2, 8)[:, i, 0:64], US[0:64, NKV + 256 * (i + 1):NKV + 256 * (i + 1) + P], ident[0:64, 0:64])
            pe.done(e, "k", mm)

        @block.vector
        def _(e):
            dve.done(e, "z0", nc.vector.memset(QBD[:, :, :, :], 0.0))
            dve.done(e, "z1", nc.vector.memset(KN[:, :, :], 0.0))
            dve.done(e, "z2", nc.vector.memset(VN[:, :, :], 0.0))
            dve.link(e, "z3", nc.vector.memset(HS[:, :, :], 0.0))
            for i in range(2):
                pe.wait(e, f"q{i}")
                for g in range(G):
                    o = g * HD
                    dve.done(e, f"q{i}{g}", nc.vector.tensor_copy(
                        QBD[o:o + HD, i, :, g * 32:(g + 1) * 32].rearrange("p b (r t) -> p b r t", r=R),
                        bk(i, 8)[o:o + HD, 0:R, 0:64].rearrange("p r (b t) -> p b r t", b=NB)))
            pe.wait(e, "k")
            dve.done(e, "k", nc.vector.tensor_copy(KNT[:, :, :], bk(2, 8)[:, 0:2, 0:64]))

    B4 = bk(4, 8)
    parts = {'c': [(B4[:, 0:2, :], 0, 2)], 'w': [(B4[:, 2:7, :], 2, 5)],
             's': [(bk(j, 8), 7 + 8 * j, 8) for j in range(4)] + [(B4[:, 7:8, :], 7 + 32, 1)]}
    BR = {'c': 0, 's': 1, 'w': 2}
    M = bk(5)
    with nc.Fori(0, NB) as b:
        with stage(["dve_s", "act_s", "pe_s", "pool_s", "sel_rows", "win_rows", "next_rows"]) as \
                (block, (dve_s, act_s, pe_s, pool_s, sel_rows, win_rows, next_rows)):
            cp = Compress(v, GT, PC, RP, HT, HS, KC, VC)
            pool = Steps(pool_s, cp.pool_names)
            chain_pe = lambda a: [f"{a}{x}" for x in ("mt", "nb", "sb", "pv")]
            pe = Steps(pe_s, cp.pe_names + ["wt", "c4", "cmt", "kt0", "kt1", "cnb"] + [f"k{j}" for j in range(6)] +
                       ["csb", "cpv", "sc", "k6", "k7", "scT"] + chain_pe("w")[:2] + ["bias"] + chain_pe("w")[2:] + chain_pe("s"))
            act = Steps(act_s, cp.act_names + ["wt", "kt0", "kt1"] + ["kt2", "kt3", "ce", "kt4", "kt5", "kt6", "kt7", "we", "se"])

            def chain_dve(a):
                n = len(parts[a])
                return ([f"{a}x{j}" for j in range(n)] + ([f"{a}x"] if n > 1 else []) + [f"{a}m", f"{a}nd", f"{a}nm"] +
                        [f"{a}s{j}" for j in range(n)] + [f"{a}ps", f"{a}cl", f"{a}rc"])

            dve = Steps(dve_s, ["qb", "kn"] + cp.dve_names + chain_dve('c') + ["pn", "pr0", "pr1", "co0", "co1", "sf", "t1", "r1", "t2", "r2", "bi", "bt"] +
                        chain_dve('w') + ["wo0", "wo1"] + chain_dve('s') + ["so0", "so1"])

            @block.sync
            def _(e):
                e.dma_start(PW[:, :, :], A['state_nsa_win'][l, b].rearrange("(c p) a g d -> p c (a g d)", p=P)).then_inc(win_rows, 16)
                for i in range(2):
                    e.dma_start(VN[0:NT, i, :], A['new_kv'][b][:, 256 * (i + 1) + P:256 * (i + 2)]).then_inc(win_rows, 16)
                load_pages(e, PS, 256, b, sel_rows)
                pe.wait(e, "H1")
                load_pages(e, PC, 0, b + 1, next_rows)
                e.wait_ge(sel_rows, NPAGE * 16)
                e.wait_ge(next_rows, NPAGE * 16)

            @block.gpsimd
            def _(e):
                cp.pool(e, pool, pe)

            @block.tensor
            def _(e):
                cp.pe(e, pool, pe, act, dve)
                e.wait_ge(win_rows, 48)
                for c in range(4):
                    mm = nc.tensor.transpose(bk(6, 4)[:, c, :], PW[:, c, 0:P], ident)
                pe.done(e, "wt", mm)
                act.wait(e, "wt")
                dve.wait(e, "C1")
                for c in range(2):
                    nc.tensor.matmul(B4[:, c, :], KC[:, c * P:(c + 1) * P], QB[:, 0, :], start=True, stop=(c == 0))
                    if c:
                        nc.tensor.matmul(B4[:, c, :], cb('identb'), cb('padmask'), start=False, stop=True)
                for c in range(4):
                    nc.tensor.matmul(B4[:, 2 + c, :], PW[:, c, 0:P], QB[:, 1, :], start=True, stop=(c > 0))
                    if c == 0:
                        nc.tensor.matmul(B4[:, 2, :], cb('identb'), cb('winmask'), start=False, stop=True)
                for i, c in ((1, 6), (0, 7)):
                    nc.tensor.matmul(B4[:, c, :], KN[:, i, :], QB[:, 1, :], start=True, stop=False)
                    mm = nc.tensor.matmul(B4[:, c, :], cb('identb'), cb('newmask'), start=False, stop=True)
                pe.done(e, "c4", mm)

                def max_t(a):
                    dve.wait(e, f"{a}x" if a == 's' else f"{a}x0")
                    pe.done(e, f"{a}mt", nc.tensor.transpose(M[0:COLS, 0:P], MX[:, 5, :], ident))

                def neg_b(a):
                    dve.wait(e, f"{a}nd")
                    pe.done(e, f"{a}nb", nc.tensor.matmul(M[:, P:P + COLS], v['ones'][0:COLS, :], nd[:, :], start=True, stop=True))

                def sum_b(a):
                    dve.wait(e, f"{a}ps")
                    pe.done(e, f"{a}sb", nc.tensor.matmul(M[:, 192:256], v['ones'][:, :], sm[:, 1, :], start=True, stop=True))

                def values(a):
                    vs = {'c': [VC[:, c, :] for c in range(2)],
                          'w': [PW[:, c, P:256] for c in range(4)] + [VN[:, 1, :]],
                          's': [PSg[:, i, P:256] for i in range(2 * GT)] + [VN[:, 0, :]]}[a]
                    o = parts[a][0][1]
                    dve.wait(e, f"{a}rc")
                    for i, vv in enumerate(vs):
                        mm = nc.tensor.matmul(M[:, 256:320], vv, PB[:, o + i, :], start=(i == 0), stop=(i == len(vs) - 1))
                    pe.done(e, f"{a}pv", mm)

                def key_t(j):
                    if j < 2:
                        if j == 0:
                            e.wait_ge(sel_rows, NPAGE * 16)
                            act.wait(e, "wt")
                    else:
                        act.wait(e, f"kt{j-2}")
                    for c in range(4):
                        i = 4 * j + c
                        mm = nc.tensor.transpose(bk(6 + j % 2, 4)[:, c, :], PSg[:, i, 0:P], ident)
                    return mm

                def key_scores(j):
                    act.wait(e, f"kt{j}")
                    if j + 2 < 8:
                        key_t(j + 2)
                    for c in range(4):
                        i = 4 * j + c
                        mm = nc.tensor.matmul(bk(i // 8, 8)[:, i % 8, :], PSg[:, i, 0:P], QB[:, 1, :], start=(i % 8 == 0), stop=False,
                                              skip_group_check=True)
                    pe.done(e, f"k{j}", mm)

                max_t('c')
                for j in range(2):
                    pe.done(e, f"kt{j}", key_t(j))
                neg_b('c')
                for j in range(6):
                    key_scores(j)
                sum_b('c')
                values('c')
                dve.wait(e, "co1")
                for c in range(2):
                    mm = nc.tensor.matmul(M[0:16, 320:320 + NBLK], PR[:, 1, c, 0:16], cf('overlap', NBLK)[:, c, :], start=(c == 0), stop=(c == 1))
                pe.done(e, "sc", mm)
                key_scores(6)
                key_scores(7)
                dve.wait(e, "bi")
                pe.done(e, "scT", nc.tensor.transpose(M[0:HD, 400:416], top[:, 1, 0:HD], ident[0:16, 0:16]))
                dve.wait(e, "bt")
                max_t('w')
                neg_b('w')
                for i in range(GT):
                    mm = nc.tensor.matmul(bk(i // 4, 8)[:, 2 * (i % 4):2 * (i % 4) + 2, :], cb('blockof', P)[0:HD, i, :],
                                          b_(BT[:, :], 1, [HD, 2, COLS]), start=False, stop=(i % 4 == 3), skip_group_check=True)
                pe.done(e, "bias", mm)
                sum_b('w')
                values('w')
                max_t('s')
                neg_b('s')
                sum_b('s')
                values('s')

            @block.scalar
            def _(e):
                cp.act(e, pe, act, dve)
                pe.wait(e, "wt")
                act.done(e, "wt", nc.scalar.activation(PW[:, :, 0:P], bk(6, 4), ACT.Copy))

                def kt(j):
                    pe.wait(e, f"kt{j}" if j < 2 else f"k{j-2}")
                    act.done(e, f"kt{j}", nc.scalar.activation(PSg[:, 4 * j:4 * j + 4, 0:P], bk(6 + j % 2, 4), ACT.Copy))

                def ex(a):
                    p = parts[a]
                    dve.wait(e, f"{a}s{len(p)-1}")
                    ap = PB[:, p[0][1]:p[-1][1] + p[-1][2], :]
                    act.done(e, f"{a}e", nc.scalar.activation(ap, ap, ACT.Exp, scale=SCALE))

                for j in range(4):
                    kt(j)
                ex('c')
                for j in range(4, 8):
                    kt(j)
                ex('w')
                ex('s')

            @block.vector
            def _(e):
                dve.done(e, "qb", nc.vector.tensor_copy(QB[:, :, :], QBD[:, :, bass.ds(b, 1), :].rearrange("p i b c -> p i (b c)")))
                dve.done(e, "kn", nc.vector.tensor_copy(KN[:, :, 0:NT], KNT[:, :, bass.ds(b * NT, NT)]))
                cp.dve(e, pe, act, dve)

                def chain(a):
                    p = parts[a]
                    if a == 'c':
                        pe.wait(e, "c4")
                    if a == 's':
                        pe.wait(e, "bias")
                    n = len(p)
                    for j, (src, o, ng) in enumerate(p):
                        dve.link(e, f"{a}x{j}", nc.vector.tensor_reduce(MX[:, j if n > 1 else 5, :], src.rearrange("p n c -> p c n"), AX.X, ALU.max))
                    if n > 1:
                        dve.link(e, f"{a}x", nc.vector.tensor_reduce(MX[:, 5, :], MX[:, 0:n, :].rearrange("p n c -> p c n"), AX.X, ALU.max))
                    pe.wait(e, f"{a}mt")
                    dve.link(e, f"{a}m", nc.vector.tensor_reduce(m1[:, :], M[0:COLS, 0:P], AX.X, ALU.max))
                    dve.link(e, f"{a}nd", nc.vector.tensor_scalar(nd[:, :], ident[0:COLS, 0:COLS], m1[:, 0:1], -1.0, ALU.mult, ALU.mult))
                    pe.wait(e, f"{a}nb")
                    dve.link(e, f"{a}nm", nc.vector.tensor_copy(sm[:, 0, :], M[:, P:P + COLS]))
                    for j, (src, o, ng) in enumerate(p):
                        dve.done(e, f"{a}s{j}", nc.vector.tensor_tensor(PB[:, o:o + ng, :], src, b_(sm[:, 0, :], 1, [P, ng, COLS]), ALU.add))
                    act.wait(e, f"{a}e")
                    dve.link(e, f"{a}ps", nc.vector.tensor_reduce(sm[:, 1, :], PB[:, p[0][1]:p[-1][1] + p[-1][2], :].rearrange("p n c -> p c n"), AX.X, ALU.add))
                    pe.wait(e, f"{a}sb")
                    dve.link(e, f"{a}cl", nc.vector.tensor_scalar(sm[:, 2, :], M[:, 192:256], 1e-30, None, ALU.max))
                    dve.link(e, f"{a}rc", nc.vector.reciprocal(sm[:, 3, :], sm[:, 2, :]))

                def outs(a):
                    pe.wait(e, f"{a}pv")
                    for g in range(G):
                        o = g * HD
                        dve.link(e, f"{a}o{g}", nc.vector.tensor_tensor(OT[o:o + HD, BR[a], :, bass.ds(b, 1), :].rearrange("p r b t -> p r (b t)"),
                                                                         M[o:o + HD, 256 + g * 32:256 + (g + 1) * 32].rearrange("p (r t) -> p r t", r=R),
                                                                         sm[o:o + HD, 3, g * 32:(g + 1) * 32].rearrange("p (r t) -> p r t", r=R), ALU.mult))

                chain('c')
                dve.link(e, "pn", nc.vector.tensor_tensor(PR[:, 0, :, :], PB[:, 0:2, :], b_(sm[:, 3, :], 1, [P, 2, COLS]), ALU.mult))
                for c in range(2):
                    dve.link(e, f"pr{c}", nc.vector.tensor_reduce(PR[:, 1, c, 0:16].rearrange("p (g t) -> p g t", g=G),
                                                                   PR[:, 0, c, :].rearrange("p (g r t) -> p g t r", g=G, r=R), AX.X, ALU.add))
                outs('c')
                pe.wait(e, "sc")
                dve.link(e, "sf", nc.vector.tensor_tensor(top[:, 0, 0:NBLK], M[0:16, 320:320 + NBLK], cf('force')[0:16, :], ALU.add))
                dve.link(e, "t1", nc.vector.max(t8[:, 0, :], top[:, 0, 0:NBLK]))
                dve.link(e, "r1", nc.vector.match_replace(top[:, 1, 0:NBLK], t8[:, 0, :], top[:, 0, 0:NBLK], -1.0))
                dve.link(e, "t2", nc.vector.max(t8[:, 1, :], top[:, 1, 0:NBLK]))
                dve.link(e, "r2", nc.vector.match_replace(top[:, 2, 0:NBLK], t8[:, 1, :], top[:, 1, 0:NBLK], -1.0))
                dve.link(e, "bi", nc.vector.tensor_scalar(top[:, 1, 0:NBLK], top[:, 2, 0:NBLK], -0.5, NEG, ALU.is_gt, ALU.mult))
                pe.wait(e, "scT")
                dve.link(e, "bt", nc.vector.tensor_copy(BT[:, :].rearrange("p (g r t) -> p g r t", g=G, r=R),
                                                         M[0:HD, 400:416].rearrange("p (g t) -> p g t", g=G).unsqueeze(2).broadcast_to([HD, G, R, NT])))
                chain('w')
                outs('w')
                chain('s')
                outs('s')

    NO = sb(scope, "NOs", [64, 3, 512])
    with stage(["dve_s", "pe_s"]) as (block, (dve_s, pe_s)):
        dve = Steps(dve_s, ["m0", "m1", "a1", "m2", "a2", "mix"])
        pe = Steps(pe_s, ["t0", "t1", "t2"])

        @block.tensor
        def _(e):
            for i in range(3):
                for r in range(R):
                    mm = nc.tensor.transpose(bk(i, 4)[0:64, r, :], OT[:, i, r, :, :].rearrange("p b t -> p (b t)"), ident)
                pe.done(e, f"t{i}", mm)

        @block.vector
        def _(e):
            for i in range(3):
                pe.wait(e, f"t{i}")
                dve.link(e, f"m{i}", nc.vector.tensor_tensor(
                    NO[:, i, :].rearrange("p (g r d) -> p g r d", g=G, r=R), bk(i)[0:64, :].rearrange("p (r g d) -> p g r d", r=R, g=G),
                    US[0:64, NGATE + i * NH:NGATE + (i + 1) * NH].rearrange("p (g r) -> p g r", g=G).unsqueeze(3).broadcast_to([64, G, R, HD]), ALU.mult))
                if i:
                    dve.link(e, f"a{i}", nc.vector.tensor_tensor(NO[:, 0, :], NO[:, 0, :], NO[:, i, :], ALU.add))
            dve.link(e, "mix", nc.vector.tensor_tensor(MIX[0:64, 4, 256:768], NO[:, 0, :], US[0:64, NG:NG + 512], ALU.mult))


def out_project(nc, A, l, scope, sb, stage, v):
    X, MIX, ident, bk = v['X'], v['MIX'], v['ident'], v['bk']
    mT = sb(scope, "mT", [P, KD, 4 * P + 64])
    W = sb(scope, "Wo", [P, KD, D])
    YO = sb(scope, "YO", [P, 2, D])
    sq = sb(scope, "sq", [P, D])
    ss = sb(scope, "ss", [P, NTILE])
    gpost = sb(scope, "gpost", [P, D])
    with stage(["w_half", "gain", "act_s", "dve_s", "pe_s"]) as (block, (w_half, gain, act_s, dve_s, pe_s)):
        pe = Steps(pe_s, [f"T{t}" for t in range(NTILE)] + [f"{x}{t}" for t in range(NTILE) for x in ("y0", "y1")])
        dve = Steps(dve_s, [f"{x}{t}" for t in range(NTILE) for x in ("m0", "m1")] + [f"{x}{t}" for t in range(NTILE) for x in ("rc", "g", "x")])
        act = Steps(act_s, [f"{x}{t}" for t in range(NTILE) for x in ("c0", "c1", "sq", "rt")])

        @block.sync
        def _(e):
            e.dma_start(gpost[:, :], A['norm_post'][l].partition_broadcast(P)).then_inc(gain, 16)
            wv = A['w_out'][l].rearrange("(k p) c -> p k c", p=P)
            for h in range(2):
                e.dma_start(W[:, :, h * 512:(h + 1) * 512], wv[:, :, h * 512:(h + 1) * 512]).then_inc(w_half, 16)

        @block.tensor
        def _(e):
            for t in range(NTILE):
                n = ROWS[t]
                if t >= 2:
                    dve.wait(e, f"m1{t-2}")
                for k in range(KD):
                    mm = nc.tensor.transpose(bk(2 * (t % 2) + k // 4, 4)[:, k % 4, 0:n], MIX[0:n, t, k * P:(k + 1) * P], ident[0:n, 0:n])
                pe.done(e, f"T{t}", mm)
            e.wait_ge(w_half, 32)
            for t in range(NTILE):
                n = ROWS[t]
                dve.wait(e, f"m1{t}")
                if t >= 2:
                    act.wait(e, f"c1{t-2}")
                for h in range(2):
                    for k in range(KD):
                        mm = nc.tensor.matmul(bk(4 + 2 * (t % 2) + h)[0:n, :], mT[:, k, t * P:t * P + n], W[:, k, h * 512:(h + 1) * 512],
                                              start=(k == 0), stop=(k == KD - 1))
                    pe.done(e, f"y{h}{t}", mm)

        @block.scalar
        def _(e):
            for t in range(NTILE):
                n = ROWS[t]
                if t >= 2:
                    dve.wait(e, f"x{t-2}")
                for h in range(2):
                    pe.wait(e, f"y{h}{t}")
                    act.link(e, f"c{h}{t}", nc.scalar.activation(YO[0:n, t % 2, h * 512:(h + 1) * 512], bk(4 + 2 * (t % 2) + h)[0:n, :], ACT.Copy))
                act.link(e, f"sq{t}", nc.scalar.activation(sq[0:n, :], YO[0:n, t % 2, :], ACT.Square, accum_out=ss[0:n, t:t + 1]))
                act.link(e, f"rt{t}", nc.scalar.activation(ss[0:n, t:t + 1], ss[0:n, t:t + 1], ACT.Sqrt, scale=1.0 / D, bias=v['eps'][0:n, :]))

        @block.vector
        def _(e):
            for t in range(NTILE):
                n = ROWS[t]
                pe.wait(e, f"T{t}")
                for h in range(2):
                    dve.done(e, f"m{h}{t}", nc.vector.tensor_copy(mT[:, 4 * h:4 * h + 4, t * P:t * P + n], bk(2 * (t % 2) + h, 4)[:, :, 0:n]))
            e.wait_ge(gain, 16)
            for t in range(NTILE):
                n = ROWS[t]
                y = YO[0:n, t % 2, :]
                act.wait(e, f"rt{t}")
                dve.link(e, f"rc{t}", nc.vector.reciprocal(ss[0:n, t:t + 1], ss[0:n, t:t + 1]))
                dve.link(e, f"g{t}", nc.vector.scalar_tensor_tensor(y, y, ss[0:n, t:t + 1], gpost[0:n, :], ALU.mult, ALU.mult))
                dve.link(e, f"x{t}", nc.vector.tensor_tensor(X[0:n, t, :], X[0:n, t, :], y, ALU.add))



INPUTS = ['x_prompt', 'x_sample', 'cache_nsa_kv', 'page_table', 'state_nsa_win', 'state_ret', 'state_gdn', 'state_gdn_conv',
          'w_in', 'w_out', 'norm_pre', 'norm_post', 'ret_gn', 'gdn_norm', 'gdn_conv', 'gdn_a_log', 'gdn_dt_bias',
          'cmp_w1', 'cmp_b1', 'cmp_w2']
OUTPUTS = [('y_prompt', (1, SEQ, D)), ('y_sample', (NB, NT, D)),
           ('kv_prompt', (DEPTH, 1, SEQ, 4, G, HD)), ('kv_sample', (DEPTH, NB, NT, 4, G, HD)),
           ('win_prompt', (DEPTH, 1, WIN, 2, G, HD)), ('win_sample', (DEPTH, NB, WIN, 2, G, HD)),
           ('ret_prompt', (DEPTH, 1, H4, HD, HD)), ('ret_sample', (DEPTH, NB, H4, HD, HD)),
           ('gdn_prompt', (DEPTH, 1, H4, HD, HD)), ('gdn_sample', (DEPTH, NB, H4, HD, HD)),
           ('conv_prompt', (DEPTH, 1, CONV - 1, CW)), ('conv_sample', (DEPTH, NB, CONV - 1, CW))]
SCRATCH = [('conv_p', (SEQ + 3, CW)), ('conv_s', (NB, NT + 3, CW)), ('q_rot', (SEQ, 1024)), ('new_kv', (NB, NT, CW))]


def kernel(**inputs):
    import ml_dtypes
    import concourse.bacc as bacc
    from concourse.bass_utils import run_bass_kernel_spmd

    nc = bacc.Bacc("TRN2", target_bir_lowering=False, num_devices=1)
    arrays = {n: np.ascontiguousarray(inputs[n]) for n in INPUTS}
    arrays['cf'] = np.concatenate(list(constants().values()), 1)
    arrays['cb'] = np.concatenate(list(bf_constants().values()), 1).astype(ml_dtypes.bfloat16)
    A = {n: nc.dram_tensor(f"in_{n}", a.shape, mybir.dt.from_np(a.dtype), kind="ExternalInput").ap() for n, a in arrays.items()}
    O = {n: nc.dram_tensor(f"out_{n}", s, F32, kind="ExternalOutput").ap() for n, s in OUTPUTS}
    for n, s in SCRATCH:
        A[n] = nc.dram_tensor(f"scratch_{n}", s, F32, kind="Internal").ap()
    build(nc, A, O)
    r = run_bass_kernel_spmd(nc, [{f"in_{n}": a for n, a in arrays.items()}], core_ids=[0])
    return tuple(r.results[0][f"out_{n}"] for n, _ in OUTPUTS)
```

```python
import concourse.bass as bass
from concourse import mybir
from contextlib import ExitStack, contextmanager
import numpy as np

F32 = mybir.dt.float32
BF16 = mybir.dt.bfloat16
I32 = mybir.dt.int32
ALU = mybir.AluOpType
ACT = mybir.ActivationFunctionType
AX = mybir.AxisListType

D = 1024
SEQ = 512
DEPTH = 2
NB, NT = 8, 8
PAST = 4096
PAGE = 128
HD = 64
H4 = 4
NH, G, R = 8, 2, 4
WIN = 512
NPHYS = 320
NPAGE = PAST // PAGE
P = 128
KD = D // P
NTILE = 5
ROWS = [P, P, P, P, NB * NT]
CONV = 4
CW = 768
EPS = 1e-6
NEG = -1e30
SCALE = HD ** -0.5
RQ, RK, RV, RG = 0, 256, 512, 768
NQ, NKV, NGATE, NG = 1024, 1536, 2304, 2328
GQKV, GB, GA, GG = 2840, 3608, 3612, 3616
PROJ = 3872
SEL_BLOCK = 64
NSEL = 16
NBLK = PAST // SEL_BLOCK + 1
PAIRS = 2
GT = PAST // (P * PAIRS)
SEG = 16
NSEG = PAST // SEG
NSEGP = SEQ // SEG
NCP = NSEGP - 1
COLS = NH * NT
NKEYG = 2 * GT + 1



def constants():
    c = {}
    i = np.arange(P)
    c['ident'] = np.eye(P)
    half = HD // 2
    inv = (np.float32(10000.0) ** (-np.arange(half, dtype=np.float32) / np.float32(half))).astype(np.float32)
    pos = np.zeros((P, NTILE), np.float32)
    for t in range(4):
        pos[:, t] = t * P + i
    pos[:, 4] = PAST + i % NT
    ang = (pos[:, :, None] * inv[None, None, :]).astype(np.float32).astype(np.float64)
    c['cos'] = np.cos(ang)
    c['sin'] = np.sin(ang)
    blk = [np.ones((P, P)), np.zeros((P, P))]
    j = i[:, None]
    k = i[None, :]
    blk[1][:64, :64] = (j[:64] // NT == k[:, :64] // NT)
    c['same'] = np.stack(blk, 1)
    c['tri'] = np.stack([b * (j <= k) for b in blk], 1)
    c['neg'] = (1 - c['tri']) * NEG
    lev = np.zeros((P, 7, P))
    for s in range(7):
        w = 1 << s
        lev[:, s] = (j // (2 * w) == k // (2 * w)) & (j % (2 * w) < w) & (k % (2 * w) >= w)
    c['level'] = lev
    c['pair'] = (j // HD == k // HD).astype(np.float64)
    lg = np.log1p(-np.exp2(-5.0 - np.arange(H4)))
    rel = (k - j).astype(np.float64)
    for n, b in enumerate(blk):
        c[f'dm{n}'] = np.stack([np.where(b * (j <= k) > 0, np.exp(np.maximum(rel, 0) * g), 0) * SCALE for g in lg], 1)
    step = [i, i % NT]
    last = [P, NT]
    c['qdec'] = np.stack([np.exp((s[:, None] + 1) * lg[None]) for s in step], 1)
    c['kdec'] = np.stack([np.exp((n - 1 - s[:, None]) * lg[None]) * SCALE for s, n in zip(step, last)], 1)
    sd = np.zeros((P, 2, 2))
    for n in range(2):
        for hp in range(2):
            sd[:, n, hp] = np.exp(last[n] * lg[2 * hp + i // HD])
    c['sdec'] = sd
    own = np.zeros((P, NB, 64))
    for b in range(NB):
        own[:, b] = (np.arange(64)[None] // NT == b)
    c['own'] = own
    c['ownrow'] = (i[:, None] // NT == np.arange(NB)[None, :])
    ci = (np.arange(2 * P) * SEG)[:, None]
    sj = (np.arange(NBLK) * SEL_BLOCK)[None, :]
    ov = ((ci < sj + SEL_BLOCK) & (ci + 2 * SEG > sj)).astype(np.float64)
    ov[255] = 0
    c['overlap'] = np.stack([ov[:P], ov[P:]], 1)
    force = np.zeros((P, NBLK))
    force[:, [0, NBLK - 2, NBLK - 1]] = -NEG
    c['force'] = force
    return {n: np.ascontiguousarray(a, np.float32).reshape(P, -1) for n, a in c.items()}


def bf_constants():
    c = {}
    i = np.arange(P)
    c['identb'] = np.eye(P)
    c['causal'] = np.where(i[None] <= i[:, None], 0, NEG)
    cm = np.zeros((P, 4, 32))
    for t in range(4):
        cm[:, t] = np.where((np.arange(32) * SEG + 2 * SEG - 1)[None] <= (t * P + i)[:, None], 0, NEG)
    c['cmask'] = cm
    be = np.zeros((P, GT, P))
    for t in range(GT):
        be[:, t] = (i[:, None] == 4 * t + i[None] // 32)
    c['blockof'] = be
    stepc = (np.arange(COLS) % NT)[None]
    c['newmask'] = np.where(i[:, None] <= stepc, 0, NEG)
    c['winmask'] = np.where(i[:, None] > stepc, 0, NEG)
    c['padmask'] = np.where(i[:, None] < P - 1, 0, NEG) + 0 * stepc
    return {n: np.ascontiguousarray(a, np.float32).reshape(P, -1) for n, a in c.items()}


KEPT = ('ident', 'overlap', 'force')


def layout(c):
    at, out = 0, {}
    for n, a in c.items():
        out[n] = (at, a.shape[1])
        at += a.shape[1]
    return out, at



class Steps:

    def __init__(self, sem, names):
        self.sem, self.names, self.at = sem, list(names), {n: i + 1 for i, n in enumerate(names)}
        assert len(self.at) == len(self.names)
        self.next = 0

    def done(self, eng, name, ins):
        assert self.next < len(self.names) and self.names[self.next] == name, (name, self.names[self.next:self.next + 2])
        self.next += 1
        return ins.then_inc(self.sem, 1)

    def link(self, eng, name, ins):
        self.done(eng, name, ins)
        eng.wait_ge(self.sem, self.next)

    def wait(self, eng, name):
        eng.wait_ge(self.sem, self.at[name])


def b_(ap, axis, shape):
    return ap.unsqueeze(axis).broadcast_to(shape)


def build(nc, A, O):
    es = ExitStack()

    used = []

    def sb(scope, name, shape, dt=F32):
        used.append(name)
        name = name if used.count(name) == 1 else f"{name}_{used.count(name)}"
        return scope.enter_context(nc.sbuf_tensor(name, shape, dt))

    @contextmanager
    def stage(sems):
        with ExitStack() as st:
            got = [st.enter_context(nc.semaphore(n)) for n in sems]
            with nc.Block() as block:
                yield block, got
            for s in got:
                nc.gpsimd.sem_clear(s)
            nc.all_engine_barrier()

    every = constants()
    cl, cn = layout({n: every[n] for n in KEPT})
    el, en = layout({n: a for n, a in every.items() if n not in KEPT})
    bl, bn = layout(bf_constants())

    with es:
        X = sb(es, "X", [P, NTILE, D])
        MIX = sb(es, "MIX", [P, NTILE, D])
        CF = sb(es, "CF", [P, cn])
        CB = sb(es, "CB", [P, bn], BF16)
        US = sb(es, "US", [P, PROJ])
        QRS = sb(es, "QRS", [P, 2, NH * HD])
        ones = sb(es, "ones", [P, P])
        W1 = sb(es, "W1", [P, 2, SEG // PAIRS, P])
        W2 = sb(es, "W2", [HD, 2, G, P])
        B1 = sb(es, "B1", [HD, 2])
        eps = sb(es, "eps", [P, 1])

        def cf(n, shape=None):
            o, w = cl[n] if n in cl else el[n]
            ap = (CF if n in cl else v['CE'])[:, o:o + w]
            if shape:
                ap = ap.rearrange("p (a b) -> p a b", b=shape)
            return ap

        def cb(n, shape=None):
            o, w = bl[n]
            ap = CB[:, o:o + w]
            if shape:
                ap = ap.rearrange("p (a b) -> p a b", b=shape)
            return ap

        ident = cf('ident')
        bank = [es.enter_context(nc.psum_tensor(f"bank{i}", [P, 512], F32)) for i in range(8)]

        def bk(i, a=None):
            ap = bank[i][:, :]
            return ap if a is None else ap.rearrange("p (a b) -> p a b", a=a)

        with stage(["loaded", "filled"]) as (block, (loaded, filled)):
            @block.sync
            def _(sp):
                sp.dma_start(CF[:, :], A['cf']).then_inc(loaded, 16)
                sp.dma_start(CB[:, :], A['cb']).then_inc(loaded, 16)
                sp.dma_start(X[:, 0:4, :], A['x_prompt'][0].rearrange("(t p) d -> p t d", p=P)).then_inc(loaded, 16)
                sp.dma_start(X[0:64, 4, :], A['x_sample'].rearrange("b t d -> (b t) d")).then_inc(loaded, 16)
                sp.wait_ge(loaded, 64)

            @block.vector
            def _(dve):
                nc.vector.memset(ones[:, :], 1.0).then_inc(filled, 1)
                nc.vector.memset(eps[:, :], EPS).then_inc(filled, 1)
                dve.wait_ge(filled, 2)

        REGS = [[e.alloc_register(f"page{k}") for k in range(24)] for e in (nc.sync, nc.gpsimd)]
        with nc.Fori(0, DEPTH) as l:
            v = dict(X=X, MIX=MIX, US=US, QRS=QRS, ones=ones, eps=eps, cf=cf, cb=cb, ident=ident, bk=bk, nc=nc, W1=W1, W2=W2, B1=B1,
                     early_columns=en, REGS=REGS)
            layer(nc, A, O, l, sb, stage, v)

        with stage(["written"]) as (block, (written,)):
            @block.sync
            def _(sp):
                sp.dma_start(O['y_prompt'][0].rearrange("(t p) d -> p t d", p=P), X[:, 0:4, :]).then_inc(written, 16)
                sp.dma_start(O['y_sample'].rearrange("b t d -> (b t) d"), X[0:64, 4, :]).then_inc(written, 16)
                sp.wait_ge(written, 32)


def layer(nc, A, O, l, sb, stage, v):
    with ExitStack() as scope:
        UP = sb(scope, "UP", [P, 4, PROJ])
        v['CE'] = sb(scope, "CE", [P, v['early_columns']])
        U = [UP[:, t, :] for t in range(4)] + [v['US'][0:64, :]]
        project(nc, A, l, sb, stage, v, U)
        with ExitStack() as s2:
            Y = [u[:, GQKV:GQKV + CW] for u in U]
            g_log = sb(s2, "g_log", [P, NTILE, H4])
            with ExitStack() as s3:
                pointwise(nc, A, O, l, s3, sb, stage, v, U, Y, g_log)
            with ExitStack() as s3:
                retention(nc, A, O, l, s3, sb, stage, v, U)
            with ExitStack() as s3:
                delta(nc, A, O, l, s3, sb, stage, v, U, Y, g_log)
        with ExitStack() as s2:
            prompt_attention(nc, A, O, l, s2, sb, stage, v, U)
    with ExitStack() as scope:
        sample_attention(nc, A, O, l, scope, sb, stage, v)
    with ExitStack() as scope:
        out_project(nc, A, l, scope, sb, stage, v)


def project(nc, A, l, sb, stage, v, U):
    X, ident = v['X'], v['ident']
    chunks = [(c, min(c + 512, PROJ)) for c in range(0, PROJ, 512)]
    NC = len(chunks)
    with ExitStack() as scope:
        hT = sb(scope, "hT", [P, KD, 4 * P + 64])
        W = sb(scope, "W", [P, 2, KD, 512])
        ss = sb(scope, "ss", [P, NTILE])
        xn = sb(scope, "xn", [P, D])
        gpre = sb(scope, "gpre", [P, KD])
        with stage(["w0", "w1", "gain", "act_s", "dve_s", "pe_s", "e_act", "e_dve", "chunk_done", "proj_done"]) as \
                (block, (w0, w1, gain, act_s, dve_s, pe_s, e_act, e_dve, chunk_done, proj_done)):
            wsem = [w0, w1]
            act = Steps(act_s, [f"{n}{t}" for t in range(NTILE) for n in ("sq", "rt")])
            dve = Steps(dve_s, [f"{n}{t}" for t in range(NTILE) for n in ("rs", "xn", "h0", "h1")])
            pe = Steps(pe_s, [f"T{t}" for t in range(NTILE)])
            wv = A['w_in'][l].rearrange("(k p) c -> p k c", p=P)

            @block.sync
            def _(e):
                e.dma_start(v['CE'][:, :], A['ce']).then_inc(gain, 16)
                e.dma_start(gpre[:, :], A['norm_pre'][l].rearrange("(k p) -> p k", p=P),
                            allow_slow_non_contiguous=True).then_inc(gain, 16)
                for c, (a, b) in enumerate(chunks):
                    if c >= 2:
                        e.wait_ge(chunk_done, c - 1)
                    e.dma_start(W[:, c % 2, :, 0:b - a], wv[:, :, a:b]).then_inc(wsem[c % 2], 16)

            def evacuate(e, u):
                c, t = divmod(u, NTILE)
                a, b = chunks[c]
                e.wait_ge(proj_done, u + 1)
                return U[t][:, a:b], v['bk'](4 + u % 4)[0:ROWS[t], 0:b - a]

            @block.scalar
            def _(e):
                for t in range(NTILE):
                    n = ROWS[t]
                    if t:
                        dve.wait(e, f"xn{t-1}")
                        pe.wait(e, f"T{t-1}")
                    act.link(e, f"sq{t}", nc.scalar.activation(xn[0:n, :], X[0:n, t, :], ACT.Square, accum_out=ss[0:n, t:t + 1]))
                    act.link(e, f"rt{t}", nc.scalar.activation(ss[0:n, t:t + 1], ss[0:n, t:t + 1], ACT.Sqrt,
                                                               scale=1.0 / D, bias=v['eps'][0:n, :]))
                for u in range(0, NC * NTILE, 2):
                    o, i = evacuate(e, u)
                    nc.scalar.activation(o, i, ACT.Copy).then_inc(e_act, 1)

            @block.vector
            def _(e):
                e.wait_ge(gain, 32)
                for t in range(NTILE):
                    n = ROWS[t]
                    act.wait(e, f"rt{t}")
                    dve.link(e, f"rs{t}", nc.vector.reciprocal(ss[0:n, t:t + 1], ss[0:n, t:t + 1]))
                    dve.link(e, f"xn{t}", nc.vector.tensor_scalar(xn[0:n, :], X[0:n, t, :], ss[0:n, t:t + 1], None, ALU.mult))
                    pe.wait(e, f"T{t}")
                    for h in range(2):
                        dve.done(e, f"h{h}{t}", nc.vector.tensor_tensor(
                            hT[:, 4 * h:4 * h + 4, t * P:t * P + n], v['bk'](2 * (t % 2) + h, 4)[:, :, 0:n],
                            b_(gpre[:, 4 * h:4 * h + 4], 2, [P, 4, n]), ALU.mult))
                for u in range(1, NC * NTILE, 2):
                    o, i = evacuate(e, u)
                    nc.vector.tensor_copy(o, i).then_inc(e_dve, 1)

            @block.tensor
            def _(e):
                for t in range(NTILE):
                    n = ROWS[t]
                    dve.wait(e, f"xn{t}")
                    if t >= 2:
                        dve.wait(e, f"h1{t-2}")
                    for k in range(KD):
                        mm = nc.tensor.transpose(v['bk'](2 * (t % 2) + k // 4, 4)[:, k % 4, 0:n],
                                                 xn[0:n, k * P:(k + 1) * P], ident[0:n, 0:n])
                    pe.done(e, f"T{t}", mm)
                dve.wait(e, f"h1{NTILE-1}")
                u = 0
                for c, (a, b) in enumerate(chunks):
                    e.wait_ge(wsem[c % 2], 16 * (c // 2 + 1))
                    for t in range(NTILE):
                        if u >= 4:
                            e.wait_ge(e_dve if (u - 4) % 2 else e_act, (u - 4) // 2 + 1)
                        for k in range(KD):
                            mm = nc.tensor.matmul(v['bk'](4 + u % 4)[0:ROWS[t], 0:b - a], hT[:, k, t * P:t * P + ROWS[t]],
                                                  W[:, c % 2, k, 0:b - a], start=(k == 0), stop=(k == KD - 1))
                        mm.then_inc(proj_done, 1)
                        u += 1
                    nc.tensor.matmul(v['bk'](0)[0:1, 0:1], ident[:, 0:1], ident[:, 0:1], start=True, stop=True).then_inc(chunk_done, 1)


def pointwise(nc, A, O, l, scope, sb, stage, v, U, Y, g_log):
    cw = sb(scope, "cw", [P, CONV, CW])
    XS = sb(scope, "XS", [P, CONV - 1, CW])
    QR = sb(scope, "QR", [P, 2, 512])
    ta = sb(scope, "ta", [P, CW])
    tb = sb(scope, "tb", [P, CW])
    alog = sb(scope, "alog", [P, H4])
    dtb = sb(scope, "dtb", [P, H4])
    sp_ = sb(scope, "sp_", [P, 3, H4])
    nrm = sb(scope, "nrm", [P, 8])
    zero = sb(scope, "zero", [CONV - 1, CW])
    cos, sin = v['cf']('cos', 32), v['cf']('sin', 32)
    names = []
    for t in range(NTILE):
        for r in ("rq", "nq", "kv"):
            names += [f"{r}{x}{t}" for x in ("ab12" if r != "nq" else "ab12c")]
        names += [f"{x}{t}" for x in ("a1", "mx", "sg", "gl", "c0", "c1", "c1a", "c2", "c2a", "c3", "c3a", "s2", "ss",
                                      "rc", "q8", "nm")]
    with stage(["dve_s", "act_s", "par", "raw", "shift", "rot", "outs"]) as (block, (dve_s, act_s, par, raw, shift, rot, outs)):
        dve = Steps(dve_s, ["zero", "al"] + names)
        act = Steps(act_s, ["al"] + [f"{x}{t}" for t in range(NTILE) for x in ("rg", "ng", "gg", "gt", "bt", "ab", "ex", "ln", "ys", "sq")])
        XP, XC = A['conv_p'], A['conv_s']

        @block.sync
        def _(e):
            e.dma_start(cw[:, :, :].rearrange("p a b -> p (a b)"),
                        A['gdn_conv'][l].rearrange("a b -> (a b)").partition_broadcast(P)).then_inc(par, 16)
            e.dma_start(alog[:, :], A['gdn_a_log'][l].partition_broadcast(P)).then_inc(par, 16)
            e.dma_start(dtb[:, :], A['gdn_dt_bias'][l].partition_broadcast(P)).then_inc(par, 16)
            dve.wait(e, "zero")
            e.dma_start(XP[0:3, :], zero[:, :]).then_inc(raw, 16)
            for t in range(4):
                e.dma_start(XP[3 + t * P:3 + (t + 1) * P, :], U[t][:, GQKV:GQKV + CW]).then_inc(raw, 16)
            e.dma_start(XC[:, 0:3, :], A['state_gdn_conv'][l]).then_inc(raw, 16)
            e.dma_start(XC[:, 3:3 + NT, :], U[4][:, GQKV:GQKV + CW]).then_inc(raw, 16)
            e.wait_ge(raw, 7 * 16)
            e.dma_start(O['conv_prompt'][l, 0], XP[SEQ:SEQ + 3, :]).then_inc(outs, 16)
            e.dma_start(O['conv_sample'][l], XC[:, NT:NT + 3, :]).then_inc(outs, 16)
            nout = 2
            for t in range(NTILE):
                if t:
                    dve.wait(e, f"c3a{t-1}")
                for k in range(1, 4):
                    src = XP[3 - k + t * P:3 - k + (t + 1) * P, :] if t < 4 else XC[:, 3 - k:3 - k + NT, :]
                    e.dma_start(XS[0:ROWS[t], k - 1, :], src).then_inc(shift, 16)
                dve.wait(e, f"kv2{t}")
                n = ROWS[t]
                if t < 4:
                    kvo = O['kv_prompt'][l, 0].rearrange("s a g d -> s (a g d)")[t * P:(t + 1) * P]
                    wno = O['win_prompt'][l, 0].rearrange("s a g d -> s (a g d)")[t * P:(t + 1) * P]
                    e.dma_start(A['q_rot'][t * P:(t + 1) * P, :], QR[:, :, :].rearrange("p i c -> p (i c)")).then_inc(rot, 16)
                else:
                    kvo = O['kv_sample'][l].rearrange("b s a g d -> (b s) (a g d)")
                    wno = O['win_sample'][l].rearrange("b s a g d -> b s (a g d)")[:, WIN - NT:WIN, :]
                e.dma_start(kvo, U[t][:, NKV:NKV + 512]).then_inc(outs, 16)
                e.dma_start(wno, U[t][:, NKV + 512:NKV + 768]).then_inc(outs, 16)
                nout += 2
            e.dma_start(O['win_sample'][l].rearrange("b s a g d -> b s (a g d)")[:, 0:WIN - NT, :],
                        A['state_nsa_win'][l].rearrange("b s a g d -> b s (a g d)")[:, NT:WIN, :]).then_inc(outs, 16)
            e.wait_ge(outs, 16 * (nout + 1))
            e.wait_ge(rot, 64)

        @block.scalar
        def _(e):
            e.wait_ge(par, 48)
            act.link(e, "al", nc.scalar.activation(alog[:, :], alog[:, :], ACT.Exp))
            for t in range(NTILE):
                u, n = U[t], ROWS[t]
                for nm, a, w, f in (("rg", RG, 256, ACT.Silu), ("ng", NG, 512, ACT.Silu), ("gg", GG, 256, ACT.Silu),
                                    ("gt", NGATE, 24, ACT.Sigmoid), ("bt", GB, H4, ACT.Sigmoid)):
                    act.done(e, f"{nm}{t}", nc.scalar.activation(u[:, a:a + w], u[:, a:a + w], f))
                dve.wait(e, f"a1{t}")
                act.link(e, f"ab{t}", nc.scalar.activation(sp_[0:n, 1, :], sp_[0:n, 0, :], ACT.Abs))
                act.link(e, f"ex{t}", nc.scalar.activation(sp_[0:n, 1, :], sp_[0:n, 1, :], ACT.Exp, scale=-1.0))
                act.link(e, f"ln{t}", nc.scalar.activation(sp_[0:n, 1, :], sp_[0:n, 1, :], ACT.Ln, bias=1.0))
                dve.wait(e, f"c3a{t}")
                act.link(e, f"ys{t}", nc.scalar.activation(Y[t], Y[t], ACT.Silu))
                dve.wait(e, f"ss{t}")
                act.link(e, f"sq{t}", nc.scalar.activation(nrm[0:n, :], nrm[0:n, :], ACT.Sqrt, bias=v['eps'][0:n, :]))

        @block.vector
        def _(e):
            dve.link(e, "zero", nc.vector.memset(zero[:, :], 0.0))
            act.wait(e, "al")
            dve.link(e, "al", nc.vector.tensor_scalar(alog[:, :], alog[:, :], -1.0, None, ALU.mult))
            for t in range(NTILE):
                u, n = U[t], ROWS[t]
                co, si = cos[0:n, t, :], sin[0:n, t, :]

                def rope(nm, src, dst, s, w):
                    m = w // 32
                    A1 = ta[0:n, 0:s * w].rearrange("p (s m c) -> p s m c", s=s, m=m)
                    B1 = tb[0:n, 0:s * w].rearrange("p (s m c) -> p s m c", s=s, m=m)
                    sv = src.rearrange("p s (m c) -> p s m c", c=32)
                    bc = [n, s, m, 32]
                    dve.link(e, f"{nm}a{t}", nc.vector.tensor_tensor(A1, sv, co.unsqueeze(1).unsqueeze(1).broadcast_to(bc), ALU.mult))
                    dve.link(e, f"{nm}b{t}", nc.vector.tensor_tensor(B1, sv, si.unsqueeze(1).unsqueeze(1).broadcast_to(bc), ALU.mult))
                    dve.link(e, f"{nm}1{t}", nc.vector.tensor_tensor(dst[:, :, :, 0:32], A1[:, :, 0::2, :], B1[:, :, 1::2, :], ALU.subtract))
                    dve.link(e, f"{nm}2{t}", nc.vector.tensor_tensor(dst[:, :, :, 32:64], A1[:, :, 1::2, :], B1[:, :, 0::2, :], ALU.add))

                rqv = u[:, RQ:RQ + 512].unsqueeze(1)
                rope("rq", rqv, rqv.rearrange("p s (h c) -> p s h c", c=HD), 1, 512)
                if 0 < t < 4:
                    e.wait_ge(rot, 16 * t)
                q_to = (QR if t < 4 else v['QRS'])[0:n, :, :].rearrange("p i (r g c) -> p i g r c", r=R, g=G)
                qv = u[:, NQ:NQ + 512].rearrange("p (g w) -> p g w", g=G)
                rope("nq", qv, q_to[:, 1], 2, 256)
                dve.link(e, f"nqc{t}", nc.vector.tensor_copy(q_to[:, 0], qv.rearrange("p g (r c) -> p g r c", r=R)))
                kv = u[:, NKV + 256:NKV + 768].rearrange("p (s w) -> p s w", s=2)[:, :, 0:128]
                rope("kv", kv, kv.rearrange("p s (h c) -> p s h c", c=HD), 2, 128)
                dve.link(e, f"a1{t}", nc.vector.tensor_tensor(sp_[0:n, 0, :], u[:, GA:GA + H4], dtb[0:n, :], ALU.add))
                dve.link(e, f"mx{t}", nc.vector.tensor_scalar(sp_[0:n, 2, :], sp_[0:n, 0, :], 0.0, None, ALU.max))
                act.wait(e, f"ln{t}")
                dve.link(e, f"sg{t}", nc.vector.tensor_tensor(sp_[0:n, 2, :], sp_[0:n, 2, :], sp_[0:n, 1, :], ALU.add))
                dve.link(e, f"gl{t}", nc.vector.tensor_tensor(g_log[0:n, t, :], sp_[0:n, 2, :], alog[0:n, :], ALU.mult))
                y = Y[t]
                e.wait_ge(shift, 48 * (t + 1))
                dve.link(e, f"c0{t}", nc.vector.tensor_tensor(y, y, cw[0:n, 3, :], ALU.mult))
                for k in range(1, 4):
                    dve.link(e, f"c{k}{t}", nc.vector.tensor_tensor(ta[0:n, :], XS[0:n, k - 1, :], cw[0:n, 3 - k, :], ALU.mult))
                    dve.link(e, f"c{k}a{t}", nc.vector.tensor_tensor(y, y, ta[0:n, :], ALU.add))
                act.wait(e, f"ys{t}")
                qk = Y[t][:, 0:512].rearrange("p (h c) -> p h c", c=HD)
                tq = ta[0:n, 0:512].rearrange("p (h c) -> p h c", c=HD)
                dve.link(e, f"s2{t}", nc.vector.tensor_tensor(tq, qk, qk, ALU.mult))
                dve.link(e, f"ss{t}", nc.vector.tensor_reduce(nrm[0:n, :], tq, AX.X, ALU.add))
                act.wait(e, f"sq{t}")
                dve.link(e, f"rc{t}", nc.vector.reciprocal(nrm[0:n, :], nrm[0:n, :]))
                dve.link(e, f"q8{t}", nc.vector.tensor_scalar(nrm[0:n, 0:4], nrm[0:n, 0:4], SCALE, None, ALU.mult))
                dve.link(e, f"nm{t}", nc.vector.tensor_tensor(qk, qk, b_(nrm[0:n, :], 2, [n, 8, HD]), ALU.mult))


def load_states(e, S, src, loaded, l):
    for h in range(H4):
        hp, o = h // 2, (h % 2) * HD
        e.dma_start(S[o:o + HD, :, hp, o:o + HD], src[l].rearrange("b h d e -> h d b e")[h]).then_inc(loaded, 16)


def retention(nc, A, O, l, scope, sb, stage, v, U):
    QK = sb(scope, "QK", [P, 4, P])
    ATT = sb(scope, "ATT", [P, H4, P])
    KDc = sb(scope, "KDc", [P, 256])
    S = sb(scope, "S", [P, 2, P])
    SS = sb(scope, "SS", [P, NB, 2, P])
    QM = sb(scope, "QM", [P, 2, NB, 64])
    VM = sb(scope, "VM", [P, NB, 256])
    T1 = sb(scope, "T1", [P, 512])
    Ot = sb(scope, "Ot", [P, 256])
    st = sb(scope, "st", [P, 4, H4])
    gn = sb(scope, "gn", [P, 256])
    bk, cf, ident, MIX = v['bk'], v['cf'], v['ident'], v['MIX']
    dn = ["z1", "z2"]
    for t in range(NTILE):
        dn += [f"{x}{t}" for x in ("qk", "att0", "att1", "kd")]
        dn += [f"qm{hp}" for hp in range(2)] + ["vm"] if t == 4 else []
        dn += [f"{x}{t}" for x in ("qs", "o")]
        dn += [f"{x}{t}" for x in ("m", "m2", "ce", "sq", "va", "rc", "n1", "n2", "n3")]
        dn += [f"{x}{t}" for x in ("sm", "s0", "s1")] if t < 4 else [f"ss{i}{j}" for i in range(4) for j in "ms"]
    pn = [f"{x}{t}" for t in range(NTILE) for x in ("T", "a", "qs", "av", "su")]
    with stage(["dve_s", "act_s", "pe_s", "loaded", "gl", "outs"]) as (block, (dve_s, act_s, pe_s, loaded, gl, outs)):
        dve = Steps(dve_s, dn)
        act = Steps(act_s, [f"sq{t}" for t in range(NTILE)])
        pe = Steps(pe_s, pn)

        @block.sync
        def _(e):
            e.dma_start(gn[:, :], A['ret_gn'][l].partition_broadcast(P)).then_inc(gl, 16)
            dve.wait(e, "z2")
            load_states(e, SS, A['state_ret'], loaded, l)
            dve.wait(e, "s13")
            for h in range(H4):
                hp, o = h // 2, (h % 2) * HD
                e.dma_start(O['ret_prompt'][l, 0, h], S[o:o + HD, hp, o:o + HD]).then_inc(outs, 16)
            dve.wait(e, "ss3s")
            for h in range(H4):
                hp, o = h // 2, (h % 2) * HD
                e.dma_start(O['ret_sample'][l].rearrange("b h d e -> h d b e")[h], SS[o:o + HD, :, hp, o:o + HD]).then_inc(outs, 16)
            e.wait_ge(outs, 2 * H4 * 16)

        @block.scalar
        def _(e):
            for t in range(NTILE):
                dve.wait(e, f"va{t}")
                act.done(e, f"sq{t}", nc.scalar.activation(st[0:ROWS[t], 2, :], st[0:ROWS[t], 2, :], ACT.Sqrt,
                                                           scale=1.0 / HD, bias=v['eps'][0:ROWS[t], :]))

        @block.tensor
        def _(e):
            for t in range(NTILE):
                u, n, k = U[t], ROWS[t], int(t == 4)
                if t:
                    dve.wait(e, f"qk{t-1}")
                for i in range(4):
                    mm = nc.tensor.transpose(bk(0, 4)[:, i, 0:n], u[:, i * P:(i + 1) * P], ident[0:n, 0:n])
                pe.done(e, f"T{t}", mm)
                dve.wait(e, f"qk{t}")
                for h in range(H4):
                    o = (h % 2) * HD
                    mm = nc.tensor.matmul(bk(1 + 4 * (h % 2), 4)[0:n, h // 2, 0:n], QK[o:o + HD, 2 + h // 2, 0:n], QK[o:o + HD, h // 2, 0:n],
                                          start=True, stop=True)
                pe.done(e, f"a{t}", mm)
                if t < 4:
                    if t:
                        dve.wait(e, f"s1{t-1}")
                    else:
                        dve.wait(e, "z1")
                    for hp in range(2):
                        mm = nc.tensor.matmul(bk(2, 4)[0:n, hp, :], QK[:, hp, 0:n], S[:, hp, :], start=True, stop=True)
                else:
                    dve.wait(e, "qm1")
                    e.wait_ge(loaded, H4 * 16)
                    for hp in range(2):
                        for b in range(NB):
                            mm = nc.tensor.matmul(bk(2, 4)[0:n, hp, :], QM[:, hp, b, :], SS[:, b, hp, :],
                                                  start=(b == 0), stop=(b == NB - 1))
                pe.done(e, f"qs{t}", mm)
                dve.wait(e, f"att1{t}")
                for h in range(H4):
                    mm = nc.tensor.matmul(bk(3)[0:n, h * HD:(h + 1) * HD], ATT[0:n, h, 0:n], u[:, RV + h * HD:RV + (h + 1) * HD],
                                          start=True, stop=True)
                pe.done(e, f"av{t}", mm)
                dve.wait(e, f"kd{t}" if t < 4 else "vm")
                if t < 4:
                    for hp in range(2):
                        mm = nc.tensor.matmul(bk(4, 4)[:, hp, :], KDc[0:n, hp * P:(hp + 1) * P], u[:, RV + hp * P:RV + (hp + 1) * P],
                                              start=True, stop=True)
                else:
                    for i in range(4):
                        hp, q = divmod(i, 2)
                        mm = nc.tensor.matmul(bk(4 + i), KDc[0:n, hp * P:(hp + 1) * P], VM[0:n, 4 * q:4 * q + 4, hp * P:(hp + 1) * P],
                                              start=True, stop=True)
                pe.done(e, f"su{t}", mm)

        @block.vector
        def _(e):
            dve.link(e, "z1", nc.vector.memset(S[:, :, :], 0.0))
            dve.link(e, "z2", nc.vector.memset(SS[:, :, :, :], 0.0))
            e.wait_ge(gl, 16)
            pair = cf('pair')
            for t in range(NTILE):
                u, n, k = U[t], ROWS[t], int(t == 4)
                pe.wait(e, f"T{t}")
                dve.link(e, f"qk{t}", nc.vector.tensor_copy(QK[:, :, 0:n], bk(0, 4)[:, :, 0:n]))
                pe.wait(e, f"a{t}")
                for o in range(2):
                    dve.link(e, f"att{o}{t}", nc.vector.tensor_tensor(ATT[0:n, o::2, 0:n], bk(1 + 4 * o, 4)[0:n, 0:2, 0:n],
                                                                       cf(f'dm{k}', P)[0:n, o::2, 0:n], ALU.mult))
                h3 = lambda ap: ap.rearrange("p (h c) -> p h c", c=HD)
                dve.link(e, f"kd{t}", nc.vector.tensor_tensor(h3(KDc[0:n, :]), h3(u[:, RK:RK + 256]),
                                                               b_(cf('kdec', 4)[0:n, k, :], 2, [n, H4, HD]), ALU.mult))
                if t == 4:
                    for hp in range(2):
                        dve.link(e, f"qm{hp}", nc.vector.tensor_tensor(QM[:, hp, :, :], b_(QK[:, hp, 0:64], 1, [P, NB, 64]), cf('own', 64), ALU.mult))
                    dve.link(e, "vm", nc.vector.tensor_tensor(VM[0:n, :, :], b_(u[:, RV:RV + 256], 1, [n, NB, 256]),
                                                               b_(cf('ownrow')[0:n, :], 2, [n, NB, 256]), ALU.mult))
                pe.wait(e, f"qs{t}")
                dve.link(e, f"qs{t}", nc.vector.tensor_tensor(h3(T1[0:n, 0:256]), h3(bk(2)[0:n, 0:256]),
                                                               b_(cf('qdec', 4)[0:n, k, :], 2, [n, H4, HD]), ALU.mult))
                pe.wait(e, f"av{t}")
                dve.link(e, f"o{t}", nc.vector.tensor_tensor(Ot[0:n, :], bk(3)[0:n, 0:256], T1[0:n, 0:256], ALU.add))
                o3 = h3(Ot[0:n, :])
                dve.link(e, f"m{t}", nc.vector.tensor_reduce(st[0:n, 0, :], o3, AX.X, ALU.add))
                dve.link(e, f"m2{t}", nc.vector.tensor_scalar(st[0:n, 1, :], st[0:n, 0, :], 1.0 / HD, None, ALU.mult))
                dve.link(e, f"ce{t}", nc.vector.tensor_tensor(o3, o3, b_(st[0:n, 1, :], 2, [n, H4, HD]), ALU.subtract))
                dve.link(e, f"sq{t}", nc.vector.tensor_tensor(T1[0:n, 0:256], Ot[0:n, :], Ot[0:n, :], ALU.mult))
                dve.link(e, f"va{t}", nc.vector.tensor_reduce(st[0:n, 2, :], h3(T1[0:n, 0:256]), AX.X, ALU.add))
                act.wait(e, f"sq{t}")
                dve.link(e, f"rc{t}", nc.vector.reciprocal(st[0:n, 3, :], st[0:n, 2, :]))
                dve.link(e, f"n1{t}", nc.vector.tensor_tensor(o3, o3, b_(st[0:n, 3, :], 2, [n, H4, HD]), ALU.mult))
                dve.link(e, f"n2{t}", nc.vector.tensor_tensor(Ot[0:n, :], Ot[0:n, :], gn[0:n, :], ALU.mult))
                dve.link(e, f"n3{t}", nc.vector.tensor_tensor(MIX[0:n, t, 0:256], Ot[0:n, :], u[:, RG:RG + 256], ALU.mult))
                pe.wait(e, f"su{t}")
                if t < 4:
                    dve.link(e, f"sm{t}", nc.vector.tensor_tensor(T1[:, 0:256].rearrange("p (a b) -> p a b", a=2), bk(4, 4)[:, 0:2, :],
                                                                   b_(pair, 1, [P, 2, P]), ALU.mult))
                    for hp in range(2):
                        dve.link(e, f"s{hp}{t}", nc.vector.scalar_tensor_tensor(
                            S[:, hp, :], S[:, hp, :], cf('sdec', 2)[:, 0, hp:hp + 1], T1[:, hp * P:(hp + 1) * P], ALU.mult, ALU.add))
                else:
                    for i in range(4):
                        hp, q = divmod(i, 2)
                        t3 = T1[:, :].rearrange("p (a b) -> p a b", a=4)
                        dve.link(e, f"ss{i}m", nc.vector.tensor_tensor(t3, bk(4 + i, 4), b_(pair, 1, [P, 4, P]), ALU.mult))
                        sv = SS[:, 4 * q:4 * q + 4, hp, :]
                        dve.link(e, f"ss{i}s", nc.vector.scalar_tensor_tensor(sv, sv, cf('sdec', 2)[:, 1, hp:hp + 1], t3, ALU.mult, ALU.add))


def delta(nc, A, O, l, scope, sb, stage, v, U, Y, g_log):
    PAIR = [(0, 1), (2, 3), (4,)]
    LEVELS = [7, 7, 3]
    ready = lambda t: [("ready0", t), ("ready1", t)]
    state = lambda t: [("state0", t), ("state1", t), ("state2", t), ("state3", t)]
    beside = [ready(2) + ready(3), state(0) + state(1) + ready(4), state(2) + state(3)]
    ORDER = ready(0) + ready(1)
    for tiles, levels, small in zip(PAIR, LEVELS, beside):
        per = -(-len(small) // levels)
        for s in range(levels):
            ORDER += [("level", (tiles, s, levels))] + small[s * per:(s + 1) * per]
    ORDER += state(4)

    SETS = 4
    QKT_ = sb(scope, "QKT", [P, SETS, 6, P])
    kb = sb(scope, "kb", [P, 256])
    vb_ = sb(scope, "vb", [P, SETS, 256])
    kd_ = sb(scope, "kd", [P, SETS, 256])
    work = sb(scope, "work", [P, 8, H4, P])
    NTs_, M1_, T_ = ([work[:, i + lane, :, :] for lane in range(2)] for i in (0, 2, 4))
    gb, LT = work[:, 6, :, :], work[:, 7, :, :]
    flat = work[:, :, :, :].rearrange("p a h c -> p (a h c)")
    QM = flat[:, 0:2048].rearrange("p (i b c) -> p i b c", i=4, b=NB)
    VM = flat[:, 2048:4096].rearrange("p (b c) -> p b c", b=NB)
    gs_ = sb(scope, "gs", [P, NTILE, 7, H4])
    SL_ = sb(scope, "SL", [P, NTILE, H4, NB])
    SLp = sb(scope, "SLp", [P, 2, NB])
    S = sb(scope, "S", [P, 2, P])
    SS = sb(scope, "SS", [P, NB, 2, P])
    VN = sb(scope, "VN", [P, 256])
    T1 = sb(scope, "T1", [P, 512])
    Ot = sb(scope, "Ot", [P, 256])
    st = sb(scope, "st", [P, 4, H4])
    gn = sb(scope, "gn", [P, HD])
    bk, cf, ident, MIX = v['bk'], v['cf'], v['ident'], v['MIX']
    heads = lambda t, i: U[t][:, i * 512:(i + 1) * 512].rearrange("p (h c) -> p h c", c=P)
    TT_, ATT_, NTt_ = ([heads(t, i) for t in range(NTILE)] for i in range(3))

    dn, pn, an = ["z1", "z2"], [], []
    ends = {}
    for what, x in ORDER:
        if what == "level":
            tiles, s, levels = x
            if s == 0:
                dn += [f"ns{t}.0" for t in tiles]
                pn += [f"a{t}.0" for t in tiles]
                dn += [f"{n}{t}.0" for t in tiles for n in ("t", "tt", "nn")]
            else:
                pn += [f"a{t}.{s}" for t in tiles] + [f"{n}{t}.{s}" for t in tiles for n in (("b",) if s < levels - 1 else ()) + ("c",)]
                an += [f"m{t}.{s}" for t in tiles]
                dn += [f"nn{t}.{s}" for t in tiles if s < levels - 1]
                dn += [f"{n}{t}.{s}" for t in tiles for n in (("t",) if s < levels - 1 else ()) + ("tt",)]
            continue
        t = x
        if what == "ready0":
            dn += [f"{n}{t}" for n in ("kb", "vb", "gb", "g0", "g1", "g3", "gd", "lt", "tr", "tr2")]
            pn += [f"{n}{t}" for n in ("g", "gr", "T")]
            an += [f"{n}{t}" for n in ("eg", "el", "sl", "L0", "L1", "L2", "L3")]
        if what == "ready1":
            dn += [f"{n}{t}" for n in ("nt0", "nt1", "att0", "att1", "be", "kd")]
            pn += [f"{n}{t}" for n in ("kk", "qk")]
        if what == "state0":
            dn += ([f"qm{i}" for i in range(4)] if t == 4 else []) + [f"{n}{t}" for n in ("ks", "r")]
            pn += [f"ks{t}"]
        if what == "state1":
            dn += [f"vn{t}"]
            pn += [f"vn{t}", f"qs{t}"]
        if what == "state2":
            dn += [f"{n}{t}" for n in ("sp0", "sp1")] + ([f"{n}{t}" for n in ("sm", "s0", "s1")] if t < 4 else ["vm"])
            dn += [f"qs{t}", f"o{t}"]
            pn += [f"av{t}", f"su{t}"] if t < 4 else [f"av{t}"]
        if what == "state3":
            dn += [f"{n}{t}" for n in ("sq", "va", "rc", "n1", "n2", "n3")]
            if t == 4:
                pn += [f"su{t}"]
                dn += [f"ss{i}{j}" for i in range(4) for j in "nms"]
            an += [f"rt{t}"]
        ends[what, t] = dn[-1]

    with stage(["dve_s", "act_s", "pe_s", "loaded", "gl", "outs"]) as (block, (dve_s, act_s, pe_s, loaded, gl, outs)):
        dve, act, pe = Steps(dve_s, dn), Steps(act_s, an), Steps(pe_s, pn)

        @block.sync
        def _(e):
            e.dma_start(gn[:, :], A['gdn_norm'][l].partition_broadcast(P)).then_inc(gl, 16)
            dve.wait(e, "z2")
            load_states(e, SS, A['state_gdn'], loaded, l)
            dve.wait(e, "s13")
            for h in range(H4):
                hp, o = h // 2, (h % 2) * HD
                e.dma_start(O['gdn_prompt'][l, 0, h], S[o:o + HD, hp, o:o + HD]).then_inc(outs, 16)
            dve.wait(e, "ss3s")
            for h in range(H4):
                hp, o = h // 2, (h % 2) * HD
                e.dma_start(O['gdn_sample'][l].rearrange("b h d e -> h d b e")[h], SS[o:o + HD, :, hp, o:o + HD]).then_inc(outs, 16)
            e.wait_ge(outs, 2 * H4 * 16)

        @block.scalar
        def _(e):
            for what, x in ORDER:
                if what == "level":
                    tiles, s, levels = x
                    for t in tiles if s else ():
                        n = ROWS[t]
                        pe.wait(e, f"a{t}.{s}")
                        act.done(e, f"m{t}.{s}", nc.scalar.activation(M1_[t % 2][0:n, :, 0:n], bk(4 + 2 * (t % 2), 4)[0:n, :, 0:n], ACT.Copy))
                    continue
                t = x
                n, gs = ROWS[t], gs_[:, t]
                if what == "ready0":
                    dve.wait(e, f"gd{t}")
                    act.done(e, f"eg{t}", nc.scalar.activation(gs[0:n, 2, :], gs[0:n, 0, :], ACT.Exp))
                    act.done(e, f"el{t}", nc.scalar.activation(gs[0:n, 4, :], gs[0:n, 5, :], ACT.Exp))
                    pe.wait(e, f"gr{t}")
                    src = bk(1, 4)[:, :, P - 1:P] if t < 4 else bk(1, 4)[:, :, NT - 1:64:NT]
                    act.done(e, f"sl{t}", nc.scalar.activation(SL_[:, t, :, 0:1] if t < 4 else SL_[:, t, :, :], src, ACT.Exp))
                    dve.wait(e, f"lt{t}")
                    for h in range(H4):
                        act.done(e, f"L{h}{t}", nc.scalar.activation(LT[0:n, h, 0:n], LT[0:n, h, 0:n], ACT.Exp, bias=gs[0:n, 1, h:h + 1]))
                if what == "state3":
                    dve.wait(e, f"va{t}")
                    act.done(e, f"rt{t}", nc.scalar.activation(st[0:n, 2, :], st[0:n, 2, :], ACT.Sqrt, scale=1.0 / HD, bias=v['eps'][0:n, :]))

        @block.tensor
        def _(e):
            before = "z2"
            for what, x in ORDER:
                if what == "level":
                    tiles, s, levels = x
                    for t in tiles:
                        n, lane = ROWS[t], t % 2
                        dve.wait(e, f"ns{t}.0" if s == 0 else f"tt{t}.{s-1}" if s > 1 else f"nn{t}.0")
                        for h in range(H4):
                            mm = nc.tensor.matmul(bk(4 + 2 * lane, 4)[0:n, h, 0:n], NTs_[lane][0:n, h, 0:n],
                                                  T_[lane][0:n, h, 0:n] if s else ident[0:n, 0:n], start=True, stop=True)
                        pe.done(e, f"a{t}.{s}", mm)
                    for t in tiles if s else ():
                        n, lane = ROWS[t], t % 2
                        T, TT, M1 = T_[lane], TT_[t], M1_[lane]
                        act.wait(e, f"m{t}.{s}")
                        if s < levels - 1:
                            for h in range(H4):
                                mm = nc.tensor.matmul(bk(5 + 2 * lane, 4)[0:n, h, 0:n], TT[0:n, h, 0:n], M1[0:n, h, 0:n], start=True, stop=True)
                            pe.done(e, f"b{t}.{s}", mm)
                        for h in range(H4):
                            mm = nc.tensor.matmul(bk(4 + 2 * lane, 4)[0:n, h, 0:n], M1[0:n, h, 0:n], TT[0:n, h, 0:n], start=True, stop=True)
                        pe.done(e, f"c{t}.{s}", mm)
                    continue
                t = x
                n, k, y = ROWS[t], int(t == 4), Y[t]
                QKT, vb, kd, TT, ATT = QKT_[:, t % SETS], vb_[:, t % SETS], kd_[:, t % SETS], TT_[t], ATT_[t]
                tri, same = cf('tri', P)[0:n, k, 0:n], cf('same', P)[0:n, k, 0:n]
                dve.wait(e, before)
                before = ends[what, t]
                if what == "ready0":
                    dve.wait(e, f"gb{t}")
                    nc.tensor.matmul(bk(0)[0:n, 0:4], tri, g_log[0:n, t, :], start=True, stop=True)
                    pe.done(e, f"g{t}", nc.tensor.matmul(bk(0)[0:n, 4:8], same, g_log[0:n, t, :], start=True, stop=True))
                    for h in range(H4):
                        mm = nc.tensor.matmul(bk(1, 4)[:, h, 0:n], gb[0:n, h, :], tri, start=True, stop=True)
                    pe.done(e, f"gr{t}", mm)
                    for i in range(6):
                        src = y[:, i * P:(i + 1) * P] if i < 4 else kb[0:n, (i - 4) * P:(i - 3) * P]
                        mm = nc.tensor.transpose(bk(2 + i // 4, 4)[:, i % 4, 0:n], src, ident[0:n, 0:n])
                    pe.done(e, f"T{t}", mm)
                if what == "ready1":
                    for nm, b, c in (("kk", 2, 4), ("qk", 0, 0)):
                        for h in range(H4):
                            o = (h % 2) * HD
                            mm = nc.tensor.matmul(bk(b + h % 2, 4)[0:n, h // 2, 0:n], QKT[o:o + HD, 2 + h // 2, 0:n], QKT[o:o + HD, c + h // 2, 0:n],
                                                  start=True, stop=True)
                        pe.done(e, f"{nm}{t}", mm)
                if what == "state0":
                    if t < 4:
                        dve.wait(e, f"s1{t-1}" if t else "z1")
                        for hp in range(2):
                            mm = nc.tensor.matmul(bk(0, 4)[0:n, hp, :], QKT[:, 2 + hp, 0:n], S[:, hp, :], start=True, stop=True)
                    else:
                        dve.wait(e, "qm3")
                        e.wait_ge(loaded, H4 * 16)
                        for hp in range(2):
                            for b in range(NB):
                                mm = nc.tensor.matmul(bk(0, 4)[0:n, hp, :], QM[:, 2 + hp, b, :], SS[:, b, hp, :], start=(b == 0), stop=(b == NB - 1))
                    pe.done(e, f"ks{t}", mm)
                if what == "state1":
                    dve.wait(e, f"tt{t}.{LEVELS[t//2]-1}")
                    for h in range(H4):
                        mm = nc.tensor.matmul(bk(1)[0:n, h * HD:(h + 1) * HD], TT[0:n, h, 0:n], T1[0:n, 256 + h * HD:256 + (h + 1) * HD],
                                              start=True, stop=True)
                    pe.done(e, f"vn{t}", mm)
                    for hp in range(2):
                        if t < 4:
                            mm = nc.tensor.matmul(bk(2, 4)[0:n, hp, :], QKT[:, hp, 0:n], S[:, hp, :], start=True, stop=True)
                        else:
                            for b in range(NB):
                                mm = nc.tensor.matmul(bk(2, 4)[0:n, hp, :], QM[:, hp, b, :], SS[:, b, hp, :], start=(b == 0), stop=(b == NB - 1))
                    pe.done(e, f"qs{t}", mm)
                if what == "state2":
                    for h in range(H4):
                        mm = nc.tensor.matmul(bk(3)[0:n, h * HD:(h + 1) * HD], ATT[0:n, h, 0:n], VN[0:n, h * HD:(h + 1) * HD], start=True, stop=True)
                    pe.done(e, f"av{t}", mm)
                    if t < 4:
                        for hp in range(2):
                            mm = nc.tensor.matmul(bk(0, 4)[:, hp, :], kd[0:n, hp * P:(hp + 1) * P], VN[0:n, hp * P:(hp + 1) * P], start=True, stop=True)
                        pe.done(e, f"su{t}", mm)
                if what == "state3" and t == 4:
                    for i in range(4):
                        hp, q = divmod(i, 2)
                        mm = nc.tensor.matmul(bk(4 + i), kd[0:n, hp * P:(hp + 1) * P], VM[0:n, 4 * q:4 * q + 4, hp * P:(hp + 1) * P],
                                              start=True, stop=True)
                    pe.done(e, f"su{t}", mm)

        @block.vector
        def _(e):
            dve.link(e, "z1", nc.vector.memset(S[:, :, :], 0.0))
            dve.link(e, "z2", nc.vector.memset(SS[:, :, :, :], 0.0))
            e.wait_ge(gl, 16)
            pair = cf('pair')
            h3 = lambda ap: ap.rearrange("p (h c) -> p h c", c=HD)

            def level_mask(name, t, s):
                n = ROWS[t]
                dve.link(e, name, nc.vector.tensor_tensor(NTs_[t % 2][0:n, :, 0:n], NTt_[t][0:n, :, 0:n],
                                                           b_(cf('level', P)[0:n, s, 0:n], 1, [n, H4, n]), ALU.mult))

            for what, x in ORDER:
                if what == "level":
                    tiles, s, levels = x
                    if s == 0:
                        for t in tiles:
                            level_mask(f"ns{t}.0", t, 0)
                    else:
                        for t in tiles if s < levels - 1 else ():
                            pe.wait(e, f"a{t}.{s}")
                            level_mask(f"nn{t}.{s}", t, s + 1)
                    for t in tiles:
                        n, lane = ROWS[t], t % 2
                        T, TT = T_[lane], TT_[t]
                        eye = b_(ident[0:n, 0:n], 1, [n, H4, n])
                        if s < levels - 1:
                            pe.wait(e, f"b{t}.{s}" if s else f"a{t}.{s}")
                            dve.link(e, f"t{t}.{s}", nc.vector.tensor_tensor(T[0:n, :, 0:n], T[0:n, :, 0:n] if s else eye,
                                                                              bk(5 + 2 * lane if s else 4 + 2 * lane, 4)[0:n, :, 0:n], ALU.subtract))
                        if s:
                            pe.wait(e, f"c{t}.{s}")
                        dve.link(e, f"tt{t}.{s}", nc.vector.tensor_tensor(TT[0:n, :, 0:n], TT[0:n, :, 0:n] if s else eye,
                                                                           bk(4 + 2 * lane, 4)[0:n, :, 0:n] if s else NTs_[lane][0:n, :, 0:n], ALU.subtract))
                        if s == 0:
                            level_mask(f"nn{t}.0", t, 1)
                    continue
                t = x
                u, n, k, y = U[t], ROWS[t], int(t == 4), Y[t]
                QKT, vb, kd, NTt, ATT, gs = QKT_[:, t % SETS], vb_[:, t % SETS], kd_[:, t % SETS], NTt_[t], ATT_[t], gs_[:, t]
                hb = lambda ap: b_(ap, 2, [n, H4, HD])
                if what == "ready0":
                    dve.done(e, f"kb{t}", nc.vector.tensor_tensor(h3(kb[0:n, :]), h3(y[:, 256:512]), hb(u[:, GB:GB + H4]), ALU.mult))
                    dve.done(e, f"vb{t}", nc.vector.tensor_tensor(h3(vb[0:n, :]), h3(y[:, 512:768]), hb(u[:, GB:GB + H4]), ALU.mult))
                    dve.done(e, f"gb{t}", nc.vector.tensor_copy(gb[0:n, :, :], b_(g_log[0:n, t, :], 2, [n, H4, P])))
                    pe.wait(e, f"g{t}")
                    dve.done(e, f"g0{t}", nc.vector.tensor_copy(gs[0:n, 0, :], bk(0)[0:n, 0:4]))
                    dve.done(e, f"g1{t}", nc.vector.tensor_scalar(gs[0:n, 1, :], bk(0)[0:n, 0:4], -1.0, None, ALU.mult))
                    dve.link(e, f"g3{t}", nc.vector.tensor_copy(gs[0:n, 3, :], bk(0)[0:n, 4:8]))
                    dve.link(e, f"gd{t}", nc.vector.tensor_tensor(gs[0:n, 5, :], gs[0:n, 3, :], gs[0:n, 0, :], ALU.subtract))
                    act.wait(e, f"sl{t}")
                    dve.done(e, f"lt{t}", nc.vector.tensor_tensor(LT[0:n, :, 0:n], bk(1, 4)[0:n, :, 0:n],
                                                                   b_(cf('neg', P)[0:n, k, 0:n], 1, [n, H4, n]), ALU.add))
                    pe.wait(e, f"T{t}")
                    dve.done(e, f"tr{t}", nc.vector.tensor_copy(QKT[:, 0:4, 0:n], bk(2, 4)[:, :, 0:n]))
                    dve.done(e, f"tr2{t}", nc.vector.tensor_copy(QKT[:, 4:6, 0:n], bk(3, 4)[:, 0:2, 0:n]))
                if what == "ready1":
                    pe.wait(e, f"kk{t}")
                    act.wait(e, f"L3{t}")
                    for o in range(2):
                        dve.done(e, f"nt{o}{t}", nc.vector.tensor_tensor(NTt[0:n, o::2, 0:n], bk(2 + o, 4)[0:n, 0:2, 0:n], LT[0:n, o::2, 0:n], ALU.mult))
                    pe.wait(e, f"qk{t}")
                    for o in range(2):
                        dve.done(e, f"att{o}{t}", nc.vector.tensor_tensor(ATT[0:n, o::2, 0:n], bk(o, 4)[0:n, 0:2, 0:n], LT[0:n, o::2, 0:n], ALU.mult))
                    dve.done(e, f"be{t}", nc.vector.tensor_tensor(gs[0:n, 6, :], gs[0:n, 2, :], u[:, GB:GB + H4], ALU.mult))
                    dve.link(e, f"kd{t}", nc.vector.tensor_tensor(h3(kd[0:n, :]), h3(y[:, 256:512]), hb(gs[0:n, 4, :]), ALU.mult))
                if what == "state0":
                    for i in range(4) if t == 4 else ():
                        dve.link(e, f"qm{i}", nc.vector.tensor_tensor(QM[:, i, :, :], b_(QKT[:, i, 0:64], 1, [P, NB, 64]), cf('own', 64), ALU.mult))
                    pe.wait(e, f"ks{t}")
                    dve.link(e, f"ks{t}", nc.vector.tensor_tensor(h3(T1[0:n, 0:256]), h3(bk(0)[0:n, 0:256]), hb(gs[0:n, 6, :]), ALU.mult))
                    dve.link(e, f"r{t}", nc.vector.tensor_tensor(T1[0:n, 256:512], vb[0:n, :], T1[0:n, 0:256], ALU.subtract))
                if what == "state1":
                    pe.wait(e, f"vn{t}")
                    dve.link(e, f"vn{t}", nc.vector.tensor_copy(VN[0:n, :], bk(1)[0:n, 0:256]))
                if what == "state2":
                    w = 1 if t < 4 else NB
                    dve.done(e, f"sp0{t}", nc.vector.tensor_copy(SLp[0:64, :, 0:w], SL_[0:64, t, 0::2, 0:w]))
                    dve.link(e, f"sp1{t}", nc.vector.tensor_copy(SLp[64:P, :, 0:w], SL_[64:P, t, 1::2, 0:w]))
                    if t < 4:
                        pe.wait(e, f"su{t}")
                        dve.link(e, f"sm{t}", nc.vector.tensor_tensor(T1[:, 0:256].rearrange("p (a b) -> p a b", a=2), bk(0, 4)[:, 0:2, :],
                                                                       b_(pair, 1, [P, 2, P]), ALU.mult))
                        for hp in range(2):
                            dve.link(e, f"s{hp}{t}", nc.vector.scalar_tensor_tensor(
                                S[:, hp, :], S[:, hp, :], SLp[:, hp, 0:1], T1[:, hp * P:(hp + 1) * P], ALU.mult, ALU.add))
                    else:
                        dve.link(e, "vm", nc.vector.tensor_tensor(VM[0:n, :, :], b_(VN[0:n, :], 1, [n, NB, 256]),
                                                                   b_(cf('ownrow')[0:n, :], 2, [n, NB, 256]), ALU.mult))
                        pe.wait(e, f"qs{t}")
                    dve.link(e, f"qs{t}", nc.vector.tensor_tensor(h3(T1[0:n, 0:256]), h3(bk(2)[0:n, 0:256]), hb(gs[0:n, 2, :]), ALU.mult))
                    pe.wait(e, f"av{t}")
                    dve.link(e, f"o{t}", nc.vector.tensor_tensor(Ot[0:n, :], bk(3)[0:n, 0:256], T1[0:n, 0:256], ALU.add))
                if what == "state3":
                    dve.link(e, f"sq{t}", nc.vector.tensor_tensor(T1[0:n, 0:256], Ot[0:n, :], Ot[0:n, :], ALU.mult))
                    dve.link(e, f"va{t}", nc.vector.tensor_reduce(st[0:n, 2, :], h3(T1[0:n, 0:256]), AX.X, ALU.add))
                    act.wait(e, f"rt{t}")
                    dve.link(e, f"rc{t}", nc.vector.reciprocal(st[0:n, 3, :], st[0:n, 2, :]))
                    dve.link(e, f"n1{t}", nc.vector.tensor_tensor(h3(Ot[0:n, :]), h3(Ot[0:n, :]), hb(st[0:n, 3, :]), ALU.mult))
                    dve.link(e, f"n2{t}", nc.vector.tensor_tensor(h3(Ot[0:n, :]), h3(Ot[0:n, :]), b_(gn[0:n, :], 1, [n, H4, HD]), ALU.mult))
                    dve.link(e, f"n3{t}", nc.vector.tensor_tensor(MIX[0:n, t, 768:1024], Ot[0:n, :], u[:, GG:GG + 256], ALU.mult))
                    if t == 4:
                        pe.wait(e, f"su{t}")
                        for i in range(4):
                            hp, q = divmod(i, 2)
                            t3 = T1[:, :].rearrange("p (a b) -> p a b", a=4)
                            sv = SS[:, 4 * q:4 * q + 4, hp, :]
                            dve.link(e, f"ss{i}n", nc.vector.tensor_tensor(sv, sv, b_(SLp[:, hp, 4 * q:4 * q + 4], 2, [P, 4, P]), ALU.mult))
                            dve.link(e, f"ss{i}m", nc.vector.tensor_tensor(t3, bk(4 + i, 4), b_(pair, 1, [P, 4, P]), ALU.mult))
                            dve.link(e, f"ss{i}s", nc.vector.tensor_tensor(sv, sv, t3, ALU.add))




class Compress:

    RING = 4

    def __init__(self, v, tiles, PC, RP, XT, HT, HS, KC, VC):
        self.v, self.nt, self.PC, self.RP, self.XT, self.HT, self.HS, self.KC, self.VC = v, tiles, PC, RP, XT, HT, HS, KC, VC
        self.ns = tiles * P * PAIRS // SEG
        self.nc = -(-self.ns // P)

    def side_by_side(self, e, dve, pe, i, slot):
        if i >= self.RING:
            pe.wait(e, f"T{i-self.RING}")
        dve.done(e, f"R{i}", nc_(self.v).vector.tensor_copy(
            self.RP[:, i % self.RING, :, :, :].rearrange("p h r d -> p r h d"),
            self.PC[:, slot, :, :].rearrange("p r (h d) -> p r h d", d=HD)))

    def transposes(self, e, pe, act, dve, i):
        dve.wait(e, f"R{i}")
        if i >= 2:
            act.wait(e, f"X{i-2}")
        for h in range(2 * G):
            mm = nc_(self.v).tensor.transpose(self.v['bk'](6 + i % 2, 4)[:, h, :],
                                              self.RP[:, i % self.RING, h, :, :].rearrange("p r d -> p (r d)"), self.v['ident'])
        pe.done(e, f"T{i}", mm)

    def copy_out(self, e, act, pe, i):
        pe.wait(e, f"T{i}")
        act.done(e, f"X{i}", nc_(self.v).scalar.activation(self.XT[:, i, :].rearrange("p (h c) -> p h c", c=P), self.v['bk'](6 + i % 2, 4), ACT.Copy))

    def halves(self, e, pe, act, kv, rows=(0, SEG // PAIRS)):
        if rows[0] == 0:
            act.wait(e, "HT0" if kv else f"X{self.nt-1}")
        seg = self.XT[:, 0:self.nt, :].rearrange("p i (h n s) -> p h i n s", h=2 * G, s=SEG // PAIRS)[:, kv * G:(kv + 1) * G]
        out = self.v['bk'](2)[:, 0:G * self.ns].rearrange("p (g i n) -> p g i n", g=G, i=self.nt)
        for s in range(*rows):
            mm = nc_(self.v).tensor.matmul(out, self.v['W1'][:, kv, s, :], seg[:, :, :, :, s], start=(s == 0), stop=(s == SEG // PAIRS - 1))
        if rows[1] == SEG // PAIRS:
            pe.done(e, f"H{kv}", mm)

    def join(self, e, pe, act, dve, kv):
        ns, ident = self.ns, self.v['ident']
        act.wait(e, f"HT{kv}")
        if kv:
            dve.wait(e, "C0")
        ht = self.HT[:, 0:G * ns].rearrange("p (g n) -> p g n", g=G)
        out = self.v['bk'](3)[0:HD, 0:G * (ns - 1)].rearrange("p (g n) -> p g n", g=G)
        nc_(self.v).tensor.matmul(out, ident[:, 0:HD], ht[:, :, 0:ns - 1], start=True, stop=False)
        pe.done(e, f"J{kv}", nc_(self.v).tensor.matmul(out, ident[:, HD:P], ht[:, :, 1:ns], start=False, stop=True))

    def second(self, e, pe, act, kv):
        v, ns, hs = self.v, self.ns, self.HS
        act.wait(e, f"HS{kv}")
        if kv == 0:
            for g in range(G):
                mm = nc_(v).tensor.matmul(v['bk'](3)[:, 0:ns], v['W2'][:, kv, g, :], hs[:, g, 0:ns], start=(g == 0), stop=(g == G - 1))
        else:
            for c in range(self.nc):
                for g in range(G):
                    mm = nc_(v).tensor.matmul(v['bk'](3)[0:min(P, ns), c * P + g * HD:c * P + (g + 1) * HD],
                                              hs[:, g, c * P:min(ns, (c + 1) * P)], v['W2'][:, kv, 0, 0:HD], start=True, stop=True)
        pe.done(e, f"C{kv}", mm)

    def half_copy(self, e, act, pe, kv):
        pe.wait(e, f"H{kv}")
        if kv:
            pe.wait(e, "J0")
        act.done(e, f"HT{kv}", nc_(self.v).scalar.activation(self.HT[:, 0:G * self.ns], self.v['bk'](2)[:, 0:G * self.ns], ACT.Copy))

    def silu(self, e, act, pe, kv):
        ns = self.ns
        pe.wait(e, f"J{kv}")
        if kv:
            pe.wait(e, "C0")
        act.done(e, f"HS{kv}", nc_(self.v).scalar.activation(
            self.HS[:, :, 0:ns - 1], self.v['bk'](3)[0:HD, 0:G * (ns - 1)].rearrange("p (g n) -> p g n", g=G),
            ACT.Silu, bias=self.v['B1'][:, kv:kv + 1]))

    def keep(self, e, dve, pe, kv):
        pe.wait(e, f"C{kv}")
        m = min(P, self.ns)
        if kv == 0:
            dve.done(e, "C0", nc_(self.v).vector.tensor_copy(self.KC[:, 0:self.ns], self.v['bk'](3)[:, 0:self.ns]))
        else:
            dve.done(e, "C1", nc_(self.v).vector.tensor_copy(self.VC[0:m, 0:self.nc, :], self.v['bk'](3, 4)[0:m, 0:self.nc, :]))


def nc_(v):
    return v['nc']


def prompt_attention(nc, A, O, l, scope, sb, stage, v, U):
    bk, cf, cb, ident, MIX = v['bk'], v['cf'], v['cb'], v['ident'], v['MIX']
    QT = sb(scope, "QT", [P, 2, R, SEQ])
    KT = sb(scope, "KT", [P, 2, SEQ])
    KC = sb(scope, "KCp", [P, 32])
    VC = sb(scope, "VCp", [P, 1, P])
    early = scope.enter_context(ExitStack())
    QRP = sb(early, "QRP", [P, 4, 2, 512])
    PG = sb(early, "PG", [P, 2, PAIRS, 256])
    RP = sb(early, "RPp", [P, 4, 2 * G, PAIRS, HD])
    XT = sb(early, "XTp", [P, 2, 512])
    HT = sb(early, "HTp", [P, 64])
    HS = sb(early, "HSp", [HD, G, 32])
    W1, W2, B1 = v['W1'], v['W2'], v['B1']
    with stage(["dve_s", "act_s", "pe_s", "weights", "rows"]) as (block, (dve_s, act_s, pe_s, weights, rows)):
        cp = Compress(v, 2, PG, RP, XT, HT, HS, KC, VC)
        pe = Steps(pe_s, ["T0", "T1", "H0", "J0", "C0", "H1", "J1", "C1"] + [f"{x}{t}" for t in range(4) for x in ("Tq", "Tr", "Tk")])
        act = Steps(act_s, ["X0", "X1", "HT0", "HS0", "HT1", "HS1"] + [f"Tr{t}" for t in range(4)])
        dve = Steps(dve_s, ["z0", "z1", "R0", "R1", "C0", "C1"] + [f"{x}{t}" for t in range(4) for x in ("Tq", "Tk")])

        @block.sync
        def _(e):
            for i in range(2):
                e.dma_start(PG[:, i, :, :], O['kv_prompt'][l, 0].rearrange("(t p r) a g d -> t p r (a g d)", p=P, r=PAIRS)[i, :, :, 0:256]).then_inc(rows, 16)
            e.dma_start(QRP[:, :, :, :].rearrange("p t i c -> p t (i c)"), A['q_rot'].rearrange("(t p) c -> p t c", p=P)).then_inc(rows, 16)
            dve.wait(e, "z0")
            for kv in range(2):
                for half in range(2):
                    for r in range(PAIRS):
                        e.dma_start(W1[r * HD:(r + 1) * HD, kv, :, half * HD:(half + 1) * HD],
                                    A['cmp_w1'][l, kv].rearrange("(h s r) d e -> h r d s e", h=2, r=PAIRS)[half, r]).then_inc(weights, 16)
                for g in range(G):
                    e.dma_start(W2[:, kv, g, g * HD:(g + 1) * HD], A['cmp_w2'][l, kv]).then_inc(weights, 16)
            e.dma_start(B1[:, :], A['cmp_b1'][l].rearrange("k e -> e k"), allow_slow_non_contiguous=True).then_inc(weights, 16)

        @block.tensor
        def _(e):
            e.wait_ge(weights, 13 * 16)
            e.wait_ge(rows, 48)
            for i in range(2):
                cp.transposes(e, pe, act, dve, i)
            for kv in range(2):
                cp.halves(e, pe, act, kv)
                cp.join(e, pe, act, dve, kv)
                cp.second(e, pe, act, kv)
            dve.wait(e, "C1")
            for t in range(4):
                if t:
                    dve.wait(e, f"Tq{t-1}")
                for r in range(R):
                    mm = nc.tensor.transpose(bk(0, 4)[:, r, :], QRP[:, t, 0, r * P:(r + 1) * P], ident)
                pe.done(e, f"Tq{t}", mm)
                if t:
                    act.wait(e, f"Tr{t-1}")
                for r in range(R):
                    mm = nc.tensor.transpose(bk(1, 4)[:, r, :], QRP[:, t, 1, r * P:(r + 1) * P], ident)
                pe.done(e, f"Tr{t}", mm)
                if t:
                    dve.wait(e, f"Tk{t-1}")
                for i in range(2):
                    mm = nc.tensor.transpose(bk(2, 4)[:, i, :], U[t][:, NKV + 256 * (i + 1):NKV + 256 * (i + 1) + P], ident)
                pe.done(e, f"Tk{t}", mm)

        @block.scalar
        def _(e):
            e.wait_ge(weights, 13 * 16)
            dve.wait(e, "z1")
            for i in range(2):
                cp.copy_out(e, act, pe, i)
            for kv in range(2):
                cp.half_copy(e, act, pe, kv)
                cp.silu(e, act, pe, kv)
            for t in range(4):
                pe.wait(e, f"Tr{t}")
                act.done(e, f"Tr{t}", nc.scalar.activation(QT[:, 1, :, t * P:(t + 1) * P], bk(1, 4), ACT.Copy))

        @block.vector
        def _(e):
            dve.link(e, "z0", nc.vector.memset(W2[:, :, :, :], 0.0))
            dve.link(e, "z1", nc.vector.memset(HS[:, :, :], 0.0))
            e.wait_ge(rows, 48)
            for i in range(2):
                cp.side_by_side(e, dve, pe, i, i)
            for kv in range(2):
                cp.keep(e, dve, pe, kv)
            for t in range(4):
                pe.wait(e, f"Tq{t}")
                dve.done(e, f"Tq{t}", nc.vector.tensor_copy(QT[:, 0, :, t * P:(t + 1) * P], bk(0, 4)))
                pe.wait(e, f"Tk{t}")
                dve.done(e, f"Tk{t}", nc.vector.tensor_copy(KT[:, :, t * P:(t + 1) * P], bk(2, 4)[:, 0:2, :]))

    early.close()
    Pr = sb(scope, "Pr", [P, 2, SEQ])
    PT = sb(scope, "PT", [P, 2, 4, P])
    mx = sb(scope, "mx", [P, 2, 2])
    SUM = sb(scope, "SUM", [P, 2, NH])
    fac = sb(scope, "fac", [P, NH])
    T1 = sb(scope, "T1", [P, 512])
    NO = sb(scope, "NO", [P, 512])
    units = [(qt, br, h) for qt in range(4) for br in range(3) for h in range(NH)]
    NU = len(units)
    with stage(["score", "shift", "exped", "turned", "copied", "used", "link_s", "merged"]) as \
            (block, (score, shift, exped, turned, copied, used, link_s, merged)):

        def keys(u):
            qt, br, h = units[u]
            return NCP if br == 0 else (qt + 1) * P

        @block.tensor
        def _(e):
            def scores(u):
                qt, br, h = units[u]
                g, r, n = h // R, h % R, keys(u)
                if u >= 2:
                    e.wait_ge(exped, u - 1)
                kt = KC[g * HD:(g + 1) * HD, 0:n] if br == 0 else KT[g * HD:(g + 1) * HD, br - 1, 0:n]
                nc.tensor.matmul(bk(u % 2)[:, 0:n], QT[g * HD:(g + 1) * HD, min(br, 1), r, qt * P:(qt + 1) * P], kt, start=True, stop=False)
                m = cb('cmask', 32)[:, qt, 0:n] if br == 0 else cb('causal')
                nc.tensor.matmul(bk(u % 2)[:, 0 if br == 0 else qt * P:n], cb('identb'), m, start=False, stop=True).then_inc(score, 1)

            def turn(u):
                n = keys(u)
                e.wait_ge(exped, u + 1)
                if u >= 2:
                    e.wait_ge(copied, u - 1)
                for j in range(-(-n // P)):
                    m = min(P, n - j * P)
                    mm = nc.tensor.transpose(bk(2 + u % 2, 4)[0:m, j, :], Pr[:, u % 2, j * P:j * P + m], ident)
                mm.then_inc(turned, 1)

            def values(u):
                qt, br, h = units[u]
                g, n, q = h // R, keys(u), u // NH
                e.wait_ge(copied, u + 1)
                if h == 0 and q >= 2:
                    e.wait_ge(merged, q - 1)
                for j in range(-(-n // P)):
                    m = min(P, n - j * P)
                    vv = VC[0:m, 0, g * HD:(g + 1) * HD] if br == 0 else U[j][:, NKV + P + 256 * br + g * HD:NKV + P + 256 * br + (g + 1) * HD]
                    mm = nc.tensor.matmul(bk(4 + q % 2)[:, h * HD:(h + 1) * HD], PT[0:m, u % 2, j, :], vv, start=(j == 0), stop=(j == -(-n // P) - 1))
                mm.then_inc(used, 1)

            for u in range(NU + 2):
                if u < NU:
                    scores(u)
                if 0 < u <= NU:
                    turn(u - 1)
                if u >= 2:
                    values(u - 2)

        @block.scalar
        def _(e):
            for u in range(NU):
                qt, br, h = units[u]
                n = keys(u)
                e.wait_ge(shift, u + 1)
                if u >= 2:
                    e.wait_ge(turned, u - 1)
                nc.scalar.activation(Pr[:, u % 2, 0:n], bk(u % 2)[:, 0:n], ACT.Exp, scale=SCALE, bias=mx[:, u % 2, 1:2],
                                     accum_out=SUM[:, (u // NH) % 2, h:h + 1]).then_inc(exped, 1)

        @block.vector
        def _(e):
            links = [0]

            def link(ins):
                links[0] += 1
                ins.then_inc(link_s, 1)
                e.wait_ge(link_s, links[0])

            def biggest(u):
                n = keys(u)
                e.wait_ge(score, u + 1)
                link(nc.vector.tensor_reduce(mx[:, u % 2, 0:1], bk(u % 2)[:, 0:n], AX.X, ALU.max))
                nc.vector.tensor_scalar(mx[:, u % 2, 1:2], mx[:, u % 2, 0:1], -1e20, -SCALE, ALU.max, ALU.mult).then_inc(shift, 1)

            def copy(u):
                n = keys(u)
                m, k = (n, 1) if n < P else (P, n // P)
                e.wait_ge(turned, u + 1)
                if u >= 2:
                    e.wait_ge(used, u - 1)
                nc.vector.tensor_copy(PT[0:m, u % 2, 0:k, :], bk(2 + u % 2, 4)[0:m, 0:k, :]).then_inc(copied, 1)

            def merge(u):
                qt, br, h = units[u]
                q = u // NH
                hb = lambda ap: ap.rearrange("p (h c) -> p h c", c=HD)
                e.wait_ge(used, u + 1)
                e.wait_ge(exped, u + 1)
                link(nc.vector.tensor_scalar(fac[:, :], SUM[:, q % 2, :], 1e-30, None, ALU.max))
                link(nc.vector.reciprocal(fac[:, :], fac[:, :]))
                link(nc.vector.tensor_tensor(fac[:, :], fac[:, :], U[qt][:, NGATE + br * NH:NGATE + (br + 1) * NH], ALU.mult))
                dst = NO if br == 0 else T1
                links[0] += 1
                nc.vector.tensor_tensor(hb(dst[:, :]), hb(bk(4 + q % 2)), b_(fac[:, :], 2, [P, NH, HD]), ALU.mult).then_inc(link_s, 1)
                e.wait_ge(link_s, links[0])
                if br:
                    link(nc.vector.tensor_tensor(NO[:, :], NO[:, :], T1[:, :], ALU.add))
                if br == 2:
                    link(nc.vector.tensor_tensor(MIX[:, qt, 256:768], NO[:, :], U[qt][:, NG:NG + 512], ALU.mult))
                nc.vector.engine_nop().then_inc(merged, 1)

            for u in range(NU + 2):
                if u < NU:
                    biggest(u)
                if 0 < u <= NU:
                    copy(u - 1)
                if u >= 2 and (u - 2) % NH == NH - 1:
                    merge(u - 2)


def sample_attention(nc, A, O, l, scope, sb, stage, v):
    bk, cf, cb, ident, MIX, US = v['bk'], v['cf'], v['cb'], v['ident'], v['MIX'], v['US']
    SLOTS = 8
    PC = sb(scope, "PC", [P, SLOTS, PAIRS, 256])
    XT = sb(scope, "XT", [P, GT, 512])
    pc_rows = [[scope.enter_context(nc.semaphore(f"pc_{x}{i}")) for i in range(SLOTS)] for x in ("even", "odd")]
    sel_rows = [[scope.enter_context(nc.semaphore(f"sel_{x}{i}")) for i in range(8)] for x in ("even", "odd")]
    PS = sb(scope, "PS", [P, GT, PAIRS, 256])
    PSg = PS[:, :, :, :].rearrange("p i r c -> p (i r) c")
    HT = sb(scope, "HT", [P, 512])
    HS = sb(scope, "HS", [HD, G, NSEG])
    KC = sb(scope, "KC", [P, NSEG])
    VC = sb(scope, "VC", [P, 2, P])
    PW = sb(scope, "PW", [P, 4, 256])
    PB = sb(scope, "PB", [P, 2 + 5 + NKEYG, COLS])
    QBD = sb(scope, "QBD", [P, 2, NB, COLS])
    QB = sb(scope, "QB", [P, 2, COLS])
    KNT = sb(scope, "KNT", [P, 2, NB * NT])
    KN = sb(scope, "KN", [P, 2, P])
    VN = sb(scope, "VNn", [P, 2, P])
    OT = sb(scope, "OT", [P, 3, R, NB, NT])
    RP = sb(scope, "RP", [P, 4, 2 * G, PAIRS, HD])
    MX = sb(scope, "MX", [P, 2, COLS])
    sm = sb(scope, "sm", [P, 2, 4, COLS])
    PR = sb(scope, "PR", [P, 2, 2, COLS])
    m1 = sb(scope, "m1", [COLS, 2])
    nd = sb(scope, "nd", [COLS, 2, COLS])
    top = sb(scope, "top", [16, 3, NBLK + 1])
    t8 = sb(scope, "t8", [16, 2, 8])
    BT = sb(scope, "BT", [HD, COLS], BF16)
    ids = sb(scope, "ids", [1, 2, (NB + 2) * GT], I32)
    REGS = v['REGS']

    def fetch(e, where, slot, side, page, c, sem):
        e.dma_start(where[side * HD:(side + 1) * HD, slot, :, :],
                    A['cache_nsa_kv'][l, page].rearrange("(p r) a g d -> p r (a g d)", r=PAIRS)[:, :, c:c + 256]).then_inc(sem, 16)

    def first_pages(e, side):
        e.load(REGS[side][0:8], ids[0:1, side, 0:SLOTS])
        for n, r in enumerate(REGS[side][0:8]):
            fetch(e, PC, n, side, e.snap(r), 0, pc_rows[side][n])

    with stage(["dve_s", "pe_s", "kv", "idl"]) as (block, (dve_s, pe_s, kv, idl)):
        dve = Steps(dve_s, ["z0", "z1", "z2", "z3"] + [f"q{i}{g}" for i in range(2) for g in range(G)] + ["k"])
        pe = Steps(pe_s, ["q0", "q1", "k"])

        @block.sync
        def _(e):
            for side in range(2):
                pages = A['page_table'].rearrange("b (n s) -> s (b n)", s=2)[side:side + 1]
                for at, n in ((0, NB * GT), (NB * GT, 2 * GT)):
                    e.dma_start(ids[0:1, side, at:at + n], pages[:, 0:n], allow_slow_non_contiguous=True).then_inc(idl, 16)
            e.dma_start(A['new_kv'].rearrange("b t c -> (b t) c"), US[0:64, NKV:NKV + CW]).then_inc(kv, 16)
            e.wait_ge(idl, 64)
            first_pages(e, 0)
            e.wait_ge(kv, 16)

        @block.gpsimd
        def _(e):
            e.wait_ge(idl, 64)
            first_pages(e, 1)

        @block.tensor
        def _(e):
            for i in range(2):
                for r in range(R):
                    mm = nc.tensor.transpose(bk(i, 8)[:, r, 0:64], v['QRS'][0:64, i, r * P:(r + 1) * P], ident[0:64, 0:64])
                pe.done(e, f"q{i}", mm)
            for i in range(2):
                mm = nc.tensor.transpose(bk(2, 8)[:, i, 0:64], US[0:64, NKV + 256 * (i + 1):NKV + 256 * (i + 1) + P], ident[0:64, 0:64])
            pe.done(e, "k", mm)

        @block.vector
        def _(e):
            dve.done(e, "z0", nc.vector.memset(QBD[:, :, :, :], 0.0))
            dve.done(e, "z1", nc.vector.memset(KN[:, :, :], 0.0))
            dve.done(e, "z2", nc.vector.memset(VN[:, :, :], 0.0))
            dve.link(e, "z3", nc.vector.memset(HS[:, :, :], 0.0))
            for i in range(2):
                pe.wait(e, f"q{i}")
                for g in range(G):
                    o = g * HD
                    dve.done(e, f"q{i}{g}", nc.vector.tensor_copy(
                        QBD[o:o + HD, i, :, g * 32:(g + 1) * 32].rearrange("p b (r t) -> p b r t", r=R),
                        bk(i, 8)[o:o + HD, 0:R, 0:64].rearrange("p r (b t) -> p b r t", b=NB)))
            pe.wait(e, "k")
            dve.done(e, "k", nc.vector.tensor_copy(KNT[:, :, :], bk(2, 8)[:, 0:2, 0:64]))

    B4 = bk(4, 8)
    SEL = 7
    CHAIN = {'w': (bk(5), bk(5), 0), 's': (bk(5), bk(6), 0), 'c': (bk(7), bk(7), 1)}

    def step(b, attend, compress):
        sems = ["dve_s", "act_s", "pe_s"] + (["win_rows"] if attend else [])
        with stage(sems) as (block, got):
            dve_s, act_s, pe_s = got[0:3]
            win_rows = got[3] if attend else None
            cp = Compress(v, GT, PC, RP, XT, HT, HS, KC, VC)
            at = lambda *n: list(n) if attend else []
            co = lambda *n: list(n) if compress else []
            two = lambda x, i: co(f"{x}{i}", f"{x}{i+1}")
            AFTER = {1: ["wt"], 2: ["w4"], 3: ["wmt"], 4: ["wnb"], 6: ["wsb"], 7: ["wpv"]}
            pe = Steps(pe_s, at("kt0", "kt1") + two("T", 0) +
                       sum([at(f"ks{j}") + (two("T", 2 * j + 2) if j < 7 else []) + at(*AFTER.get(j, [])) for j in range(8)], []) +
                       at("smt", "snb") + co("H0", "J0", "C0", "c4", "cmt", "cnb") + at("ssb") + co("csb", "H1") + at("spa") + co("sc", "J1", "scT") + at("spv") + co("C1", "cpv"))
            act = Steps(act_s, at("kt0", "kt1") + two("X", 0) +
                        sum([(at(f"kt{j+2}") if j < 6 else []) + (at(f"S{j//2}") if j % 2 else []) + (two("X", 2 * j + 2) if j < 7 else []) +
                             at(*{1: ["wt"], 4: ["we"]}.get(j, [])) for j in range(8)], []) +
                        co("HT0") + at("se") + co("HS0", "ce", "HT1", "HS1"))
            dve = Steps(dve_s, co("qp") + at("qb", "kn") + co(*[f"R{i}" for i in range(10)]) + at("wx0") + two("R", 10) + at("wm", "wnd") + two("R", 12) +
                        at("wnm", "ws0", "S4") + two("R", 14) + at("wps", "wcl", "wrc", "wo0", "wo1") +
                        at("sx0", "sm", "snd", "snm", "ss0", "sps") + co("C0", "cx0", "cm", "cnd", "cnm", "cs0") + at("scl", "src") +
                        co("cps", "ccl", "crc", "pn", "pr0", "pr1", "sf", "t1", "r1", "t2", "r2", "bi") + co("bt", "C1") + at("so0", "so1") + co("co0", "co1"))
            here = (lambda n: slice(b * n, (b + 1) * n)) if isinstance(b, int) else (lambda n: bass.ds(b * n, n))
            after = (lambda n: slice((b + 1) * n, (b + 2) * n)) if isinstance(b, int) else (lambda n: bass.ds(b * n + n, n))

            def eight(e, regs, side, n):
                at_ = (b * GT + n) if isinstance(b, int) else bass.ds(b * GT + n, 8)
                e.load(regs, ids[0:1, side, at_:at_ + 8] if isinstance(b, int) else ids[0:1, side, at_])
                return [e.snap(r) for r in regs]

            def ahead(e, side, j, pages):
                dve.wait(e, f"R{j}")
                fetch(e, PC, j % SLOTS, side, pages[j % 8], 0, pc_rows[side][j % SLOTS])

            def selected(e, side, k, pages):
                fetch(e, PS, k, side, pages[k % 8], 256, sel_rows[side][k // 2])

            @block.sync
            def _(e):
                if attend:
                    even, odd = eight(e, REGS[0][0:8], 0, GT // 2), eight(e, REGS[0][8:16], 1, GT // 2)
                if compress:
                    stream = eight(e, REGS[0][16:24], 0, GT + SLOTS)
                for k in range(8):
                    if attend:
                        selected(e, 0, 8 + k, even)
                        if k // 2 % 2 == 0:
                            selected(e, 1, 8 + k, odd)
                    if compress:
                        ahead(e, 0, k, stream)
                    if attend and k == 1:
                        e.dma_start(PW[:, :, :], A['state_nsa_win'][l, b].rearrange("(c p) a g d -> p c (a g d)", p=P)).then_inc(win_rows, 16)
                        for i in range(2):
                            e.dma_start(VN[0:NT, i, :], A['new_kv'][b][:, 256 * (i + 1) + P:256 * (i + 2)]).then_inc(win_rows, 16)
                if compress:
                    stream = eight(e, REGS[0][16:24], 0, GT + SLOTS + 8)
                    even, odd = eight(e, REGS[0][0:8], 0, GT), eight(e, REGS[0][8:16], 1, GT)
                    for k in range(8, GT):
                        ahead(e, 0, k, stream)
                    if attend:
                        pe.wait(e, "spa")
                    for k in range(8):
                        selected(e, 0, k, even)
                        if k // 2 % 2 == 0:
                            selected(e, 1, k, odd)

            @block.gpsimd
            def _(e):
                if attend:
                    odd = eight(e, REGS[1][0:8], 1, GT // 2)
                if compress:
                    stream = eight(e, REGS[1][8:16], 1, GT + SLOTS)
                for k in range(8):
                    if compress:
                        ahead(e, 1, k, stream)
                    if attend and k % 2:
                        selected(e, 1, (10, 11, 14, 15)[k // 2], odd)
                if compress:
                    stream = eight(e, REGS[1][8:16], 1, GT + SLOTS + 8)
                    odd = eight(e, REGS[1][0:8], 1, GT)
                    for k in range(8, GT):
                        ahead(e, 1, k, stream)
                    if attend:
                        pe.wait(e, "spa")
                    for k in (2, 3, 6, 7):
                        selected(e, 1, k, odd)

            @block.tensor
            def _(e):
                def T(i):
                    for k in (i, i + 1) if compress else ():
                        cp.transposes(e, pe, act, dve, k)

                def max_t(a):
                    M, _, s = CHAIN[a]
                    dve.wait(e, f"{a}x0")
                    pe.done(e, f"{a}mt", nc.tensor.transpose(M[0:COLS, 0:P], MX[:, s, :], ident))

                def neg_b(a):
                    M, _, s = CHAIN[a]
                    dve.wait(e, f"{a}nd")
                    pe.done(e, f"{a}nb", nc.tensor.matmul(M[:, P:P + COLS], v['ones'][0:COLS, :], nd[:, s, :], start=True, stop=True))

                def sum_b(a):
                    M, _, s = CHAIN[a]
                    dve.wait(e, f"{a}ps")
                    pe.done(e, f"{a}sb", nc.tensor.matmul(M[:, 192:256], v['ones'][:, :], sm[:, s, 1, :], start=True, stop=True))

                def values(a, lo=0, hi=None):
                    vs, o = {'c': ([VC[:, c, :] for c in range(2)], 0),
                             'w': ([PW[:, c, P:256] for c in range(4)] + [VN[:, 1, :]], 2),
                             's': ([PSg[:, i, P:256] for i in range(2 * GT)] + [VN[:, 0, :]], SEL)}[a]
                    out = CHAIN[a][1][:, 256:320]
                    hi = len(vs) if hi is None else hi
                    for i in range(lo, hi):
                        mm = nc.tensor.matmul(out, vs[i], PB[:, o + i, :], start=(i == 0), stop=(i == len(vs) - 1))
                    if hi in (len(vs), GT):
                        pe.done(e, f"{a}pv" if hi == len(vs) else f"{a}pa", mm)

                def key_t(j):
                    for side in range(2):
                        e.wait_ge(sel_rows[side][j], 32 * (b + 1))
                    if j >= 2:
                        act.wait(e, f"kt{j-2}")
                    for c in range(4):
                        mm = nc.tensor.transpose(bk(2 + j % 2, 4)[:, c, :], PSg[:, 4 * j + c, 0:P], ident)
                    return mm

                def key_scores(j):
                    act.wait(e, f"kt{j}")
                    if j + 2 < 8:
                        key_t(j + 2)
                    if j % 2 == 0 and j >= 4:
                        act.wait(e, f"S{j//2-2}")
                    for c in range(4):
                        i = 4 * j + c
                        mm = nc.tensor.matmul(bk((j // 2) % 2, 8)[:, i % 8, :], PSg[:, i, 0:P], QB[:, 1, :], start=(i % 8 == 0), stop=False,
                                              skip_group_check=True)
                    if j % 2:
                        for t in range(2 * j - 2, 2 * j + 2):
                            mm = nc.tensor.matmul(bk((j // 2) % 2, 8)[:, 2 * (t % 4):2 * (t % 4) + 2, :], cb('blockof', P)[0:HD, t, :],
                                                  b_(BT[:, :], 1, [HD, 2, COLS]), start=False, stop=(t % 4 == 3), skip_group_check=True)
                    pe.done(e, f"ks{j}", mm)

                if attend:
                    dve.wait(e, "kn")
                    for j in range(2):
                        pe.done(e, f"kt{j}", key_t(j))
                T(0)
                for j in range(8):
                    if attend:
                        key_scores(j)
                    if j < 7:
                        T(2 * j + 2)
                    if attend and j == 1:
                        e.wait_ge(win_rows, 48)
                        for c in range(4):
                            mm = nc.tensor.transpose(bk(4, 4)[:, c, :], PW[:, c, 0:P], ident)
                        pe.done(e, "wt", mm)
                    if attend and j == 2:
                        act.wait(e, "wt")
                        for c in range(4):
                            nc.tensor.matmul(B4[:, 2 + c, :], PW[:, c, 0:P], QB[:, 1, :], start=True, stop=(c > 0))
                            if c == 0:
                                nc.tensor.matmul(B4[:, 2, :], cb('identb'), cb('winmask'), start=False, stop=True)
                        for i, c in ((1, 6), (0, 7)):
                            nc.tensor.matmul(B4[:, c, :], KN[:, i, :], QB[:, 1, :], start=True, stop=False)
                            mm = nc.tensor.matmul(B4[:, c, :], cb('identb'), cb('newmask'), start=False, stop=True)
                        pe.done(e, "w4", mm)
                    if attend and j == 3:
                        max_t('w')
                    if attend and j == 4:
                        neg_b('w')
                    if attend and j == 6:
                        sum_b('w')
                    if attend and j == 7:
                        dve.wait(e, "wrc")
                        values('w')
                if compress:
                    cp.halves(e, pe, act, 0, (0, 3))
                if attend:
                    dve.wait(e, "wo1")
                    max_t('s')
                if compress:
                    cp.halves(e, pe, act, 0, (3, 6))
                if attend:
                    neg_b('s')
                if compress:
                    cp.halves(e, pe, act, 0, (6, 8))
                    cp.join(e, pe, act, dve, 0)
                    cp.halves(e, pe, act, 1, (0, 3))
                    cp.second(e, pe, act, 0)
                    cp.halves(e, pe, act, 1, (3, 4))
                    dve.wait(e, "C0")
                    if attend:
                        act.wait(e, "S2")
                    for c in range(2):
                        mm = nc.tensor.matmul(bk(0, 8)[:, c, :], KC[:, c * P:(c + 1) * P], QB[:, 0, :], start=True, stop=(c == 0))
                        if c:
                            mm = nc.tensor.matmul(bk(0, 8)[:, c, :], cb('identb'), cb('padmask'), start=False, stop=True)
                    pe.done(e, "c4", mm)
                if attend:
                    act.wait(e, "se")
                    values('s', 0, 3)
                if compress:
                    max_t('c')
                if attend:
                    values('s', 3, 6)
                if compress:
                    neg_b('c')
                    cp.halves(e, pe, act, 1, (4, 7))
                if attend:
                    sum_b('s')
                if compress:
                    sum_b('c')
                    cp.halves(e, pe, act, 1, (7, 8))
                if attend:
                    values('s', 6, GT)
                if compress:
                    dve.wait(e, "pr1")
                    for c in range(2):
                        mm = nc.tensor.matmul(bk(7)[0:16, 320:320 + NBLK], PR[:, 1, c, 0:16], cf('overlap', NBLK)[:, c, :], start=(c == 0), stop=(c == 1))
                    pe.done(e, "sc", mm)
                    cp.join(e, pe, act, dve, 1)
                if attend:
                    values('s', GT, GT + 6)
                if compress:
                    dve.wait(e, "bi")
                    pe.done(e, "scT", nc.tensor.transpose(bk(7)[0:HD, 400:416], top[:, 1, 0:HD], ident[0:16, 0:16]))
                if attend:
                    values('s', GT + 6)
                if compress:
                    cp.second(e, pe, act, 1)
                    dve.wait(e, "C1")
                    values('c')

            @block.scalar
            def _(e):
                def X(i):
                    for k in (i, i + 1) if compress else ():
                        cp.copy_out(e, act, pe, k)

                def ex(a, o, n):
                    dve.wait(e, f"{a}s0")
                    ap = PB[:, o:o + n, :]
                    act.done(e, f"{a}e", nc.scalar.activation(ap, ap, ACT.Exp, scale=SCALE))

                def kt(j):
                    pe.wait(e, f"kt{j}" if j < 2 else f"ks{j-2}")
                    act.done(e, f"kt{j}", nc.scalar.activation(PSg[:, 4 * j:4 * j + 4, 0:P], bk(2 + j % 2, 4), ACT.Copy))

                if attend:
                    kt(0)
                    kt(1)
                X(0)
                for j in range(8):
                    if attend and j < 6:
                        kt(j + 2)
                    if attend and j % 2:
                        pe.wait(e, f"ks{j}")
                        act.done(e, f"S{j//2}", nc.scalar.activation(PB[:, SEL + 4 * j - 4:SEL + 4 * j + 4, :], bk(j // 2 % 2, 8), ACT.Copy))
                    if j < 7:
                        X(2 * j + 2)
                    if attend and j == 1:
                        pe.wait(e, "wt")
                        act.done(e, "wt", nc.scalar.activation(PW[:, :, 0:P], bk(4, 4), ACT.Copy))
                    if attend and j == 4:
                        ex('w', 2, 5)
                if compress:
                    cp.half_copy(e, act, pe, 0)
                if attend:
                    ex('s', SEL, NKEYG)
                if compress:
                    cp.silu(e, act, pe, 0)
                    ex('c', 0, 2)
                    cp.half_copy(e, act, pe, 1)
                    cp.silu(e, act, pe, 1)

            @block.vector
            def _(e):
                def Rr(a, z):
                    for i in range(a, z) if compress else ():
                        for side in range(2):
                            e.wait_ge(pc_rows[side][i % SLOTS], 16 * (2 * (b + 1) + i // SLOTS + 1))
                        cp.side_by_side(e, dve, pe, i, i % SLOTS)

                def biggest(a, src):
                    dve.link(e, f"{a}x0", nc.vector.tensor_reduce(MX[:, CHAIN[a][2], :], src.rearrange("p n c -> p c n"), AX.X, ALU.max))

                def to_row(a):
                    M, _, s = CHAIN[a]
                    pe.wait(e, f"{a}mt")
                    dve.link(e, f"{a}m", nc.vector.tensor_reduce(m1[:, s:s + 1], M[0:COLS, 0:P], AX.X, ALU.max))
                    dve.link(e, f"{a}nd", nc.vector.tensor_scalar(nd[:, s, :], ident[0:COLS, 0:COLS], m1[:, s:s + 1], -1.0, ALU.mult, ALU.mult))

                def shift(a, src, o, n):
                    M, _, s = CHAIN[a]
                    pe.wait(e, f"{a}nb")
                    dve.link(e, f"{a}nm", nc.vector.tensor_copy(sm[:, s, 0, :], M[:, P:P + COLS]))
                    dve.done(e, f"{a}s0", nc.vector.tensor_tensor(PB[:, o:o + n, :], src, b_(sm[:, s, 0, :], 1, [P, n, COLS]), ALU.add))

                def sums(a, o, n):
                    act.wait(e, f"{a}e")
                    dve.link(e, f"{a}ps", nc.vector.tensor_reduce(sm[:, CHAIN[a][2], 1, :], PB[:, o:o + n, :].rearrange("p n c -> p c n"), AX.X, ALU.add))

                def inverse(a):
                    M, _, s = CHAIN[a]
                    pe.wait(e, f"{a}sb")
                    dve.link(e, f"{a}cl", nc.vector.tensor_scalar(sm[:, s, 2, :], M[:, 192:256], 1e-30, None, ALU.max))
                    dve.link(e, f"{a}rc", nc.vector.reciprocal(sm[:, s, 3, :], sm[:, s, 2, :]))

                def outs(a, br, where):
                    pe.wait(e, f"{a}pv")
                    _, V, s = CHAIN[a]
                    for g in range(G):
                        o = g * HD
                        dve.link(e, f"{a}{'o'}{g}", nc.vector.tensor_tensor(OT[o:o + HD, br, :, where, :].rearrange("p r b t -> p r (b t)"),
                                                                         V[o:o + HD, 256 + g * 32:256 + (g + 1) * 32].rearrange("p (r t) -> p r t", r=R),
                                                                         sm[o:o + HD, s, 3, g * 32:(g + 1) * 32].rearrange("p (r t) -> p r t", r=R), ALU.mult))

                if compress:
                    dve.done(e, "qp", nc.vector.tensor_copy(QB[:, 0, :], QBD[:, 0, after(1), :].rearrange("p b c -> p (b c)")))
                if attend:
                    dve.done(e, "qb", nc.vector.tensor_copy(QB[:, 1, :], QBD[:, 1, here(1), :].rearrange("p b c -> p (b c)")))
                    dve.done(e, "kn", nc.vector.tensor_copy(KN[:, :, 0:NT], KNT[:, :, here(NT)]))
                Rr(0, 10)
                if attend:
                    pe.wait(e, "w4")
                    biggest('w', B4[:, 2:7, :])
                Rr(10, 12)
                if attend:
                    to_row('w')
                Rr(12, 14)
                if attend:
                    shift('w', B4[:, 2:7, :], 2, 5)
                    dve.done(e, "S4", nc.vector.tensor_copy(PB[:, SEL + 2 * GT, :], B4[:, 7, :]))
                Rr(14, 16)
                if attend:
                    sums('w', 2, 5)
                    inverse('w')
                    outs('w', 2, here(1))
                    S = PB[:, SEL:SEL + NKEYG, :]
                    act.wait(e, "S3")
                    biggest('s', S)
                    to_row('s')
                    shift('s', S, SEL, NKEYG)
                    sums('s', SEL, NKEYG)
                if compress:
                    cp.keep(e, dve, pe, 0)
                    pe.wait(e, "c4")
                    C = bk(0, 8)[:, 0:2, :]
                    biggest('c', C)
                    to_row('c')
                    shift('c', C, 0, 2)
                if attend:
                    inverse('s')
                if compress:
                    sums('c', 0, 2)
                    inverse('c')
                    dve.link(e, "pn", nc.vector.tensor_tensor(PR[:, 0, :, :], PB[:, 0:2, :], b_(sm[:, 1, 3, :], 1, [P, 2, COLS]), ALU.mult))
                    for c in range(2):
                        dve.done(e, f"pr{c}", nc.vector.tensor_reduce(PR[:, 1, c, 0:16].rearrange("p (g t) -> p g t", g=G),
                                                                       PR[:, 0, c, :].rearrange("p (g r t) -> p g t r", g=G, r=R), AX.X, ALU.add))
                    pe.wait(e, "sc")
                    dve.link(e, "sf", nc.vector.tensor_tensor(top[:, 0, 0:NBLK], bk(7)[0:16, 320:320 + NBLK], cf('force')[0:16, :], ALU.add))
                    dve.link(e, "t1", nc.vector.max(t8[:, 0, :], top[:, 0, 0:NBLK]))
                    dve.link(e, "r1", nc.vector.match_replace(top[:, 1, 0:NBLK], t8[:, 0, :], top[:, 0, 0:NBLK], -1.0))
                    dve.link(e, "t2", nc.vector.max(t8[:, 1, :], top[:, 1, 0:NBLK]))
                    dve.link(e, "r2", nc.vector.match_replace(top[:, 2, 0:NBLK], t8[:, 1, :], top[:, 1, 0:NBLK], -1.0))
                    dve.link(e, "bi", nc.vector.tensor_scalar(top[:, 1, 0:NBLK], top[:, 2, 0:NBLK], -0.5, NEG, ALU.is_gt, ALU.mult))
                if compress:
                    pe.wait(e, "scT")
                    dve.link(e, "bt", nc.vector.tensor_copy(BT[:, :].rearrange("p (g r t) -> p g r t", g=G, r=R),
                                                             bk(7)[0:HD, 400:416].rearrange("p (g t) -> p g t", g=G).unsqueeze(2).broadcast_to([HD, G, R, NT])))
                    cp.keep(e, dve, pe, 1)
                if attend:
                    outs('s', 1, here(1))
                if compress:
                    outs('c', 0, after(1))

    step(-1, False, True)
    with nc.Fori(0, NB - 1) as b:
        step(b, True, True)
    step(NB - 1, True, False)

    with stage([]) as (block, _):
        @block.sync
        def _(e):
            for s in pc_rows[0] + pc_rows[1]:
                e.wait_ge(s, 16 * (2 * NB + 1))
            for s in sel_rows[0] + sel_rows[1]:
                e.wait_ge(s, 32 * NB)
    nc.gpsimd.dma_reset()
    for s in pc_rows[0] + pc_rows[1] + sel_rows[0] + sel_rows[1]:
        nc.gpsimd.sem_clear(s)
    nc.all_engine_barrier()

    NO = sb(scope, "NOs", [64, 3, 512])
    with stage(["dve_s", "pe_s"]) as (block, (dve_s, pe_s)):
        dve = Steps(dve_s, ["m0", "m1", "a1", "m2", "a2", "mix"])
        pe = Steps(pe_s, ["t0", "t1", "t2"])

        @block.tensor
        def _(e):
            for i in range(3):
                for r in range(R):
                    mm = nc.tensor.transpose(bk(i, 4)[0:64, r, :], OT[:, i, r, :, :].rearrange("p b t -> p (b t)"), ident)
                pe.done(e, f"t{i}", mm)

        @block.vector
        def _(e):
            for i in range(3):
                pe.wait(e, f"t{i}")
                dve.link(e, f"m{i}", nc.vector.tensor_tensor(
                    NO[:, i, :].rearrange("p (g r d) -> p g r d", g=G, r=R), bk(i)[0:64, :].rearrange("p (r g d) -> p g r d", r=R, g=G),
                    US[0:64, NGATE + i * NH:NGATE + (i + 1) * NH].rearrange("p (g r) -> p g r", g=G).unsqueeze(3).broadcast_to([64, G, R, HD]), ALU.mult))
                if i:
                    dve.link(e, f"a{i}", nc.vector.tensor_tensor(NO[:, 0, :], NO[:, 0, :], NO[:, i, :], ALU.add))
            dve.link(e, "mix", nc.vector.tensor_tensor(MIX[0:64, 4, 256:768], NO[:, 0, :], US[0:64, NG:NG + 512], ALU.mult))


def out_project(nc, A, l, scope, sb, stage, v):
    X, MIX, ident, bk = v['X'], v['MIX'], v['ident'], v['bk']
    mT = sb(scope, "mT", [P, KD, 4 * P + 64])
    W = sb(scope, "Wo", [P, KD, D])
    YO = sb(scope, "YO", [P, 2, D])
    sq = sb(scope, "sq", [P, D])
    ss = sb(scope, "ss", [P, NTILE])
    gpost = sb(scope, "gpost", [P, D])
    with stage(["w_half", "gain", "act_s", "dve_s", "pe_s"]) as (block, (w_half, gain, act_s, dve_s, pe_s)):
        pe = Steps(pe_s, [f"T{t}" for t in range(NTILE)] + [f"{x}{t}" for t in range(NTILE) for x in ("y0", "y1")])
        dve = Steps(dve_s, [f"{x}{t}" for t in range(NTILE) for x in ("m0", "m1")] + [f"{x}{t}" for t in range(NTILE) for x in ("rc", "g", "x")])
        act = Steps(act_s, [f"{x}{t}" for t in range(NTILE) for x in ("c0", "c1", "sq", "rt")])

        @block.sync
        def _(e):
            e.dma_start(gpost[:, :], A['norm_post'][l].partition_broadcast(P)).then_inc(gain, 16)
            wv = A['w_out'][l].rearrange("(k p) c -> p k c", p=P)
            for h in range(2):
                e.dma_start(W[:, :, h * 512:(h + 1) * 512], wv[:, :, h * 512:(h + 1) * 512]).then_inc(w_half, 16)

        @block.tensor
        def _(e):
            for t in range(NTILE):
                n = ROWS[t]
                if t >= 2:
                    dve.wait(e, f"m1{t-2}")
                for k in range(KD):
                    mm = nc.tensor.transpose(bk(2 * (t % 2) + k // 4, 4)[:, k % 4, 0:n], MIX[0:n, t, k * P:(k + 1) * P], ident[0:n, 0:n])
                pe.done(e, f"T{t}", mm)
            e.wait_ge(w_half, 32)
            for t in range(NTILE):
                n = ROWS[t]
                dve.wait(e, f"m1{t}")
                if t >= 2:
                    act.wait(e, f"c1{t-2}")
                for h in range(2):
                    for k in range(KD):
                        mm = nc.tensor.matmul(bk(4 + 2 * (t % 2) + h)[0:n, :], mT[:, k, t * P:t * P + n], W[:, k, h * 512:(h + 1) * 512],
                                              start=(k == 0), stop=(k == KD - 1))
                    pe.done(e, f"y{h}{t}", mm)

        @block.scalar
        def _(e):
            for t in range(NTILE):
                n = ROWS[t]
                if t >= 2:
                    dve.wait(e, f"x{t-2}")
                for h in range(2):
                    pe.wait(e, f"y{h}{t}")
                    act.link(e, f"c{h}{t}", nc.scalar.activation(YO[0:n, t % 2, h * 512:(h + 1) * 512], bk(4 + 2 * (t % 2) + h)[0:n, :], ACT.Copy))
                act.link(e, f"sq{t}", nc.scalar.activation(sq[0:n, :], YO[0:n, t % 2, :], ACT.Square, accum_out=ss[0:n, t:t + 1]))
                act.link(e, f"rt{t}", nc.scalar.activation(ss[0:n, t:t + 1], ss[0:n, t:t + 1], ACT.Sqrt, scale=1.0 / D, bias=v['eps'][0:n, :]))

        @block.vector
        def _(e):
            for t in range(NTILE):
                n = ROWS[t]
                pe.wait(e, f"T{t}")
                for h in range(2):
                    dve.done(e, f"m{h}{t}", nc.vector.tensor_copy(mT[:, 4 * h:4 * h + 4, t * P:t * P + n], bk(2 * (t % 2) + h, 4)[:, :, 0:n]))
            e.wait_ge(gain, 16)
            for t in range(NTILE):
                n = ROWS[t]
                y = YO[0:n, t % 2, :]
                act.wait(e, f"rt{t}")
                dve.link(e, f"rc{t}", nc.vector.reciprocal(ss[0:n, t:t + 1], ss[0:n, t:t + 1]))
                dve.link(e, f"g{t}", nc.vector.scalar_tensor_tensor(y, y, ss[0:n, t:t + 1], gpost[0:n, :], ALU.mult, ALU.mult))
                dve.link(e, f"x{t}", nc.vector.tensor_tensor(X[0:n, t, :], X[0:n, t, :], y, ALU.add))



INPUTS = ['x_prompt', 'x_sample', 'cache_nsa_kv', 'page_table', 'state_nsa_win', 'state_ret', 'state_gdn', 'state_gdn_conv',
          'w_in', 'w_out', 'norm_pre', 'norm_post', 'ret_gn', 'gdn_norm', 'gdn_conv', 'gdn_a_log', 'gdn_dt_bias',
          'cmp_w1', 'cmp_b1', 'cmp_w2']
OUTPUTS = [('y_prompt', (1, SEQ, D)), ('y_sample', (NB, NT, D)),
           ('kv_prompt', (DEPTH, 1, SEQ, 4, G, HD)), ('kv_sample', (DEPTH, NB, NT, 4, G, HD)),
           ('win_prompt', (DEPTH, 1, WIN, 2, G, HD)), ('win_sample', (DEPTH, NB, WIN, 2, G, HD)),
           ('ret_prompt', (DEPTH, 1, H4, HD, HD)), ('ret_sample', (DEPTH, NB, H4, HD, HD)),
           ('gdn_prompt', (DEPTH, 1, H4, HD, HD)), ('gdn_sample', (DEPTH, NB, H4, HD, HD)),
           ('conv_prompt', (DEPTH, 1, CONV - 1, CW)), ('conv_sample', (DEPTH, NB, CONV - 1, CW))]
SCRATCH = [('conv_p', (SEQ + 3, CW)), ('conv_s', (NB, NT + 3, CW)), ('q_rot', (SEQ, 1024)), ('new_kv', (NB, NT, CW))]


def kernel(**inputs):
    import ml_dtypes
    import concourse.bacc as bacc
    from concourse.bass_utils import run_bass_kernel_spmd

    nc = bacc.Bacc("TRN2", target_bir_lowering=False, num_devices=1)
    arrays = {n: np.ascontiguousarray(inputs[n]) for n in INPUTS}
    c = constants()
    arrays['cf'] = np.concatenate([c[n] for n in KEPT], 1)
    arrays['ce'] = np.concatenate([a for n, a in c.items() if n not in KEPT], 1)
    arrays['cb'] = np.concatenate(list(bf_constants().values()), 1).astype(ml_dtypes.bfloat16)
    A = {n: nc.dram_tensor(f"in_{n}", a.shape, mybir.dt.from_np(a.dtype), kind="ExternalInput").ap() for n, a in arrays.items()}
    O = {n: nc.dram_tensor(f"out_{n}", s, F32, kind="ExternalOutput").ap() for n, s in OUTPUTS}
    for n, s in SCRATCH:
        A[n] = nc.dram_tensor(f"scratch_{n}", s, F32, kind="Internal").ap()
    build(nc, A, O)
    r = run_bass_kernel_spmd(nc, [{f"in_{n}": a for n, a in arrays.items()}], core_ids=[0])
    return tuple(r.results[0][f"out_{n}"] for n, _ in OUTPUTS)
```

```python
import concourse.bass as bass
from concourse import mybir
from contextlib import ExitStack, contextmanager
import numpy as np

F32 = mybir.dt.float32
BF16 = mybir.dt.bfloat16
I32 = mybir.dt.int32
ALU = mybir.AluOpType
ACT = mybir.ActivationFunctionType
AX = mybir.AxisListType

D = 1024
SEQ = 512
DEPTH = 2
NB, NT = 8, 8
PAST = 4096
HD = 64
H4 = 4
NH, G, R = 8, 2, 4
WIN = 512
P = 128
KD = D // P
NTILE = 5
ROWS = [P, P, P, P, NB * NT]
CONV = 4
CW = 768
EPS = 1e-6
NEG = -1e30
SCALE = HD ** -0.5
RQ, RK, RV, RG = 0, 256, 512, 768
NQ, NKV, NGATE, NG = 1024, 1536, 2304, 2328
GQKV, GB, GA, GG = 2840, 3608, 3612, 3616
PROJ = 3872
SEL_BLOCK = 64
NBLK = PAST // SEL_BLOCK + 1
PAIRS = 2
GT = PAST // (P * PAIRS)
SEG = 16
NSEG = PAST // SEG
NSEGP = SEQ // SEG
NCP = NSEGP - 1
COLS = NH * NT
NKEYG = 2 * GT + 1



def constants():
    c = {}
    i = np.arange(P)
    c['ident'] = np.eye(P)
    half = HD // 2
    inv = (np.float32(10000.0) ** (-np.arange(half, dtype=np.float32) / np.float32(half))).astype(np.float32)
    pos = np.zeros((P, NTILE), np.float32)
    for t in range(4):
        pos[:, t] = t * P + i
    pos[:, 4] = PAST + i % NT
    ang = (pos[:, :, None] * inv[None, None, :]).astype(np.float32).astype(np.float64)
    c['cos'] = np.cos(ang)
    c['sin'] = np.sin(ang)
    blk = [np.ones((P, P)), np.zeros((P, P))]
    j = i[:, None]
    k = i[None, :]
    blk[1][:64, :64] = (j[:64] // NT == k[:, :64] // NT)
    c['same'] = np.stack(blk, 1)
    c['tri'] = np.stack([b * (j <= k) for b in blk], 1)
    c['neg'] = (1 - c['tri']) * NEG
    lev = np.zeros((P, 7, P))
    for s in range(7):
        w = 1 << s
        lev[:, s] = (j // (2 * w) == k // (2 * w)) & (j % (2 * w) < w) & (k % (2 * w) >= w)
    c['level'] = lev
    c['pair'] = (j // HD == k // HD).astype(np.float64)
    lg = np.log1p(-np.exp2(-5.0 - np.arange(H4)))
    rel = (k - j).astype(np.float64)
    for n, b in enumerate(blk):
        c[f'dm{n}'] = np.stack([np.where(b * (j <= k) > 0, np.exp(np.maximum(rel, 0) * g), 0) * SCALE for g in lg], 1)
    step = [i, i % NT]
    last = [P, NT]
    c['qdec'] = np.stack([np.exp((s[:, None] + 1) * lg[None]) for s in step], 1)
    c['kdec'] = np.stack([np.exp((n - 1 - s[:, None]) * lg[None]) * SCALE for s, n in zip(step, last)], 1)
    sd = np.zeros((P, 2, 2))
    for n in range(2):
        for hp in range(2):
            sd[:, n, hp] = np.exp(last[n] * lg[2 * hp + i // HD])
    c['sdec'] = sd
    own = np.zeros((P, NB, 64))
    for b in range(NB):
        own[:, b] = (np.arange(64)[None] // NT == b)
    c['own'] = own
    c['ownrow'] = (i[:, None] // NT == np.arange(NB)[None, :])
    ci = (np.arange(2 * P) * SEG)[:, None]
    sj = (np.arange(NBLK) * SEL_BLOCK)[None, :]
    ov = ((ci < sj + SEL_BLOCK) & (ci + 2 * SEG > sj)).astype(np.float64)
    ov[255] = 0
    c['overlap'] = np.stack([ov[:P], ov[P:]], 1)
    force = np.zeros((P, NBLK))
    force[:, [0, NBLK - 2, NBLK - 1]] = -NEG
    c['force'] = force
    return {n: np.ascontiguousarray(a, np.float32).reshape(P, -1) for n, a in c.items()}


def bf_constants():
    c = {}
    i = np.arange(P)
    c['identb'] = np.eye(P)
    c['causal'] = np.where(i[None] <= i[:, None], 0, NEG)
    cm = np.zeros((P, 4, 32))
    for t in range(4):
        cm[:, t] = np.where((np.arange(32) * SEG + 2 * SEG - 1)[None] <= (t * P + i)[:, None], 0, NEG)
    c['cmask'] = cm
    be = np.zeros((P, GT, P))
    for t in range(GT):
        be[:, t] = (i[:, None] == 4 * t + i[None] // 32)
    c['blockof'] = be
    stepc = (np.arange(COLS) % NT)[None]
    c['newmask'] = np.where(i[:, None] <= stepc, 0, NEG)
    c['winmask'] = np.where(i[:, None] > stepc, 0, NEG)
    c['padmask'] = np.where(i[:, None] < P - 1, 0, NEG) + 0 * stepc
    return {n: np.ascontiguousarray(a, np.float32).reshape(P, -1) for n, a in c.items()}


KEPT = ('ident', 'overlap', 'force')


def layout(c):
    at, out = 0, {}
    for n, a in c.items():
        out[n] = (at, a.shape[1])
        at += a.shape[1]
    return out, at



class Steps:

    def __init__(self, sem, names):
        self.sem, self.names, self.at = sem, list(names), {n: i + 1 for i, n in enumerate(names)}
        assert len(self.at) == len(self.names)
        self.next = 0

    def done(self, eng, name, ins):
        assert self.next < len(self.names) and self.names[self.next] == name, (name, self.names[self.next:self.next + 2])
        self.next += 1
        return ins.then_inc(self.sem, 1)

    def link(self, eng, name, ins):
        self.done(eng, name, ins)
        eng.wait_ge(self.sem, self.next)

    def wait(self, eng, name):
        eng.wait_ge(self.sem, self.at[name])


def b_(ap, axis, shape):
    return ap.unsqueeze(axis).broadcast_to(shape)


def build(nc, A, O):
    es = ExitStack()

    used = []

    def sb(scope, name, shape, dt=F32):
        used.append(name)
        name = name if used.count(name) == 1 else f"{name}_{used.count(name)}"
        return scope.enter_context(nc.sbuf_tensor(name, shape, dt))

    @contextmanager
    def stage(sems):
        with ExitStack() as st:
            got = [st.enter_context(nc.semaphore(n)) for n in sems]
            with nc.Block() as block:
                yield block, got
            for s in got:
                nc.gpsimd.sem_clear(s)
            nc.all_engine_barrier()

    every = constants()
    cl, cn = layout({n: every[n] for n in KEPT})
    el, en = layout({n: a for n, a in every.items() if n not in KEPT})
    bl, bn = layout(bf_constants())

    with es:
        X = sb(es, "X", [P, NTILE, D])
        MIX = sb(es, "MIX", [P, NTILE, D])
        CF = sb(es, "CF", [P, cn])
        CB = sb(es, "CB", [P, bn], BF16)
        US = sb(es, "US", [P, PROJ])
        QRS = sb(es, "QRS", [P, 2, NH * HD])
        ones = sb(es, "ones", [P, P])
        W1 = sb(es, "W1", [P, 2, SEG // PAIRS, P])
        W2 = sb(es, "W2", [HD, 2, G, P])
        B1 = sb(es, "B1", [HD, 2])
        eps = sb(es, "eps", [P, 1])

        def cf(n, shape=None):
            o, w = cl[n] if n in cl else el[n]
            ap = (CF if n in cl else v['CE'])[:, o:o + w]
            if shape:
                ap = ap.rearrange("p (a b) -> p a b", b=shape)
            return ap

        def cb(n, shape=None):
            o, w = bl[n]
            ap = CB[:, o:o + w]
            if shape:
                ap = ap.rearrange("p (a b) -> p a b", b=shape)
            return ap

        ident = cf('ident')
        bank = [es.enter_context(nc.psum_tensor(f"bank{i}", [P, 512], F32)) for i in range(8)]

        def bk(i, a=None):
            ap = bank[i][:, :]
            return ap if a is None else ap.rearrange("p (a b) -> p a b", a=a)

        with stage(["loaded", "filled"]) as (block, (loaded, filled)):
            @block.sync
            def _(sp):
                sp.dma_start(CF[:, :], A['cf']).then_inc(loaded, 16)
                sp.dma_start(CB[:, :], A['cb']).then_inc(loaded, 16)
                sp.dma_start(X[:, 0:4, :], A['x_prompt'][0].rearrange("(t p) d -> p t d", p=P)).then_inc(loaded, 16)
                sp.dma_start(X[0:64, 4, :], A['x_sample'].rearrange("b t d -> (b t) d")).then_inc(loaded, 16)
                sp.wait_ge(loaded, 64)

            @block.vector
            def _(dve):
                nc.vector.memset(ones[:, :], 1.0).then_inc(filled, 1)
                nc.vector.memset(eps[:, :], EPS).then_inc(filled, 1)
                dve.wait_ge(filled, 2)

        REGS = [[e.alloc_register(f"page{k}") for k in range(24)] for e in (nc.sync, nc.gpsimd)]
        with nc.Fori(0, DEPTH) as l:
            v = dict(X=X, MIX=MIX, US=US, QRS=QRS, ones=ones, eps=eps, cf=cf, cb=cb, ident=ident, bk=bk, nc=nc, W1=W1, W2=W2, B1=B1,
                     early_columns=en, REGS=REGS)
            layer(nc, A, O, l, sb, stage, v)

        with stage(["written"]) as (block, (written,)):
            @block.sync
            def _(sp):
                sp.dma_start(O['y_prompt'][0].rearrange("(t p) d -> p t d", p=P), X[:, 0:4, :]).then_inc(written, 16)
                sp.dma_start(O['y_sample'].rearrange("b t d -> (b t) d"), X[0:64, 4, :]).then_inc(written, 16)
                sp.wait_ge(written, 32)


def layer(nc, A, O, l, sb, stage, v):
    with ExitStack() as scope:
        UP = sb(scope, "UP", [P, 4, PROJ])
        v['CE'] = sb(scope, "CE", [P, v['early_columns']])
        U = [UP[:, t, :] for t in range(4)] + [v['US'][0:64, :]]
        with ExitStack() as s2:
            Y = [u[:, GQKV:GQKV + CW] for u in U]
            g_log = sb(s2, "g_log", [P, NTILE, H4])
            with ExitStack() as s3:
                project(nc, A, O, l, s3, sb, stage, v, U, Y, g_log)
            with ExitStack() as s3:
                retention(nc, A, O, l, s3, sb, stage, v, U)
            with ExitStack() as s3:
                delta(nc, A, O, l, s3, sb, stage, v, U, Y, g_log)
        with ExitStack() as s2:
            prompt_attention(nc, A, O, l, s2, sb, stage, v, U)
    with ExitStack() as scope:
        sample_attention(nc, A, O, l, scope, sb, stage, v)
    with ExitStack() as scope:
        out_project(nc, A, l, scope, sb, stage, v)


def project(nc, A, O, l, scope, sb, stage, v, U, Y, g_log):
    X, ident, bk, MIX = v['X'], v['ident'], v['bk'], v['MIX']
    chunks = [(2840, 3352), (3352, 3608), (3608, 3872), (1536, 2048), (2048, 2560), (2560, 2840), (1024, 1536), (0, 512), (512, 1024)]
    C_RAW, C_GATES, C_KV, C_NG, C_NQ, C_RQK, C_RG = 1, 2, 4, 5, 6, 7, 8
    assert sum(b - a for a, b in chunks) == PROJ
    NC, RING = len(chunks), 4
    hT = sb(scope, "hT", [P, KD, 4 * P + 64])
    W = sb(scope, "W", [P, RING, 2, 512])
    ss = sb(scope, "ss", [P, NTILE])
    gpre = sb(scope, "gpre", [P, KD])
    XS = sb(scope, "XS", [P, CONV - 1, CW])
    QR = sb(scope, "QR", [P, 2, 512])
    alog = sb(scope, "alog", [P, H4])
    dtb = sb(scope, "dtb", [P, H4])
    sp_ = sb(scope, "sp_", [P, 3, NTILE, H4])
    nrm = sb(scope, "nrm", [P, NTILE, 8])
    zero = sb(scope, "zero", [CONV - 1, CW])
    xn = MIX[:, 3:5, :]
    cw = MIX[:, 0:3, :].rearrange("p a c -> p (a c)").rearrange("p (k c) -> p k c", k=CONV)
    ta, tb = MIX[:, 3, 0:CW], MIX[:, 4, 0:CW]
    cos, sin = v['cf']('cos', 32), v['cf']('sin', 32)
    XP, XC = A['conv_p'], A['conv_s']
    every = range(NTILE)
    conv = lambda t: [f"{x}{t}" for x in ("c0", "c1", "c1a", "c2", "c2a", "c3", "c3a")]
    rope_n = lambda r, t: [f"{r}{x}{t}" for x in "ab12"]
    with stage(["gain", "act_s", "dve_s", "pe_s", "w_used", "proj_done", "e_act", "e_dve", "par", "raw", "shift", "rot", "outs"] +
               [f"w{i}" for i in range(RING)]) as \
            (block, (gain, act_s, dve_s, pe_s, w_used, proj_done, e_act, e_dve, par, raw, shift, rot, outs, *wsem)):
        act = Steps(act_s, [f"{n}{t}" for t in every for n in ("sq", "rt")] + ["al"] + [f"gg{t}" for t in every] + [f"bt{t}" for t in every] +
                    ["ab", "ex", "ln"] + [f"ys{t}" for t in every] + [f"gt{t}" for t in every] + [f"ng{t}" for t in every] + ["sq"] +
                    [f"rg{t}" for t in every])
        dve = Steps(dve_s, ["zero", "z1", "z2"] + [f"{n}{t}" for t in every for n in ("rs", "xn", "h0", "h1")] + ["al"] + [f"a1{t}" for t in every] +
                    ["mx"] + conv(0) + ["sg", "gl"] + sum([conv(t) for t in range(1, 5)], []) + sum([rope_n("kv", t) for t in every], []) +
                    [f"{n}{t}" for t in every for n in ("s2", "ss")] + ["rc", "q8"] + [f"nm{t}" for t in every] +
                    sum([rope_n("nq", t) + [f"nqc{t}"] for t in every], []) + sum([rope_n("rq", t) for t in every], []))
        pe = Steps(pe_s, [f"T{t}" for t in every])
        wv = A['w_in'][l].rearrange("(k p) c -> p k c", p=P)

        def have(e, c, t):
            u = c * NTILE + t
            e.wait_ge(e_dve if u % 2 else e_act, u // 2 + 1)

        def copies(e, c, engine):
            for t in every:
                u = c * NTILE + t
                if u % 2 == engine:
                    a, b = chunks[c]
                    e.wait_ge(proj_done, u + 1)
                    o, i = U[t][:, a:b], bk(u % 8)[0:ROWS[t], 0:b - a]
                    if engine:
                        nc.vector.tensor_copy(o, i).then_inc(e_dve, 1)
                    else:
                        nc.scalar.activation(o, i, ACT.Copy).then_inc(e_act, 1)

        @block.sync
        def _(e):
            def weights(c, j):
                a, b = chunks[c]
                if c == 1 or c and j == RING - 1:
                    e.wait_ge(proj_done, c * NTILE)
                elif c:
                    e.wait_ge(w_used, (c - 2) * (RING - 1) + j + 1)
                e.dma_start(W[:, j, :, 0:b - a], wv[:, 2 * j:2 * j + 2, a:b]).then_inc(wsem[j], 16)

            def shifted(t):
                if t:
                    dve.wait(e, f"c3a{t-1}")
                for k in range(1, 4):
                    src = XP[3 - k + t * P:3 - k + (t + 1) * P, :] if t < 4 else XC[:, 3 - k:3 - k + NT, :]
                    e.dma_start(XS[0:ROWS[t], k - 1, :], src).then_inc(shift, 16)

            def kv_out(t):
                dve.wait(e, f"kv2{t}")
                if t < 4:
                    kvo = O['kv_prompt'][l, 0].rearrange("s a g d -> s (a g d)")[t * P:(t + 1) * P]
                    wno = O['win_prompt'][l, 0].rearrange("s a g d -> s (a g d)")[t * P:(t + 1) * P]
                else:
                    kvo = O['kv_sample'][l].rearrange("b s a g d -> (b s) (a g d)")
                    wno = O['win_sample'][l].rearrange("b s a g d -> b s (a g d)")[:, WIN - NT:WIN, :]
                e.dma_start(kvo, U[t][:, NKV:NKV + 512]).then_inc(outs, 16)
                e.dma_start(wno, U[t][:, NKV + 512:NKV + 768]).then_inc(outs, 16)

            e.dma_start(gpre[:, :], A['norm_pre'][l].rearrange("(k p) -> p k", p=P), allow_slow_non_contiguous=True).then_inc(gain, 16)
            for j in range(RING):
                weights(0, j)
            e.dma_start(v['CE'][:, :], A['ce']).then_inc(par, 16)
            e.dma_start(cw.rearrange("p a b -> p (a b)"), A['gdn_conv'][l].rearrange("a b -> (a b)").partition_broadcast(P)).then_inc(par, 16)
            e.dma_start(alog[:, :], A['gdn_a_log'][l].partition_broadcast(P)).then_inc(par, 16)
            e.dma_start(dtb[:, :], A['gdn_dt_bias'][l].partition_broadcast(P)).then_inc(par, 16)
            for c in (1, 2):
                for j in range(RING):
                    weights(c, j)
            dve.wait(e, "zero")
            e.dma_start(XP[0:3, :], zero[:, :]).then_inc(raw, 16)
            for t in every:
                have(e, C_RAW - 1, t)
                have(e, C_RAW, t)
                e.dma_start(XP[3 + t * P:3 + (t + 1) * P, :] if t < 4 else XC[:, 3:3 + NT, :], U[t][:, GQKV:GQKV + CW]).then_inc(raw, 16)
            e.dma_start(XC[:, 0:3, :], A['state_gdn_conv'][l]).then_inc(raw, 16)
            for j in range(RING):
                weights(3, j)
            e.wait_ge(raw, 7 * 16)
            shifted(0)
            for j in range(RING):
                weights(4, j)
                if j < 3:
                    shifted(j + 1)
            weights(5, 0)
            shifted(4)
            for j in range(1, RING):
                weights(5, j)
            e.dma_start(O['conv_prompt'][l, 0], XP[SEQ:SEQ + 3, :]).then_inc(outs, 16)
            e.dma_start(O['conv_sample'][l], XC[:, NT:NT + 3, :]).then_inc(outs, 16)
            e.dma_start(O['win_sample'][l].rearrange("b s a g d -> b s (a g d)")[:, 0:WIN - NT, :],
                        A['state_nsa_win'][l].rearrange("b s a g d -> b s (a g d)")[:, NT:WIN, :]).then_inc(outs, 16)
            for j in range(RING):
                weights(6, j)
            for j in range(RING):
                weights(7, j)
                kv_out(j)
            kv_out(4)
            for j in range(RING):
                weights(8, j)
                dve.wait(e, f"nqc{j}")
                e.dma_start(A['q_rot'][j * P:(j + 1) * P, :], QR[:, :, :].rearrange("p i c -> p (i c)")).then_inc(rot, 16)
            e.wait_ge(outs, 16 * (3 + 2 * NTILE))
            e.wait_ge(rot, 64)

        @block.scalar
        def _(e):
            for t in every:
                n = ROWS[t]
                x = xn[0:n, t % 2, :]
                if t >= 2:
                    pe.wait(e, f"T{t-2}")
                act.link(e, f"sq{t}", nc.scalar.activation(x, X[0:n, t, :], ACT.Square, accum_out=ss[0:n, t:t + 1]))
                act.link(e, f"rt{t}", nc.scalar.activation(ss[0:n, t:t + 1], ss[0:n, t:t + 1], ACT.Sqrt, scale=1.0 / D, bias=v['eps'][0:n, :]))
            e.wait_ge(par, 64)
            act.done(e, "al", nc.scalar.activation(alog[:, :], alog[:, :], ACT.Exp))

            def gate(name, c, a, w, f):
                for t in every:
                    have(e, c, t)
                    act.done(e, f"{name}{t}", nc.scalar.activation(U[t][:, a:a + w], U[t][:, a:a + w], f))

            def conv_silu(t):
                dve.wait(e, f"c3a{t}")
                act.done(e, f"ys{t}", nc.scalar.activation(Y[t], Y[t], ACT.Silu))

            for c in range(3):
                copies(e, c, 0)
            gate("gg", C_GATES, GG, 256, ACT.Silu)
            gate("bt", C_GATES, GB, H4, ACT.Sigmoid)
            dve.wait(e, "mx")
            act.link(e, "ab", nc.scalar.activation(sp_[:, 1, :, :], sp_[:, 0, :, :], ACT.Abs))
            act.link(e, "ex", nc.scalar.activation(sp_[:, 1, :, :], sp_[:, 1, :, :], ACT.Exp, scale=-1.0))
            act.done(e, "ln", nc.scalar.activation(sp_[:, 1, :, :], sp_[:, 1, :, :], ACT.Ln, bias=1.0))
            for t in range(3):
                conv_silu(t)
            copies(e, 3, 0)
            conv_silu(3)
            conv_silu(4)
            copies(e, 4, 0)
            gate("gt", C_KV, NGATE, 24, ACT.Sigmoid)
            copies(e, 5, 0)
            gate("ng", C_NG, NG, 512, ACT.Silu)
            dve.wait(e, "ss4")
            act.done(e, "sq", nc.scalar.activation(nrm[:, :, :], nrm[:, :, :], ACT.Sqrt, bias=v['eps'][:, :]))
            for c in range(6, NC):
                copies(e, c, 0)
            gate("rg", C_RG, RG, 256, ACT.Silu)

        @block.vector
        def _(e):
            dve.link(e, "zero", nc.vector.memset(zero[:, :], 0.0))
            dve.done(e, "z1", nc.vector.memset(sp_[:, :, :, :], 0.0))
            dve.link(e, "z2", nc.vector.memset(nrm[:, :, :], 1.0))
            e.wait_ge(gain, 16)
            for t in every:
                n = ROWS[t]
                act.wait(e, f"rt{t}")
                dve.link(e, f"rs{t}", nc.vector.reciprocal(ss[0:n, t:t + 1], ss[0:n, t:t + 1]))
                dve.done(e, f"xn{t}", nc.vector.tensor_scalar(xn[0:n, t % 2, :], X[0:n, t, :], ss[0:n, t:t + 1], None, ALU.mult))
                pe.wait(e, f"T{t}")
                for h in range(2):
                    dve.done(e, f"h{h}{t}", nc.vector.tensor_tensor(hT[:, 4 * h:4 * h + 4, t * P:t * P + n], bk(5 + h, 4)[:, :, 0:n],
                                                                     b_(gpre[:, 4 * h:4 * h + 4], 2, [P, 4, n]), ALU.mult))
            act.wait(e, "al")
            dve.link(e, "al", nc.vector.tensor_scalar(alog[:, :], alog[:, :], -1.0, None, ALU.mult))

            def rope(nm, t, src, dst, s, w):
                n, m = ROWS[t], w // 32
                co, si = cos[0:n, t, :], sin[0:n, t, :]
                A1 = ta[0:n, 0:s * w].rearrange("p (s m c) -> p s m c", s=s, m=m)
                B1 = tb[0:n, 0:s * w].rearrange("p (s m c) -> p s m c", s=s, m=m)
                sv = src.rearrange("p s (m c) -> p s m c", c=32)
                bc = [n, s, m, 32]
                dve.done(e, f"{nm}a{t}", nc.vector.tensor_tensor(A1, sv, co.unsqueeze(1).unsqueeze(1).broadcast_to(bc), ALU.mult))
                dve.link(e, f"{nm}b{t}", nc.vector.tensor_tensor(B1, sv, si.unsqueeze(1).unsqueeze(1).broadcast_to(bc), ALU.mult))
                dve.done(e, f"{nm}1{t}", nc.vector.tensor_tensor(dst[:, :, :, 0:32], A1[:, :, 0::2, :], B1[:, :, 1::2, :], ALU.subtract))
                dve.link(e, f"{nm}2{t}", nc.vector.tensor_tensor(dst[:, :, :, 32:64], A1[:, :, 1::2, :], B1[:, :, 0::2, :], ALU.add))

            def convolve(t):
                n, y = ROWS[t], Y[t]
                e.wait_ge(shift, 48 * (t + 1))
                dve.link(e, f"c0{t}", nc.vector.tensor_tensor(y, y, cw[0:n, 3, :], ALU.mult))
                for k in range(1, 4):
                    dve.link(e, f"c{k}{t}", nc.vector.tensor_tensor(ta[0:n, :], XS[0:n, k - 1, :], cw[0:n, 3 - k, :], ALU.mult))
                    dve.link(e, f"c{k}a{t}", nc.vector.tensor_tensor(y, y, ta[0:n, :], ALU.add))

            for c in range(3):
                copies(e, c, 1)
            for t in every:
                n = ROWS[t]
                have(e, C_GATES, t)
                dve.done(e, f"a1{t}", nc.vector.tensor_tensor(sp_[0:n, 0, t, :], U[t][:, GA:GA + H4], dtb[0:n, :], ALU.add))
            dve.wait(e, "a14")
            dve.done(e, "mx", nc.vector.tensor_scalar(sp_[:, 2, :, :], sp_[:, 0, :, :], 0.0, None, ALU.max))
            convolve(0)
            act.wait(e, "ln")
            dve.link(e, "sg", nc.vector.tensor_tensor(sp_[:, 2, :, :], sp_[:, 2, :, :], sp_[:, 1, :, :], ALU.add))
            dve.done(e, "gl", nc.vector.tensor_tensor(g_log[:, :, :], sp_[:, 2, :, :], b_(alog[:, :], 1, [P, NTILE, H4]), ALU.mult))
            convolve(1)
            convolve(2)
            copies(e, 3, 1)
            convolve(3)
            convolve(4)
            copies(e, 4, 1)
            for t in every:
                have(e, C_KV - 1, t)
                have(e, C_KV, t)
                kv = U[t][:, NKV + 256:NKV + 768].rearrange("p (s w) -> p s w", s=2)[:, :, 0:128]
                rope("kv", t, kv, kv.rearrange("p s (h c) -> p s h c", c=HD), 2, 128)
            copies(e, 5, 1)
            heads = lambda ap: ap.rearrange("p (h c) -> p h c", c=HD)
            for t in every:
                n = ROWS[t]
                act.wait(e, f"ys{t}")
                qk, tq = heads(Y[t][:, 0:512]), heads(ta[0:n, 0:512])
                dve.link(e, f"s2{t}", nc.vector.tensor_tensor(tq, qk, qk, ALU.mult))
                dve.link(e, f"ss{t}", nc.vector.tensor_reduce(nrm[0:n, t, :], tq, AX.X, ALU.add))
            act.wait(e, "sq")
            dve.link(e, "rc", nc.vector.reciprocal(nrm[:, :, :], nrm[:, :, :]))
            dve.link(e, "q8", nc.vector.tensor_scalar(nrm[:, :, 0:4], nrm[:, :, 0:4], SCALE, None, ALU.mult))
            for t in every:
                n, qk = ROWS[t], heads(Y[t][:, 0:512])
                dve.done(e, f"nm{t}", nc.vector.tensor_tensor(qk, qk, b_(nrm[0:n, t, :], 2, [n, 8, HD]), ALU.mult))
            copies(e, 6, 1)
            for t in every:
                n = ROWS[t]
                have(e, C_NQ, t)
                if 0 < t < 4:
                    e.wait_ge(rot, 16 * t)
                q_to = (QR if t < 4 else v['QRS'])[0:n, :, :].rearrange("p i (r g c) -> p i g r c", r=R, g=G)
                qv = U[t][:, NQ:NQ + 512].rearrange("p (g w) -> p g w", g=G)
                rope("nq", t, qv, q_to[:, 1], 2, 256)
                dve.done(e, f"nqc{t}", nc.vector.tensor_copy(q_to[:, 0], qv.rearrange("p g (r c) -> p g r c", r=R)))
            copies(e, 7, 1)
            for t in every:
                have(e, C_RQK, t)
                rqv = U[t][:, RQ:RQ + 512].unsqueeze(1)
                rope("rq", t, rqv, rqv.rearrange("p s (h c) -> p s h c", c=HD), 1, 512)
            copies(e, 8, 1)

        @block.tensor
        def _(e):
            def transpose_rows(t):
                n = ROWS[t]
                dve.wait(e, f"xn{t}")
                if t:
                    dve.wait(e, f"h1{t-1}")
                for k in range(KD):
                    mm = nc.tensor.transpose(bk(5 + k // 4, 4)[:, k % 4, 0:n], xn[0:n, t % 2, k * P:(k + 1) * P], ident[0:n, 0:n])
                pe.done(e, f"T{t}", mm)

            def product(c, t, k):
                a, b = chunks[c]
                return nc.tensor.matmul(bk((c * NTILE + t) % 8)[0:ROWS[t], 0:b - a], hT[:, k, t * P:t * P + ROWS[t]],
                                        W[:, k // 2, k % 2, 0:b - a], start=(k == 0), stop=(k == KD - 1))

            transpose_rows(0)
            for t in every:
                if t + 1 < NTILE:
                    transpose_rows(t + 1)
                dve.wait(e, f"h1{t}")
                for k in range(KD):
                    if t == 0 and k % 2 == 0:
                        e.wait_ge(wsem[k // 2], 16)
                    mm = product(0, t, k)
                    if k == KD - 1:
                        mm.then_inc(proj_done, 1)
            for c in range(1, NC):
                for j in range(RING):
                    e.wait_ge(wsem[j], 16 * (c + 1))
                    for t in every:
                        u = c * NTILE + t
                        if j == 0 and u >= 8:
                            e.wait_ge(e_dve if u % 2 else e_act, (u - 8) // 2 + 1)
                        product(c, t, 2 * j)
                        mm = product(c, t, 2 * j + 1)
                        if j == RING - 1:
                            mm.then_inc(proj_done, 1)
                    if j < RING - 1:
                        mm.then_inc(w_used, 1)


def load_states(e, S, src, loaded, l):
    for h in range(H4):
        hp, o = h // 2, (h % 2) * HD
        e.dma_start(S[o:o + HD, :, hp, o:o + HD], src[l].rearrange("b h d e -> h d b e")[h]).then_inc(loaded, 16)


def retention(nc, A, O, l, scope, sb, stage, v, U):
    TILES = (0, 1, 4, 2, 3)
    ORDER = [("front", 0), ("front", 1)]
    for i in range(NTILE):
        ORDER += [("back", i)] + ([("front", i + 2)] if i + 2 < NTILE else []) + [("norm", i)]
    ORDER = [(what, i, TILES[i]) for what, i in ORDER]
    QK_ = sb(scope, "QK", [P, 2, 4, P])
    ATT_ = sb(scope, "ATT", [P, 2, H4, P])
    KDc_ = sb(scope, "KDc", [P, 2, 256])
    S = sb(scope, "S", [P, 2, P])
    SS = sb(scope, "SS", [P, NB, 2, P])
    QM = sb(scope, "QM", [P, 2, NB, 64])
    VM = sb(scope, "VM", [P, NB, 256])
    T1 = sb(scope, "T1", [P, 512])
    Ot = sb(scope, "Ot", [P, 256])
    st = sb(scope, "st", [P, 4, H4])
    gn = sb(scope, "gn", [P, 256])
    bk, cf, ident, MIX = v['bk'], v['cf'], v['ident'], v['MIX']
    dn = ["z1", "z2"]
    pn = []
    for what, i, t in ORDER:
        if what == "front":
            dn += [f"{x}{t}" for x in ("qk", "att0", "att1", "kd")]
            dn += ["qm0", "qm1", "vm"] if t == 4 else []
            pn += [f"T{t}", f"a{t}"]
        if what == "back":
            dn += [f"{x}{t}" for x in ("sm", "s0", "s1")] if t < 4 else []
            dn += [f"{x}{t}" for x in ("qs", "o")]
            pn += [f"{x}{t}" for x in ("qs", "av", "su")]
        if what == "norm":
            dn += [f"{x}{t}" for x in ("m", "m2", "ce", "sq", "va", "rc", "n1", "n2", "n3")]
            dn += [f"ss{k}{j}" for k in range(4) for j in "ms"] if t == 4 else []
    with stage(["dve_s", "act_s", "pe_s", "loaded", "gl", "outs"]) as (block, (dve_s, act_s, pe_s, loaded, gl, outs)):
        dve = Steps(dve_s, dn)
        act = Steps(act_s, [f"sq{t}" for t in TILES])
        pe = Steps(pe_s, pn)

        @block.sync
        def _(e):
            e.dma_start(gn[:, :], A['ret_gn'][l].partition_broadcast(P)).then_inc(gl, 16)
            dve.wait(e, "z2")
            load_states(e, SS, A['state_ret'], loaded, l)
            dve.wait(e, "ss3s")
            for h in range(H4):
                hp, o = h // 2, (h % 2) * HD
                e.dma_start(O['ret_sample'][l].rearrange("b h d e -> h d b e")[h], SS[o:o + HD, :, hp, o:o + HD]).then_inc(outs, 16)
            dve.wait(e, "s13")
            for h in range(H4):
                hp, o = h // 2, (h % 2) * HD
                e.dma_start(O['ret_prompt'][l, 0, h], S[o:o + HD, hp, o:o + HD]).then_inc(outs, 16)
            e.wait_ge(outs, 2 * H4 * 16)

        @block.scalar
        def _(e):
            for t in TILES:
                dve.wait(e, f"va{t}")
                act.done(e, f"sq{t}", nc.scalar.activation(st[0:ROWS[t], 2, :], st[0:ROWS[t], 2, :], ACT.Sqrt,
                                                           scale=1.0 / HD, bias=v['eps'][0:ROWS[t], :]))

        @block.tensor
        def _(e):
            for what, i, t in ORDER:
                u, n = U[t], ROWS[t]
                QK, ATT, KDc = QK_[:, i % 2], ATT_[:, i % 2], KDc_[:, i % 2]
                if what == "front":
                    if i:
                        dve.wait(e, f"att1{TILES[i-1]}")
                    for c in range(4):
                        mm = nc.tensor.transpose(bk(0, 4)[:, c, 0:n], u[:, c * P:(c + 1) * P], ident[0:n, 0:n])
                    pe.done(e, f"T{t}", mm)
                    dve.wait(e, f"qk{t}")
                    for h in range(H4):
                        o = (h % 2) * HD
                        mm = nc.tensor.matmul(bk(1 - h % 2, 4)[0:n, h // 2, 0:n], QK[o:o + HD, 2 + h // 2, 0:n], QK[o:o + HD, h // 2, 0:n],
                                              start=True, stop=True)
                    pe.done(e, f"a{t}", mm)
                if what != "back":
                    continue
                if i:
                    dve.wait(e, f"o{TILES[i-1]}")
                if t < 4:
                    dve.wait(e, "z1")
                    for hp in range(2):
                        mm = nc.tensor.matmul(bk(2, 4)[0:n, hp, :], QK[:, hp, 0:n], S[:, hp, :], start=True, stop=True)
                else:
                    dve.wait(e, "qm1")
                    e.wait_ge(loaded, H4 * 16)
                    for hp in range(2):
                        for b in range(NB):
                            mm = nc.tensor.matmul(bk(2, 4)[0:n, hp, :], QM[:, hp, b, :], SS[:, b, hp, :],
                                                  start=(b == 0), stop=(b == NB - 1))
                pe.done(e, f"qs{t}", mm)
                dve.wait(e, f"kd{t}" if t < 4 else "vm")
                for h in range(H4):
                    mm = nc.tensor.matmul(bk(3)[0:n, h * HD:(h + 1) * HD], ATT[0:n, h, 0:n], u[:, RV + h * HD:RV + (h + 1) * HD],
                                          start=True, stop=True)
                pe.done(e, f"av{t}", mm)
                if i and TILES[i - 1] == 4:
                    dve.wait(e, "ss0m")
                if t < 4:
                    for hp in range(2):
                        mm = nc.tensor.matmul(bk(4, 4)[:, hp, :], KDc[0:n, hp * P:(hp + 1) * P], u[:, RV + hp * P:RV + (hp + 1) * P],
                                              start=True, stop=True)
                else:
                    for k in range(4):
                        hp, q = divmod(k, 2)
                        mm = nc.tensor.matmul(bk(4 + k), KDc[0:n, hp * P:(hp + 1) * P], VM[0:n, 4 * q:4 * q + 4, hp * P:(hp + 1) * P],
                                              start=True, stop=True)
                pe.done(e, f"su{t}", mm)

        @block.vector
        def _(e):
            dve.link(e, "z1", nc.vector.memset(S[:, :, :], 0.0))
            dve.link(e, "z2", nc.vector.memset(SS[:, :, :, :], 0.0))
            e.wait_ge(gl, 16)
            pair = cf('pair')
            h3 = lambda ap: ap.rearrange("p (h c) -> p h c", c=HD)
            for what, i, t in ORDER:
                u, n, k = U[t], ROWS[t], int(t == 4)
                QK, ATT, KDc = QK_[:, i % 2], ATT_[:, i % 2], KDc_[:, i % 2]
                if what == "front":
                    pe.wait(e, f"T{t}")
                    dve.done(e, f"qk{t}", nc.vector.tensor_copy(QK[:, :, 0:n], bk(0, 4)[:, :, 0:n]))
                    pe.wait(e, f"a{t}")
                    for o in range(2):
                        dve.done(e, f"att{o}{t}", nc.vector.tensor_tensor(ATT[0:n, o::2, 0:n], bk(1 - o, 4)[0:n, 0:2, 0:n],
                                                                           cf(f'dm{k}', P)[0:n, o::2, 0:n], ALU.mult))
                    dve.link(e, f"kd{t}", nc.vector.tensor_tensor(h3(KDc[0:n, :]), h3(u[:, RK:RK + 256]),
                                                                   b_(cf('kdec', 4)[0:n, k, :], 2, [n, H4, HD]), ALU.mult))
                    if t == 4:
                        for hp in range(2):
                            dve.done(e, f"qm{hp}", nc.vector.tensor_tensor(QM[:, hp, :, :], b_(QK[:, hp, 0:64], 1, [P, NB, 64]), cf('own', 64), ALU.mult))
                        dve.done(e, "vm", nc.vector.tensor_tensor(VM[0:n, :, :], b_(u[:, RV:RV + 256], 1, [n, NB, 256]),
                                                                   b_(cf('ownrow')[0:n, :], 2, [n, NB, 256]), ALU.mult))
                    continue
                o3 = h3(Ot[0:n, :])
                if what == "back":
                    pe.wait(e, f"su{t}")
                if what == "back" and t < 4:
                    dve.link(e, f"sm{t}", nc.vector.tensor_tensor(T1[:, 0:256].rearrange("p (a b) -> p a b", a=2), bk(4, 4)[:, 0:2, :],
                                                                   b_(pair, 1, [P, 2, P]), ALU.mult))
                    for hp in range(2):
                        dve.link(e, f"s{hp}{t}", nc.vector.scalar_tensor_tensor(
                            S[:, hp, :], S[:, hp, :], cf('sdec', 2)[:, 0, hp:hp + 1], T1[:, hp * P:(hp + 1) * P], ALU.mult, ALU.add))
                if what == "back":
                    dve.link(e, f"qs{t}", nc.vector.tensor_tensor(h3(T1[0:n, 0:256]), h3(bk(2)[0:n, 0:256]),
                                                                   b_(cf('qdec', 4)[0:n, k, :], 2, [n, H4, HD]), ALU.mult))
                    dve.link(e, f"o{t}", nc.vector.tensor_tensor(Ot[0:n, :], bk(3)[0:n, 0:256], T1[0:n, 0:256], ALU.add))
                    continue
                dve.link(e, f"m{t}", nc.vector.tensor_reduce(st[0:n, 0, :], o3, AX.X, ALU.add))
                dve.link(e, f"m2{t}", nc.vector.tensor_scalar(st[0:n, 1, :], st[0:n, 0, :], 1.0 / HD, None, ALU.mult))
                dve.link(e, f"ce{t}", nc.vector.tensor_tensor(o3, o3, b_(st[0:n, 1, :], 2, [n, H4, HD]), ALU.subtract))
                dve.link(e, f"sq{t}", nc.vector.tensor_tensor(T1[0:n, 0:256], Ot[0:n, :], Ot[0:n, :], ALU.mult))
                dve.link(e, f"va{t}", nc.vector.tensor_reduce(st[0:n, 2, :], h3(T1[0:n, 0:256]), AX.X, ALU.add))
                act.wait(e, f"sq{t}")
                dve.link(e, f"rc{t}", nc.vector.reciprocal(st[0:n, 3, :], st[0:n, 2, :]))
                dve.link(e, f"n1{t}", nc.vector.tensor_tensor(o3, o3, b_(st[0:n, 3, :], 2, [n, H4, HD]), ALU.mult))
                dve.link(e, f"n2{t}", nc.vector.tensor_tensor(Ot[0:n, :], Ot[0:n, :], gn[0:n, :], ALU.mult))
                dve.done(e, f"n3{t}", nc.vector.tensor_tensor(MIX[0:n, t, 0:256], Ot[0:n, :], u[:, RG:RG + 256], ALU.mult))
                if t == 4:
                    for k in range(4):
                        hp, q = divmod(k, 2)
                        t3 = T1[:, :].rearrange("p (a b) -> p a b", a=4)
                        dve.link(e, f"ss{k}m", nc.vector.tensor_tensor(t3, bk(4 + k, 4), b_(pair, 1, [P, 4, P]), ALU.mult))
                        sv = SS[:, 4 * q:4 * q + 4, hp, :]
                        dve.link(e, f"ss{k}s", nc.vector.scalar_tensor_tensor(sv, sv, cf('sdec', 2)[:, 1, hp:hp + 1], t3, ALU.mult, ALU.add))


def delta(nc, A, O, l, scope, sb, stage, v, U, Y, g_log):
    PAIR = [(0, 1), (2, 3), (4,)]
    LEVELS = [7, 7, 3]
    ready = lambda t: [("ready0", t), ("ready1", t)]
    state = lambda t: [("state0", t), ("state1", t), ("state2", t), ("state3", t)]
    beside = [ready(2) + ready(3), state(0) + state(1) + ready(4), state(2) + state(3)]
    ORDER = ready(0) + ready(1)
    for tiles, levels, small in zip(PAIR, LEVELS, beside):
        per = -(-len(small) // levels)
        for s in range(levels):
            ORDER += [("level", (tiles, s, levels))] + small[s * per:(s + 1) * per]
    ORDER += state(4)

    SETS = 4
    QKT_ = sb(scope, "QKT", [P, SETS, 6, P])
    kb = sb(scope, "kb", [P, 256])
    vb_ = sb(scope, "vb", [P, SETS, 256])
    kd_ = sb(scope, "kd", [P, SETS, 256])
    work = sb(scope, "work", [P, 8, H4, P])
    NTs_, M1_, T_ = ([work[:, i + lane, :, :] for lane in range(2)] for i in (0, 2, 4))
    gb, LT = work[:, 6, :, :], work[:, 7, :, :]
    flat = work[:, :, :, :].rearrange("p a h c -> p (a h c)")
    QM = flat[:, 0:2048].rearrange("p (i b c) -> p i b c", i=4, b=NB)
    VM = flat[:, 2048:4096].rearrange("p (b c) -> p b c", b=NB)
    gs_ = sb(scope, "gs", [P, NTILE, 7, H4])
    SL_ = sb(scope, "SL", [P, NTILE, H4, NB])
    SLp = sb(scope, "SLp", [P, 2, NB])
    S = sb(scope, "S", [P, 2, P])
    SS = sb(scope, "SS", [P, NB, 2, P])
    VN = sb(scope, "VN", [P, 256])
    T1 = sb(scope, "T1", [P, 512])
    Ot = sb(scope, "Ot", [P, 256])
    st = sb(scope, "st", [P, 4, H4])
    gn = sb(scope, "gn", [P, HD])
    bk, cf, ident, MIX = v['bk'], v['cf'], v['ident'], v['MIX']
    heads = lambda t, i: U[t][:, i * 512:(i + 1) * 512].rearrange("p (h c) -> p h c", c=P)
    TT_, ATT_, NTt_ = ([heads(t, i) for t in range(NTILE)] for i in range(3))

    dn, pn, an = ["z1", "z2", "z3"], [], []
    ends = {}
    for what, x in ORDER:
        if what == "level":
            tiles, s, levels = x
            if s == 0:
                dn += [f"ns{t}.0" for t in tiles]
                pn += [f"a{t}.0" for t in tiles]
                dn += [f"{n}{t}.0" for t in tiles for n in ("t", "tt", "nn")]
            else:
                pn += [f"a{t}.{s}" for t in tiles] + [f"{n}{t}.{s}" for t in tiles for n in (("b",) if s < levels - 1 else ()) + ("c",)]
                an += [f"m{t}.{s}" for t in tiles]
                dn += [f"nn{t}.{s}" for t in tiles if s < levels - 1]
                dn += [f"{n}{t}.{s}" for t in tiles for n in (("t",) if s < levels - 1 else ()) + ("tt",)]
            continue
        t = x
        if what == "ready0":
            dn += [f"{n}{t}" for n in ("kb", "vb", "gb", "g0", "g1", "g3", "gd", "lt", "tr", "tr2")]
            pn += [f"{n}{t}" for n in ("g", "gr", "T")]
            an += [f"{n}{t}" for n in ("eg", "el", "sl", "L0", "L1", "L2", "L3")]
        if what == "ready1":
            dn += [f"{n}{t}" for n in ("nt0", "nt1", "att0", "att1", "be", "kd")]
            pn += [f"{n}{t}" for n in ("kk", "qk")]
        if what == "state0":
            dn += ([f"qm{i}" for i in range(4)] if t == 4 else []) + [f"{n}{t}" for n in ("ks", "r")]
            pn += [f"ks{t}"]
        if what == "state1":
            dn += [f"vn{t}"]
            pn += [f"vn{t}", f"qs{t}"]
        if what == "state2":
            dn += [f"{n}{t}" for n in ("sp0", "sp1")] + ([f"{n}{t}" for n in ("sm", "s0", "s1")] if t < 4 else ["vm"])
            dn += [f"qs{t}", f"o{t}"]
            pn += [f"av{t}", f"su{t}"] if t < 4 else [f"av{t}"]
        if what == "state3":
            dn += [f"{n}{t}" for n in ("sq", "va", "rc", "n1", "n2", "n3")]
            if t == 4:
                pn += [f"su{t}"]
                dn += [f"ss{i}{j}" for i in range(4) for j in "nms"]
            an += [f"rt{t}"]
        ends[what, t] = dn[-1]

    with stage(["dve_s", "act_s", "pe_s", "loaded", "gl", "outs"]) as (block, (dve_s, act_s, pe_s, loaded, gl, outs)):
        dve, act, pe = Steps(dve_s, dn), Steps(act_s, an), Steps(pe_s, pn)

        W1, W2 = v['W1'], v['W2']

        @block.sync
        def _(e):
            e.dma_start(gn[:, :], A['gdn_norm'][l].partition_broadcast(P)).then_inc(gl, 16)
            dve.wait(e, "z2")
            load_states(e, SS, A['state_gdn'], loaded, l)
            dve.wait(e, "z3")
            for kv in range(2):
                for half in range(2):
                    for r in range(PAIRS):
                        e.dma_start(W1[r * HD:(r + 1) * HD, kv, :, half * HD:(half + 1) * HD],
                                    A['cmp_w1'][l, kv].rearrange("(h s r) d e -> h r d s e", h=2, r=PAIRS)[half, r]).then_inc(outs, 16)
                for g in range(G):
                    e.dma_start(W2[:, kv, g, g * HD:(g + 1) * HD], A['cmp_w2'][l, kv]).then_inc(outs, 16)
            e.dma_start(v['B1'][:, :], A['cmp_b1'][l].rearrange("k e -> e k"), allow_slow_non_contiguous=True).then_inc(outs, 16)
            dve.wait(e, "s13")
            for h in range(H4):
                hp, o = h // 2, (h % 2) * HD
                e.dma_start(O['gdn_prompt'][l, 0, h], S[o:o + HD, hp, o:o + HD]).then_inc(outs, 16)
            dve.wait(e, "ss3s")
            for h in range(H4):
                hp, o = h // 2, (h % 2) * HD
                e.dma_start(O['gdn_sample'][l].rearrange("b h d e -> h d b e")[h], SS[o:o + HD, :, hp, o:o + HD]).then_inc(outs, 16)
            e.wait_ge(outs, (13 + 2 * H4) * 16)

        @block.scalar
        def _(e):
            for what, x in ORDER:
                if what == "level":
                    tiles, s, levels = x
                    for t in tiles if s else ():
                        n = ROWS[t]
                        pe.wait(e, f"a{t}.{s}")
                        act.done(e, f"m{t}.{s}", nc.scalar.activation(M1_[t % 2][0:n, :, 0:n], bk(4 + 2 * (t % 2), 4)[0:n, :, 0:n], ACT.Copy))
                    continue
                t = x
                n, gs = ROWS[t], gs_[:, t]
                if what == "ready0":
                    dve.wait(e, f"gd{t}")
                    act.done(e, f"eg{t}", nc.scalar.activation(gs[0:n, 2, :], gs[0:n, 0, :], ACT.Exp))
                    act.done(e, f"el{t}", nc.scalar.activation(gs[0:n, 4, :], gs[0:n, 5, :], ACT.Exp))
                    pe.wait(e, f"gr{t}")
                    src = bk(1, 4)[:, :, P - 1:P] if t < 4 else bk(1, 4)[:, :, NT - 1:64:NT]
                    act.done(e, f"sl{t}", nc.scalar.activation(SL_[:, t, :, 0:1] if t < 4 else SL_[:, t, :, :], src, ACT.Exp))
                    dve.wait(e, f"lt{t}")
                    for h in range(H4):
                        act.done(e, f"L{h}{t}", nc.scalar.activation(LT[0:n, h, 0:n], LT[0:n, h, 0:n], ACT.Exp, bias=gs[0:n, 1, h:h + 1]))
                if what == "state3":
                    dve.wait(e, f"va{t}")
                    act.done(e, f"rt{t}", nc.scalar.activation(st[0:n, 2, :], st[0:n, 2, :], ACT.Sqrt, scale=1.0 / HD, bias=v['eps'][0:n, :]))

        @block.tensor
        def _(e):
            before = "z2"
            for what, x in ORDER:
                if what == "level":
                    tiles, s, levels = x
                    for t in tiles:
                        n, lane = ROWS[t], t % 2
                        dve.wait(e, f"ns{t}.0" if s == 0 else f"tt{t}.{s-1}" if s > 1 else f"nn{t}.0")
                        for h in range(H4):
                            mm = nc.tensor.matmul(bk(4 + 2 * lane, 4)[0:n, h, 0:n], NTs_[lane][0:n, h, 0:n],
                                                  T_[lane][0:n, h, 0:n] if s else ident[0:n, 0:n], start=True, stop=True)
                        pe.done(e, f"a{t}.{s}", mm)
                    for t in tiles if s else ():
                        n, lane = ROWS[t], t % 2
                        TT, M1 = TT_[t], M1_[lane]
                        act.wait(e, f"m{t}.{s}")
                        if s < levels - 1:
                            for h in range(H4):
                                mm = nc.tensor.matmul(bk(5 + 2 * lane, 4)[0:n, h, 0:n], TT[0:n, h, 0:n], M1[0:n, h, 0:n], start=True, stop=True)
                            pe.done(e, f"b{t}.{s}", mm)
                        for h in range(H4):
                            mm = nc.tensor.matmul(bk(4 + 2 * lane, 4)[0:n, h, 0:n], M1[0:n, h, 0:n], TT[0:n, h, 0:n], start=True, stop=True)
                        pe.done(e, f"c{t}.{s}", mm)
                    continue
                t = x
                n, k, y = ROWS[t], int(t == 4), Y[t]
                QKT, kd, TT, ATT = QKT_[:, t % SETS], kd_[:, t % SETS], TT_[t], ATT_[t]
                tri, same = cf('tri', P)[0:n, k, 0:n], cf('same', P)[0:n, k, 0:n]
                dve.wait(e, before)
                before = ends[what, t]
                if what == "ready0":
                    dve.wait(e, f"gb{t}")
                    nc.tensor.matmul(bk(0)[0:n, 0:4], tri, g_log[0:n, t, :], start=True, stop=True)
                    pe.done(e, f"g{t}", nc.tensor.matmul(bk(0)[0:n, 4:8], same, g_log[0:n, t, :], start=True, stop=True))
                    for h in range(H4):
                        mm = nc.tensor.matmul(bk(1, 4)[:, h, 0:n], gb[0:n, h, :], tri, start=True, stop=True)
                    pe.done(e, f"gr{t}", mm)
                    for i in range(6):
                        src = y[:, i * P:(i + 1) * P] if i < 4 else kb[0:n, (i - 4) * P:(i - 3) * P]
                        mm = nc.tensor.transpose(bk(2 + i // 4, 4)[:, i % 4, 0:n], src, ident[0:n, 0:n])
                    pe.done(e, f"T{t}", mm)
                if what == "ready1":
                    for nm, b, c in (("kk", 2, 4), ("qk", 0, 0)):
                        for h in range(H4):
                            o = (h % 2) * HD
                            mm = nc.tensor.matmul(bk(b + h % 2, 4)[0:n, h // 2, 0:n], QKT[o:o + HD, 2 + h // 2, 0:n], QKT[o:o + HD, c + h // 2, 0:n],
                                                  start=True, stop=True)
                        pe.done(e, f"{nm}{t}", mm)
                if what == "state0":
                    if t < 4:
                        dve.wait(e, f"s1{t-1}" if t else "z1")
                        for hp in range(2):
                            mm = nc.tensor.matmul(bk(0, 4)[0:n, hp, :], QKT[:, 2 + hp, 0:n], S[:, hp, :], start=True, stop=True)
                    else:
                        dve.wait(e, "qm3")
                        e.wait_ge(loaded, H4 * 16)
                        for hp in range(2):
                            for b in range(NB):
                                mm = nc.tensor.matmul(bk(0, 4)[0:n, hp, :], QM[:, 2 + hp, b, :], SS[:, b, hp, :], start=(b == 0), stop=(b == NB - 1))
                    pe.done(e, f"ks{t}", mm)
                if what == "state1":
                    dve.wait(e, f"tt{t}.{LEVELS[t//2]-1}")
                    for h in range(H4):
                        mm = nc.tensor.matmul(bk(1)[0:n, h * HD:(h + 1) * HD], TT[0:n, h, 0:n], T1[0:n, 256 + h * HD:256 + (h + 1) * HD],
                                              start=True, stop=True)
                    pe.done(e, f"vn{t}", mm)
                    for hp in range(2):
                        if t < 4:
                            mm = nc.tensor.matmul(bk(2, 4)[0:n, hp, :], QKT[:, hp, 0:n], S[:, hp, :], start=True, stop=True)
                        else:
                            for b in range(NB):
                                mm = nc.tensor.matmul(bk(2, 4)[0:n, hp, :], QM[:, hp, b, :], SS[:, b, hp, :], start=(b == 0), stop=(b == NB - 1))
                    pe.done(e, f"qs{t}", mm)
                if what == "state2":
                    for h in range(H4):
                        mm = nc.tensor.matmul(bk(3)[0:n, h * HD:(h + 1) * HD], ATT[0:n, h, 0:n], VN[0:n, h * HD:(h + 1) * HD], start=True, stop=True)
                    pe.done(e, f"av{t}", mm)
                    if t < 4:
                        for hp in range(2):
                            mm = nc.tensor.matmul(bk(0, 4)[:, hp, :], kd[0:n, hp * P:(hp + 1) * P], VN[0:n, hp * P:(hp + 1) * P], start=True, stop=True)
                        pe.done(e, f"su{t}", mm)
                if what == "state3" and t == 4:
                    for i in range(4):
                        hp, q = divmod(i, 2)
                        mm = nc.tensor.matmul(bk(4 + i), kd[0:n, hp * P:(hp + 1) * P], VM[0:n, 4 * q:4 * q + 4, hp * P:(hp + 1) * P],
                                              start=True, stop=True)
                    pe.done(e, f"su{t}", mm)

        @block.vector
        def _(e):
            dve.link(e, "z1", nc.vector.memset(S[:, :, :], 0.0))
            dve.link(e, "z2", nc.vector.memset(SS[:, :, :, :], 0.0))
            dve.link(e, "z3", nc.vector.memset(v['W2'][:, :, :, :], 0.0))
            e.wait_ge(gl, 16)
            pair = cf('pair')
            h3 = lambda ap: ap.rearrange("p (h c) -> p h c", c=HD)

            def level_mask(name, t, s):
                n = ROWS[t]
                dve.link(e, name, nc.vector.tensor_tensor(NTs_[t % 2][0:n, :, 0:n], NTt_[t][0:n, :, 0:n],
                                                           b_(cf('level', P)[0:n, s, 0:n], 1, [n, H4, n]), ALU.mult))

            for what, x in ORDER:
                if what == "level":
                    tiles, s, levels = x
                    if s == 0:
                        for t in tiles:
                            level_mask(f"ns{t}.0", t, 0)
                    else:
                        for t in tiles if s < levels - 1 else ():
                            pe.wait(e, f"a{t}.{s}")
                            level_mask(f"nn{t}.{s}", t, s + 1)
                    for t in tiles:
                        n, lane = ROWS[t], t % 2
                        T, TT = T_[lane], TT_[t]
                        eye = b_(ident[0:n, 0:n], 1, [n, H4, n])
                        if s < levels - 1:
                            pe.wait(e, f"b{t}.{s}" if s else f"a{t}.{s}")
                            dve.link(e, f"t{t}.{s}", nc.vector.tensor_tensor(T[0:n, :, 0:n], T[0:n, :, 0:n] if s else eye,
                                                                              bk(5 + 2 * lane if s else 4 + 2 * lane, 4)[0:n, :, 0:n], ALU.subtract))
                        if s:
                            pe.wait(e, f"c{t}.{s}")
                        dve.link(e, f"tt{t}.{s}", nc.vector.tensor_tensor(TT[0:n, :, 0:n], TT[0:n, :, 0:n] if s else eye,
                                                                           bk(4 + 2 * lane, 4)[0:n, :, 0:n] if s else NTs_[lane][0:n, :, 0:n], ALU.subtract))
                        if s == 0:
                            level_mask(f"nn{t}.0", t, 1)
                    continue
                t = x
                u, n, k, y = U[t], ROWS[t], int(t == 4), Y[t]
                QKT, vb, kd, NTt, ATT, gs = QKT_[:, t % SETS], vb_[:, t % SETS], kd_[:, t % SETS], NTt_[t], ATT_[t], gs_[:, t]
                hb = lambda ap: b_(ap, 2, [n, H4, HD])
                if what == "ready0":
                    dve.done(e, f"kb{t}", nc.vector.tensor_tensor(h3(kb[0:n, :]), h3(y[:, 256:512]), hb(u[:, GB:GB + H4]), ALU.mult))
                    dve.done(e, f"vb{t}", nc.vector.tensor_tensor(h3(vb[0:n, :]), h3(y[:, 512:768]), hb(u[:, GB:GB + H4]), ALU.mult))
                    dve.done(e, f"gb{t}", nc.vector.tensor_copy(gb[0:n, :, :], b_(g_log[0:n, t, :], 2, [n, H4, P])))
                    pe.wait(e, f"g{t}")
                    dve.done(e, f"g0{t}", nc.vector.tensor_copy(gs[0:n, 0, :], bk(0)[0:n, 0:4]))
                    dve.done(e, f"g1{t}", nc.vector.tensor_scalar(gs[0:n, 1, :], bk(0)[0:n, 0:4], -1.0, None, ALU.mult))
                    dve.link(e, f"g3{t}", nc.vector.tensor_copy(gs[0:n, 3, :], bk(0)[0:n, 4:8]))
                    dve.link(e, f"gd{t}", nc.vector.tensor_tensor(gs[0:n, 5, :], gs[0:n, 3, :], gs[0:n, 0, :], ALU.subtract))
                    act.wait(e, f"sl{t}")
                    dve.done(e, f"lt{t}", nc.vector.tensor_tensor(LT[0:n, :, 0:n], bk(1, 4)[0:n, :, 0:n],
                                                                   b_(cf('neg', P)[0:n, k, 0:n], 1, [n, H4, n]), ALU.add))
                    pe.wait(e, f"T{t}")
                    dve.done(e, f"tr{t}", nc.vector.tensor_copy(QKT[:, 0:4, 0:n], bk(2, 4)[:, :, 0:n]))
                    dve.done(e, f"tr2{t}", nc.vector.tensor_copy(QKT[:, 4:6, 0:n], bk(3, 4)[:, 0:2, 0:n]))
                if what == "ready1":
                    pe.wait(e, f"kk{t}")
                    act.wait(e, f"L3{t}")
                    for o in range(2):
                        dve.done(e, f"nt{o}{t}", nc.vector.tensor_tensor(NTt[0:n, o::2, 0:n], bk(2 + o, 4)[0:n, 0:2, 0:n], LT[0:n, o::2, 0:n], ALU.mult))
                    pe.wait(e, f"qk{t}")
                    for o in range(2):
                        dve.done(e, f"att{o}{t}", nc.vector.tensor_tensor(ATT[0:n, o::2, 0:n], bk(o, 4)[0:n, 0:2, 0:n], LT[0:n, o::2, 0:n], ALU.mult))
                    dve.done(e, f"be{t}", nc.vector.tensor_tensor(gs[0:n, 6, :], gs[0:n, 2, :], u[:, GB:GB + H4], ALU.mult))
                    dve.link(e, f"kd{t}", nc.vector.tensor_tensor(h3(kd[0:n, :]), h3(y[:, 256:512]), hb(gs[0:n, 4, :]), ALU.mult))
                if what == "state0":
                    for i in range(4) if t == 4 else ():
                        dve.link(e, f"qm{i}", nc.vector.tensor_tensor(QM[:, i, :, :], b_(QKT[:, i, 0:64], 1, [P, NB, 64]), cf('own', 64), ALU.mult))
                    pe.wait(e, f"ks{t}")
                    dve.link(e, f"ks{t}", nc.vector.tensor_tensor(h3(T1[0:n, 0:256]), h3(bk(0)[0:n, 0:256]), hb(gs[0:n, 6, :]), ALU.mult))
                    dve.link(e, f"r{t}", nc.vector.tensor_tensor(T1[0:n, 256:512], vb[0:n, :], T1[0:n, 0:256], ALU.subtract))
                if what == "state1":
                    pe.wait(e, f"vn{t}")
                    dve.link(e, f"vn{t}", nc.vector.tensor_copy(VN[0:n, :], bk(1)[0:n, 0:256]))
                if what == "state2":
                    w = 1 if t < 4 else NB
                    dve.done(e, f"sp0{t}", nc.vector.tensor_copy(SLp[0:64, :, 0:w], SL_[0:64, t, 0::2, 0:w]))
                    dve.link(e, f"sp1{t}", nc.vector.tensor_copy(SLp[64:P, :, 0:w], SL_[64:P, t, 1::2, 0:w]))
                    if t < 4:
                        pe.wait(e, f"su{t}")
                        dve.link(e, f"sm{t}", nc.vector.tensor_tensor(T1[:, 0:256].rearrange("p (a b) -> p a b", a=2), bk(0, 4)[:, 0:2, :],
                                                                       b_(pair, 1, [P, 2, P]), ALU.mult))
                        for hp in range(2):
                            dve.link(e, f"s{hp}{t}", nc.vector.scalar_tensor_tensor(
                                S[:, hp, :], S[:, hp, :], SLp[:, hp, 0:1], T1[:, hp * P:(hp + 1) * P], ALU.mult, ALU.add))
                    else:
                        dve.link(e, "vm", nc.vector.tensor_tensor(VM[0:n, :, :], b_(VN[0:n, :], 1, [n, NB, 256]),
                                                                   b_(cf('ownrow')[0:n, :], 2, [n, NB, 256]), ALU.mult))
                        pe.wait(e, f"qs{t}")
                    dve.link(e, f"qs{t}", nc.vector.tensor_tensor(h3(T1[0:n, 0:256]), h3(bk(2)[0:n, 0:256]), hb(gs[0:n, 2, :]), ALU.mult))
                    pe.wait(e, f"av{t}")
                    dve.link(e, f"o{t}", nc.vector.tensor_tensor(Ot[0:n, :], bk(3)[0:n, 0:256], T1[0:n, 0:256], ALU.add))
                if what == "state3":
                    dve.link(e, f"sq{t}", nc.vector.tensor_tensor(T1[0:n, 0:256], Ot[0:n, :], Ot[0:n, :], ALU.mult))
                    dve.link(e, f"va{t}", nc.vector.tensor_reduce(st[0:n, 2, :], h3(T1[0:n, 0:256]), AX.X, ALU.add))
                    act.wait(e, f"rt{t}")
                    dve.link(e, f"rc{t}", nc.vector.reciprocal(st[0:n, 3, :], st[0:n, 2, :]))
                    dve.link(e, f"n1{t}", nc.vector.tensor_tensor(h3(Ot[0:n, :]), h3(Ot[0:n, :]), hb(st[0:n, 3, :]), ALU.mult))
                    dve.link(e, f"n2{t}", nc.vector.tensor_tensor(h3(Ot[0:n, :]), h3(Ot[0:n, :]), b_(gn[0:n, :], 1, [n, H4, HD]), ALU.mult))
                    dve.link(e, f"n3{t}", nc.vector.tensor_tensor(MIX[0:n, t, 768:1024], Ot[0:n, :], u[:, GG:GG + 256], ALU.mult))
                    if t == 4:
                        pe.wait(e, f"su{t}")
                        for i in range(4):
                            hp, q = divmod(i, 2)
                            t3 = T1[:, :].rearrange("p (a b) -> p a b", a=4)
                            sv = SS[:, 4 * q:4 * q + 4, hp, :]
                            dve.link(e, f"ss{i}n", nc.vector.tensor_tensor(sv, sv, b_(SLp[:, hp, 4 * q:4 * q + 4], 2, [P, 4, P]), ALU.mult))
                            dve.link(e, f"ss{i}m", nc.vector.tensor_tensor(t3, bk(4 + i, 4), b_(pair, 1, [P, 4, P]), ALU.mult))
                            dve.link(e, f"ss{i}s", nc.vector.tensor_tensor(sv, sv, t3, ALU.add))




class Compress:

    RING = 4

    def __init__(self, v, tiles, PC, RP, XT, HT, HS, KC, VC):
        self.v, self.nt, self.PC, self.RP, self.XT, self.HT, self.HS, self.KC, self.VC = v, tiles, PC, RP, XT, HT, HS, KC, VC
        self.ns = tiles * P * PAIRS // SEG
        self.nc = -(-self.ns // P)

    def side_by_side(self, e, dve, pe, i, slot):
        if i >= self.RING:
            pe.wait(e, f"T{i-self.RING}")
        dve.done(e, f"R{i}", nc_(self.v).vector.tensor_copy(
            self.RP[:, i % self.RING, :, :, :].rearrange("p h r d -> p r h d"),
            self.PC[:, slot, :, :].rearrange("p r (h d) -> p r h d", d=HD)))

    def transposes(self, e, pe, act, dve, i):
        dve.wait(e, f"R{i}")
        if i >= 2:
            act.wait(e, f"X{i-2}")
        for h in range(2 * G):
            mm = nc_(self.v).tensor.transpose(self.v['bk'](6 + i % 2, 4)[:, h, :],
                                              self.RP[:, i % self.RING, h, :, :].rearrange("p r d -> p (r d)"), self.v['ident'])
        pe.done(e, f"T{i}", mm)

    def copy_out(self, e, act, pe, i):
        pe.wait(e, f"T{i}")
        act.done(e, f"X{i}", nc_(self.v).scalar.activation(self.XT[:, i, :].rearrange("p (h c) -> p h c", c=P), self.v['bk'](6 + i % 2, 4), ACT.Copy))

    def halves(self, e, pe, act, kv, rows=(0, SEG // PAIRS), tiles=None):
        lo, hi = tiles or (0, self.nt)
        if rows[0] == 0:
            act.wait(e, "HT0" if kv else f"X{hi-1}")
        seg = self.XT[:, lo:hi, :].rearrange("p i (h n s) -> p h i n s", h=2 * G, s=SEG // PAIRS)[:, kv * G:(kv + 1) * G]
        out = self.v['bk'](2)[:, 0:G * self.ns].rearrange("p (g i n) -> p g i n", g=G, i=self.nt)[:, :, lo:hi, :]
        for s in range(*rows):
            mm = nc_(self.v).tensor.matmul(out, self.v['W1'][:, kv, s, :], seg[:, :, :, :, s], start=(s == 0), stop=(s == SEG // PAIRS - 1))
        if rows[1] == SEG // PAIRS and hi == self.nt:
            pe.done(e, f"H{kv}", mm)

    def join(self, e, pe, act, dve, kv):
        ns, ident = self.ns, self.v['ident']
        act.wait(e, f"HT{kv}")
        if kv:
            dve.wait(e, "C0")
        ht = self.HT[:, 0:G * ns].rearrange("p (g n) -> p g n", g=G)
        out = self.v['bk'](3)[0:HD, 0:G * (ns - 1)].rearrange("p (g n) -> p g n", g=G)
        nc_(self.v).tensor.matmul(out, ident[:, 0:HD], ht[:, :, 0:ns - 1], start=True, stop=False)
        pe.done(e, f"J{kv}", nc_(self.v).tensor.matmul(out, ident[:, HD:P], ht[:, :, 1:ns], start=False, stop=True))

    def second(self, e, pe, act, kv):
        v, ns, hs = self.v, self.ns, self.HS
        act.wait(e, f"HS{kv}")
        if kv == 0:
            for g in range(G):
                mm = nc_(v).tensor.matmul(v['bk'](3)[:, 0:ns], v['W2'][:, kv, g, :], hs[:, g, 0:ns], start=(g == 0), stop=(g == G - 1))
        else:
            for c in range(self.nc):
                for g in range(G):
                    mm = nc_(v).tensor.matmul(v['bk'](3)[0:min(P, ns), c * P + g * HD:c * P + (g + 1) * HD],
                                              hs[:, g, c * P:min(ns, (c + 1) * P)], v['W2'][:, kv, 0, 0:HD], start=True, stop=True)
        pe.done(e, f"C{kv}", mm)

    def half_copy(self, e, act, pe, kv):
        pe.wait(e, f"H{kv}")
        if kv:
            pe.wait(e, "J0")
        act.done(e, f"HT{kv}", nc_(self.v).scalar.activation(self.HT[:, 0:G * self.ns], self.v['bk'](2)[:, 0:G * self.ns], ACT.Copy))

    def silu(self, e, act, pe, kv):
        ns = self.ns
        pe.wait(e, f"J{kv}")
        if kv:
            pe.wait(e, "C0")
        act.done(e, f"HS{kv}", nc_(self.v).scalar.activation(
            self.HS[:, :, 0:ns - 1], self.v['bk'](3)[0:HD, 0:G * (ns - 1)].rearrange("p (g n) -> p g n", g=G),
            ACT.Silu, bias=self.v['B1'][:, kv:kv + 1]))

    def keep(self, e, dve, pe, kv):
        pe.wait(e, f"C{kv}")
        m = min(P, self.ns)
        if kv == 0:
            dve.done(e, "C0", nc_(self.v).vector.tensor_copy(self.KC[:, 0:self.ns], self.v['bk'](3)[:, 0:self.ns]))
        else:
            dve.done(e, "C1", nc_(self.v).vector.tensor_copy(self.VC[0:m, 0:self.nc, :], self.v['bk'](3, 4)[0:m, 0:self.nc, :]))


def nc_(v):
    return v['nc']


def prompt_attention(nc, A, O, l, scope, sb, stage, v, U):
    bk, cb, ident, MIX = v['bk'], v['cb'], v['ident'], v['MIX']
    QT = sb(scope, "QT", [P, 2, R, SEQ])
    KT = sb(scope, "KT", [P, G, 2, SEQ])
    KCG = sb(scope, "KCG", [P, G, 32])
    KC = sb(scope, "KCp", [P, 32])
    VC = sb(scope, "VCp", [P, 1, P])
    early = scope.enter_context(ExitStack())
    QRP = sb(early, "QRP", [P, 4, 2, 512])
    PG = sb(early, "PG", [P, 2, PAIRS, 256])
    RP = sb(early, "RPp", [P, 2, 2 * G, PAIRS, HD])
    XT = sb(early, "XTp", [P, 2, 512])
    HT = sb(early, "HTp", [P, 64])
    HS = sb(early, "HSp", [HD, G, 32])
    with stage(["dve_s", "act_s", "pe_s", "rows"]) as (block, (dve_s, act_s, pe_s, rows)):
        cp = Compress(v, 2, PG, RP, XT, HT, HS, KC, VC)
        pe = Steps(pe_s, ["T0", "T1", "H0", "J0", "C0", "H1", "J1", "C1"] + [f"{x}{t}" for t in range(4) for x in ("Tq", "Tr", "Tk")])
        act = Steps(act_s, ["X0", "X1", "HT0", "HS0", "HT1", "HS1"] + [f"Tr{t}" for t in range(4)])
        dve = Steps(dve_s, ["z1", "z2", "z3", "R0", "R1", "C0", "k0", "k1", "C1"] + [f"{x}{t}" for t in range(4) for x in ("Tq", "Tk", "Tl")])

        @block.sync
        def _(e):
            for i in range(2):
                e.dma_start(PG[:, i, :, :], O['kv_prompt'][l, 0].rearrange("(t p r) a g d -> t p r (a g d)", p=P, r=PAIRS)[i, :, :, 0:256]).then_inc(rows, 16)
            e.dma_start(QRP[:, :, :, :].rearrange("p t i c -> p t (i c)"), A['q_rot'].rearrange("(t p) c -> p t c", p=P)).then_inc(rows, 16)

        @block.tensor
        def _(e):
            e.wait_ge(rows, 48)
            for i in range(2):
                cp.transposes(e, pe, act, dve, i)
            for kv in range(2):
                cp.halves(e, pe, act, kv)
                cp.join(e, pe, act, dve, kv)
                cp.second(e, pe, act, kv)
            dve.wait(e, "C1")
            for t in range(4):
                if t:
                    dve.wait(e, f"Tq{t-1}")
                for r in range(R):
                    mm = nc.tensor.transpose(bk(0, 4)[:, r, :], QRP[:, t, 0, r * P:(r + 1) * P], ident)
                pe.done(e, f"Tq{t}", mm)
                if t:
                    act.wait(e, f"Tr{t-1}")
                for r in range(R):
                    mm = nc.tensor.transpose(bk(1, 4)[:, r, :], QRP[:, t, 1, r * P:(r + 1) * P], ident)
                pe.done(e, f"Tr{t}", mm)
                if t:
                    dve.wait(e, f"Tl{t-1}")
                for i in range(2):
                    mm = nc.tensor.transpose(bk(2, 4)[:, i, :], U[t][:, NKV + 256 * (i + 1):NKV + 256 * (i + 1) + P], ident)
                pe.done(e, f"Tk{t}", mm)

        @block.scalar
        def _(e):
            dve.wait(e, "z1")
            for i in range(2):
                cp.copy_out(e, act, pe, i)
            for kv in range(2):
                cp.half_copy(e, act, pe, kv)
                cp.silu(e, act, pe, kv)
            for t in range(4):
                pe.wait(e, f"Tr{t}")
                act.done(e, f"Tr{t}", nc.scalar.activation(QT[:, 1, :, t * P:(t + 1) * P], bk(1, 4), ACT.Copy))

        @block.vector
        def _(e):
            dve.done(e, "z1", nc.vector.memset(HS[:, :, :], 0.0))
            dve.done(e, "z2", nc.vector.memset(KCG[:, :, :], 0.0))
            dve.link(e, "z3", nc.vector.memset(KT[:, :, :, :], 0.0))
            e.wait_ge(rows, 48)
            for i in range(2):
                cp.side_by_side(e, dve, pe, i, i)
            cp.keep(e, dve, pe, 0)
            dve.wait(e, "C0")
            for g in range(G):
                dve.done(e, f"k{g}", nc.vector.tensor_copy(KCG[g * HD:(g + 1) * HD, g, :], KC[g * HD:(g + 1) * HD, :]))
            cp.keep(e, dve, pe, 1)
            for t in range(4):
                pe.wait(e, f"Tq{t}")
                dve.done(e, f"Tq{t}", nc.vector.tensor_copy(QT[:, 0, :, t * P:(t + 1) * P], bk(0, 4)))
                pe.wait(e, f"Tk{t}")
                for g in range(G):
                    dve.done(e, f"T{'kl'[g]}{t}", nc.vector.tensor_copy(KT[g * HD:(g + 1) * HD, g, :, t * P:(t + 1) * P], bk(2, 4)[g * HD:(g + 1) * HD, 0:2, :]))

    early.close()
    DEEP = 4
    sbank = lambda u: bk((0, 1, 6, 7)[u % DEEP])
    Pr = sb(scope, "Pr", [P, DEEP, SEQ])
    PT = sb(scope, "PT", [P, 2, 4, P])
    mx = sb(scope, "mx", [P, DEEP, 2])
    SUM = sb(scope, "SUM", [P, 2, NH])
    fac = sb(scope, "fac", [P, NH])
    T1 = sb(scope, "T1", [P, 512])
    NO = sb(scope, "NO", [P, 512])
    units = [(qt, br, h) for qt in range(4) for br in range(3) for h in range(NH)]
    NU = len(units)
    with stage(["score", "shift", "exped", "turned", "copied_dve", "copied_act", "used", "link_s", "merged"]) as \
            (block, (score, shift, exped, turned, copied_dve, copied_act, used, link_s, merged)):
        copied = [copied_dve, copied_act]

        def keys(u):
            qt, br, h = units[u]
            return NCP if br == 0 else (qt + 1) * P

        def copy(e, u):
            n = keys(u)
            m, k = (n, 1) if n < P else (P, n // P)
            e.wait_ge(turned, u + 1)
            if u >= 2:
                e.wait_ge(used, u - 1)
            o, i = PT[0:m, u % 2, 0:k, :], bk(2 + u % 2, 4)[0:m, 0:k, :]
            (nc.scalar.activation(o, i, ACT.Copy) if u % 2 else nc.vector.tensor_copy(o, i)).then_inc(copied[u % 2], 1)

        @block.tensor
        def _(e):
            def scores(u):
                qt, br, h = units[u]
                g, r, n = h // R, h % R, keys(u)
                if u >= DEEP:
                    e.wait_ge(exped, u - DEEP + 1)
                kt = KCG[:, g, 0:n] if br == 0 else KT[:, g, br - 1, 0:n]
                nc.tensor.matmul(sbank(u)[:, 0:n], QT[:, min(br, 1), r, qt * P:(qt + 1) * P], kt, start=True, stop=False)
                m = cb('cmask', 32)[:, qt, 0:n] if br == 0 else cb('causal')
                nc.tensor.matmul(sbank(u)[:, 0 if br == 0 else qt * P:n], cb('identb'), m, start=False, stop=True).then_inc(score, 1)

            def turn(u):
                n = keys(u)
                e.wait_ge(exped, u + 1)
                if u >= 2:
                    e.wait_ge(copied[u % 2], u // 2)
                for j in range(-(-n // P)):
                    m = min(P, n - j * P)
                    mm = nc.tensor.transpose(bk(2 + u % 2, 4)[0:m, j, :], Pr[:, u % DEEP, j * P:j * P + m], ident)
                mm.then_inc(turned, 1)

            def values(u):
                qt, br, h = units[u]
                g, n, q = h // R, keys(u), u // NH
                e.wait_ge(copied[u % 2], u // 2 + 1)
                if h == 0 and q >= 2:
                    e.wait_ge(merged, q - 1)
                for j in range(-(-n // P)):
                    m = min(P, n - j * P)
                    vv = VC[0:m, 0, g * HD:(g + 1) * HD] if br == 0 else U[j][:, NKV + P + 256 * br + g * HD:NKV + P + 256 * br + (g + 1) * HD]
                    mm = nc.tensor.matmul(bk(4 + q % 2)[:, h * HD:(h + 1) * HD], PT[0:m, u % 2, j, :], vv, start=(j == 0), stop=(j == -(-n // P) - 1))
                mm.then_inc(used, 1)

            for u in range(NU + 3):
                if u < NU:
                    scores(u)
                if 2 <= u < NU + 2:
                    turn(u - 2)
                if u >= 3:
                    values(u - 3)

        @block.scalar
        def _(e):
            for u in range(NU + 2):
                if u >= 2 and u % 2:
                    copy(e, u - 2)
                if u < NU:
                    qt, br, h = units[u]
                    n = keys(u)
                    e.wait_ge(shift, u + 1)
                    if u >= DEEP:
                        e.wait_ge(turned, u - DEEP + 1)
                    nc.scalar.activation(Pr[:, u % DEEP, 0:n], sbank(u)[:, 0:n], ACT.Exp, scale=SCALE, bias=mx[:, u % DEEP, 1:2],
                                         accum_out=SUM[:, (u // NH) % 2, h:h + 1]).then_inc(exped, 1)

        @block.vector
        def _(e):
            links = [0]

            def link(ins):
                links[0] += 1
                ins.then_inc(link_s, 1)
                e.wait_ge(link_s, links[0])

            def biggest(u):
                n = keys(u)
                e.wait_ge(score, u + 1)
                link(nc.vector.tensor_reduce(mx[:, u % DEEP, 0:1], sbank(u)[:, 0:n], AX.X, ALU.max))
                nc.vector.tensor_scalar(mx[:, u % DEEP, 1:2], mx[:, u % DEEP, 0:1], -1e20, -SCALE, ALU.max, ALU.mult).then_inc(shift, 1)

            def merge(u):
                qt, br, h = units[u]
                q = u // NH
                hb = lambda ap: ap.rearrange("p (h c) -> p h c", c=HD)
                e.wait_ge(used, u + 1)
                e.wait_ge(exped, u + 1)
                link(nc.vector.tensor_scalar(fac[:, :], SUM[:, q % 2, :], 1e-30, None, ALU.max))
                link(nc.vector.reciprocal(fac[:, :], fac[:, :]))
                link(nc.vector.tensor_tensor(fac[:, :], fac[:, :], U[qt][:, NGATE + br * NH:NGATE + (br + 1) * NH], ALU.mult))
                dst = NO if br == 0 else T1
                links[0] += 1
                nc.vector.tensor_tensor(hb(dst[:, :]), hb(bk(4 + q % 2)), b_(fac[:, :], 2, [P, NH, HD]), ALU.mult).then_inc(link_s, 1)
                e.wait_ge(link_s, links[0])
                if br:
                    link(nc.vector.tensor_tensor(NO[:, :], NO[:, :], T1[:, :], ALU.add))
                if br == 2:
                    link(nc.vector.tensor_tensor(MIX[:, qt, 256:768], NO[:, :], U[qt][:, NG:NG + 512], ALU.mult))
                nc.vector.engine_nop().then_inc(merged, 1)

            for u in range(NU + 3):
                if u < NU:
                    biggest(u)
                if 2 <= u < NU + 2 and u % 2 == 0:
                    copy(e, u - 2)
                if u >= 3 and (u - 3) % NH == NH - 1:
                    merge(u - 3)


def sample_attention(nc, A, O, l, scope, sb, stage, v):
    bk, cf, cb, ident, MIX, US = v['bk'], v['cf'], v['cb'], v['ident'], v['MIX'], v['US']
    SLOTS = 8
    PC = sb(scope, "PC", [P, SLOTS, PAIRS, 256])
    XT = sb(scope, "XT", [P, GT, 512])
    pc_rows = [[scope.enter_context(nc.semaphore(f"pc_{x}{i}")) for i in range(SLOTS)] for x in ("even", "odd")]
    sel_rows = [[scope.enter_context(nc.semaphore(f"sel_{x}{i}")) for i in range(8)] for x in ("even", "odd")]
    PS = sb(scope, "PS", [P, GT, PAIRS, 256])
    PSg = PS[:, :, :, :].rearrange("p i r c -> p (i r) c")
    HT = sb(scope, "HT", [P, 512])
    HS = sb(scope, "HS", [HD, G, NSEG])
    KC = sb(scope, "KC", [P, NSEG])
    VC = sb(scope, "VC", [P, 2, P])
    PW = sb(scope, "PW", [P, 4, 256])
    PB = sb(scope, "PB", [P, 2 + 5 + NKEYG, COLS])
    QBD = sb(scope, "QBD", [P, 2, NB, COLS])
    QB = sb(scope, "QB", [P, 2, COLS])
    KNT = sb(scope, "KNT", [P, 2, NB * NT])
    KN = sb(scope, "KN", [P, 2, P])
    VN = sb(scope, "VNn", [P, 2, P])
    OT = sb(scope, "OT", [P, 3, R, NB, NT])
    RP = sb(scope, "RP", [P, 4, 2 * G, PAIRS, HD])
    MX = sb(scope, "MX", [P, 2, COLS])
    MQ = sb(scope, "MQ", [P, 4, COLS])
    sm = sb(scope, "sm", [P, 2, 4, COLS])
    PR = sb(scope, "PR", [P, 2, 2, COLS])
    m1 = sb(scope, "m1", [COLS, 2])
    nd = sb(scope, "nd", [COLS, 2, COLS])
    top = sb(scope, "top", [16, 3, NBLK + 1])
    t8 = sb(scope, "t8", [16, 2, 8])
    BT = sb(scope, "BT", [HD, COLS], BF16)
    ids = sb(scope, "ids", [1, 2, (NB + 2) * GT], I32)
    REGS = v['REGS']

    def fetch(e, where, slot, side, page, c, sem):
        e.dma_start(where[side * HD:(side + 1) * HD, slot, :, :],
                    A['cache_nsa_kv'][l, page].rearrange("(p r) a g d -> p r (a g d)", r=PAIRS)[:, :, c:c + 256]).then_inc(sem, 16)

    def first_pages(e, side):
        e.load(REGS[side][0:8], ids[0:1, side, 0:SLOTS])
        for n, r in enumerate(REGS[side][0:8]):
            fetch(e, PC, n, side, e.snap(r), 0, pc_rows[side][n])

    with stage(["dve_s", "pe_s", "kv", "idl"]) as (block, (dve_s, pe_s, kv, idl)):
        dve = Steps(dve_s, ["z0", "z1", "z2", "z3"] + [f"q{i}{g}" for i in range(2) for g in range(G)] + ["k"])
        pe = Steps(pe_s, ["q0", "q1", "k"])

        @block.sync
        def _(e):
            for side in range(2):
                pages = A['page_table'].rearrange("b (n s) -> s (b n)", s=2)[side:side + 1]
                for at, n in ((0, NB * GT), (NB * GT, 2 * GT)):
                    e.dma_start(ids[0:1, side, at:at + n], pages[:, 0:n], allow_slow_non_contiguous=True).then_inc(idl, 16)
            e.dma_start(A['new_kv'].rearrange("b t c -> (b t) c"), US[0:64, NKV:NKV + CW]).then_inc(kv, 16)
            e.wait_ge(idl, 64)
            first_pages(e, 0)
            e.wait_ge(kv, 16)

        @block.gpsimd
        def _(e):
            e.wait_ge(idl, 64)
            first_pages(e, 1)

        @block.tensor
        def _(e):
            for i in range(2):
                for r in range(R):
                    mm = nc.tensor.transpose(bk(i, 8)[:, r, 0:64], v['QRS'][0:64, i, r * P:(r + 1) * P], ident[0:64, 0:64])
                pe.done(e, f"q{i}", mm)
            for i in range(2):
                mm = nc.tensor.transpose(bk(2, 8)[:, i, 0:64], US[0:64, NKV + 256 * (i + 1):NKV + 256 * (i + 1) + P], ident[0:64, 0:64])
            pe.done(e, "k", mm)

        @block.vector
        def _(e):
            dve.done(e, "z0", nc.vector.memset(QBD[:, :, :, :], 0.0))
            dve.done(e, "z1", nc.vector.memset(KN[:, :, :], 0.0))
            dve.done(e, "z2", nc.vector.memset(VN[:, :, :], 0.0))
            dve.link(e, "z3", nc.vector.memset(HS[:, :, :], 0.0))
            for i in range(2):
                pe.wait(e, f"q{i}")
                for g in range(G):
                    o = g * HD
                    dve.done(e, f"q{i}{g}", nc.vector.tensor_copy(
                        QBD[o:o + HD, i, :, g * 32:(g + 1) * 32].rearrange("p b (r t) -> p b r t", r=R),
                        bk(i, 8)[o:o + HD, 0:R, 0:64].rearrange("p r (b t) -> p b r t", b=NB)))
            pe.wait(e, "k")
            dve.done(e, "k", nc.vector.tensor_copy(KNT[:, :, :], bk(2, 8)[:, 0:2, 0:64]))

    B4 = bk(4, 8)
    SEL = 7
    CHAIN = {'w': (bk(5), bk(5), 0), 's': (bk(5), bk(6), 0), 'c': (bk(7), bk(7), 1)}

    def step(b, attend, compress):
        sems = ["dve_s", "act_s", "pe_s"] + (["win_rows"] if attend else [])
        with stage(sems) as (block, got):
            dve_s, act_s, pe_s = got[0:3]
            win_rows = got[3] if attend else None
            cp = Compress(v, GT, PC, RP, XT, HT, HS, KC, VC)
            at = lambda *n: list(n) if attend else []
            co = lambda *n: list(n) if compress else []
            two = lambda x, i: co(f"{x}{i}", f"{x}{i+1}")
            AFTER = {1: ["wt"], 2: ["w4"], 3: ["wmt"], 4: ["wnb"], 6: ["wsb"], 7: ["wpv"]}
            pe = Steps(pe_s, at("kt0") + two("T", 0) +
                       sum([at(f"ks{j}") + (two("T", 2 * j + 2) if j < 7 else []) + at(*AFTER.get(j, [])) for j in range(8)], []) +
                       at("smt", "snb") + co("H0", "J0", "C0", "c4", "cmt") + at("spa") + co("cnb") + at("ssb") + co("csb", "H1", "sc", "J1", "scT") +
                       at("spv") + co("C1", "cpv"))
            act = Steps(act_s, at("kt0") + two("X", 0) +
                        sum([(at(f"kt{j+1}") if j < 7 else []) + (two("X", 2 * j + 2) if j < 7 else []) +
                             at(*{1: ["wt"], 4: ["we"]}.get(j, [])) for j in range(8)], []) +
                        co("HT0") + at("se0", "se1", "se2", "se3") + co("HS0", "ce", "HT1", "HS1"))
            S = lambda j: at(f"S{j}", f"xq{j}")
            dve = Steps(dve_s, co("qp") + at("qb", "kn") + co(*[f"R{i}" for i in range(8)]) + S(0) + two("R", 8) + at("wx0") + two("R", 10) + S(1) +
                        at("wm", "wnd") + two("R", 12) + at("wnm", "ws0") + at("S4") + S(2) + two("R", 14) + at("wps", "wcl", "wrc") + S(3) +
                        at("wo0", "wo1", "sx0", "sx1", "sx2", "sx3", "sm", "snd", "snm", "ss0", "ss1", "ss2", "ss3", "sps") +
                        co("C0", "cx0", "cm", "cnd", "cnm", "cs0", "cps", "ccl", "crc", "pn", "pr0", "pr1") + at("scl", "src") +
                        co("sf", "t1", "r1", "t2", "r2", "bi") + co("bt", "C1") + at("so0", "so1") + co("co0", "co1"))
            here = (lambda n: slice(b * n, (b + 1) * n)) if isinstance(b, int) else (lambda n: bass.ds(b * n, n))
            after = (lambda n: slice((b + 1) * n, (b + 2) * n)) if isinstance(b, int) else (lambda n: bass.ds(b * n + n, n))

            def eight(e, regs, side, n):
                at_ = (b * GT + n) if isinstance(b, int) else bass.ds(b * GT + n, 8)
                e.load(regs, ids[0:1, side, at_:at_ + 8] if isinstance(b, int) else ids[0:1, side, at_])
                return [e.snap(r) for r in regs]

            def ahead(e, side, j, pages):
                dve.wait(e, f"R{j}")
                fetch(e, PC, j % SLOTS, side, pages[j % 8], 0, pc_rows[side][j % SLOTS])

            def selected(e, side, k, pages):
                fetch(e, PS, k, side, pages[k % 8], 256, sel_rows[side][k // 2])

            @block.sync
            def _(e):
                if attend:
                    even, odd = eight(e, REGS[0][0:8], 0, GT // 2), eight(e, REGS[0][8:16], 1, GT // 2)
                if compress:
                    stream = eight(e, REGS[0][16:24], 0, GT + SLOTS)
                for k in range(8):
                    if attend:
                        selected(e, 0, 8 + k, even)
                        if k // 2 % 2 == 0:
                            selected(e, 1, 8 + k, odd)
                    if compress:
                        ahead(e, 0, k, stream)
                    if attend and k == 1:
                        e.dma_start(PW[:, :, :], A['state_nsa_win'][l, b].rearrange("(c p) a g d -> p c (a g d)", p=P)).then_inc(win_rows, 16)
                        for i in range(2):
                            e.dma_start(VN[0:NT, i, :], A['new_kv'][b][:, 256 * (i + 1) + P:256 * (i + 2)]).then_inc(win_rows, 16)
                if compress:
                    stream = eight(e, REGS[0][16:24], 0, GT + SLOTS + 8)
                    even, odd = eight(e, REGS[0][0:8], 0, GT), eight(e, REGS[0][8:16], 1, GT)
                    for k in range(8, GT):
                        ahead(e, 0, k, stream)
                    if attend:
                        pe.wait(e, "spa")
                    for k in range(8):
                        selected(e, 0, k, even)
                        if k // 2 % 2 == 0:
                            selected(e, 1, k, odd)

            @block.gpsimd
            def _(e):
                if attend:
                    odd = eight(e, REGS[1][0:8], 1, GT // 2)
                if compress:
                    stream = eight(e, REGS[1][8:16], 1, GT + SLOTS)
                for k in range(8):
                    if compress:
                        ahead(e, 1, k, stream)
                    if attend and k % 2:
                        selected(e, 1, (10, 11, 14, 15)[k // 2], odd)
                if compress:
                    stream = eight(e, REGS[1][8:16], 1, GT + SLOTS + 8)
                    odd = eight(e, REGS[1][0:8], 1, GT)
                    for k in range(8, GT):
                        ahead(e, 1, k, stream)
                    if attend:
                        pe.wait(e, "spa")
                    for k in (2, 3, 6, 7):
                        selected(e, 1, k, odd)

            @block.tensor
            def _(e):
                def T(i):
                    for k in (i, i + 1) if compress else ():
                        cp.transposes(e, pe, act, dve, k)

                def max_t(a):
                    M, _, s = CHAIN[a]
                    dve.wait(e, f"{a}x0" if a != 's' else "sx3")
                    pe.done(e, f"{a}mt", nc.tensor.transpose(M[0:COLS, 0:P], MX[:, s, :], ident))

                def neg_b(a):
                    M, _, s = CHAIN[a]
                    dve.wait(e, f"{a}nd")
                    pe.done(e, f"{a}nb", nc.tensor.matmul(M[:, P:P + COLS], v['ones'][0:COLS, :], nd[:, s, :], start=True, stop=True))

                def sum_b(a):
                    M, _, s = CHAIN[a]
                    dve.wait(e, f"{a}ps")
                    pe.done(e, f"{a}sb", nc.tensor.matmul(M[:, 192:256], v['ones'][:, :], sm[:, s, 1, :], start=True, stop=True))

                def values(a, lo=0, hi=None):
                    vs, o = {'c': ([VC[:, c, :] for c in range(2)], 0),
                             'w': ([PW[:, c, P:256] for c in range(4)] + [VN[:, 1, :]], 2),
                             's': ([PSg[:, i, P:256] for i in range(2 * GT)] + [VN[:, 0, :]], SEL)}[a]
                    out = CHAIN[a][1][:, 256:320]
                    hi = len(vs) if hi is None else hi
                    for i in range(lo, hi):
                        if a == 's' and (i == lo or i % 8 == 0):
                            act.wait(e, f"se{min(i // 8, 3)}")
                        mm = nc.tensor.matmul(out, vs[i], PB[:, o + i, :], start=(i == 0), stop=(i == len(vs) - 1))
                    if hi in (len(vs), GT):
                        pe.done(e, f"{a}pv" if hi == len(vs) else f"{a}pa", mm)

                def key_t(j):
                    for side in range(2):
                        e.wait_ge(sel_rows[side][j], 32 * (b + 1))
                    if j:
                        act.wait(e, f"kt{j-1}")
                    for c in range(4):
                        mm = nc.tensor.transpose(bk(3, 4)[:, c, :], PSg[:, 4 * j + c, 0:P], ident)
                    return mm

                def key_scores(j):
                    act.wait(e, f"kt{j}")
                    if j + 1 < 8:
                        key_t(j + 1)
                    if j % 2 == 0 and j >= 4:
                        dve.wait(e, f"S{j//2-2}")
                    for c in range(4):
                        i = 4 * j + c
                        mm = nc.tensor.matmul(bk((j // 2) % 2, 8)[:, i % 8, :], PSg[:, i, 0:P], QB[:, 1, :], start=(i % 8 == 0), stop=False,
                                              skip_group_check=True)
                    if j % 2:
                        for t in range(2 * j - 2, 2 * j + 2):
                            mm = nc.tensor.matmul(bk((j // 2) % 2, 8)[:, 2 * (t % 4):2 * (t % 4) + 2, :], cb('blockof', P)[0:HD, t, :],
                                                  b_(BT[:, :], 1, [HD, 2, COLS]), start=False, stop=(t % 4 == 3), skip_group_check=True)
                    pe.done(e, f"ks{j}", mm)

                if attend:
                    dve.wait(e, "kn")
                    pe.done(e, "kt0", key_t(0))
                T(0)
                for j in range(8):
                    if attend:
                        key_scores(j)
                    if j < 7:
                        T(2 * j + 2)
                    if attend and j == 1:
                        e.wait_ge(win_rows, 48)
                        for c in range(4):
                            mm = nc.tensor.transpose(bk(4, 4)[:, c, :], PW[:, c, 0:P], ident)
                        pe.done(e, "wt", mm)
                    if attend and j == 2:
                        act.wait(e, "wt")
                        for c in range(4):
                            nc.tensor.matmul(B4[:, 2 + c, :], PW[:, c, 0:P], QB[:, 1, :], start=True, stop=(c > 0))
                            if c == 0:
                                nc.tensor.matmul(B4[:, 2, :], cb('identb'), cb('winmask'), start=False, stop=True)
                        for i, c in ((1, 6), (0, 7)):
                            nc.tensor.matmul(B4[:, c, :], KN[:, i, :], QB[:, 1, :], start=True, stop=False)
                            mm = nc.tensor.matmul(B4[:, c, :], cb('identb'), cb('newmask'), start=False, stop=True)
                        pe.done(e, "w4", mm)
                    if attend and j == 3:
                        max_t('w')
                    if attend and j == 4:
                        neg_b('w')
                    if attend and j == 6:
                        sum_b('w')
                    if attend and j == 7:
                        dve.wait(e, "wrc")
                        values('w')
                    if compress and 4 <= j < 7:
                        cp.halves(e, pe, act, 0, ((0, 3), (3, 6), (6, 8))[j - 4], (0, GT // 2))
                last = (GT // 2, GT)
                if compress:
                    cp.halves(e, pe, act, 0, (0, 4), last)
                if attend:
                    dve.wait(e, "wo1")
                    max_t('s')
                if compress:
                    cp.halves(e, pe, act, 0, (4, 7), last)
                if attend:
                    neg_b('s')
                if compress:
                    cp.halves(e, pe, act, 0, (7, 8), last)
                    cp.join(e, pe, act, dve, 0)
                    cp.halves(e, pe, act, 1, (0, 3))
                    cp.second(e, pe, act, 0)
                    cp.halves(e, pe, act, 1, (3, 4))
                    dve.wait(e, "C0")
                    if attend:
                        dve.wait(e, "S2")
                    for c in range(2):
                        mm = nc.tensor.matmul(bk(0, 8)[:, c, :], KC[:, c * P:(c + 1) * P], QB[:, 0, :], start=True, stop=(c == 0))
                        if c:
                            mm = nc.tensor.matmul(bk(0, 8)[:, c, :], cb('identb'), cb('padmask'), start=False, stop=True)
                    pe.done(e, "c4", mm)
                if attend:
                    values('s', 0, 8)
                if compress:
                    max_t('c')
                if attend:
                    values('s', 8, GT)
                if compress:
                    neg_b('c')
                if attend:
                    sum_b('s')
                if compress:
                    cp.halves(e, pe, act, 1, (4, 5))
                    sum_b('c')
                    cp.halves(e, pe, act, 1, (5, 8))
                    dve.wait(e, "pr1")
                    for c in range(2):
                        mm = nc.tensor.matmul(bk(7)[0:16, 320:320 + NBLK], PR[:, 1, c, 0:16], cf('overlap', NBLK)[:, c, :], start=(c == 0), stop=(c == 1))
                    pe.done(e, "sc", mm)
                    cp.join(e, pe, act, dve, 1)
                if attend:
                    values('s', GT, GT + 8)
                if compress:
                    dve.wait(e, "bi")
                    pe.done(e, "scT", nc.tensor.transpose(bk(7)[0:HD, 400:416], top[:, 1, 0:HD], ident[0:16, 0:16]))
                if attend:
                    values('s', GT + 8)
                if compress:
                    cp.second(e, pe, act, 1)
                    dve.wait(e, "C1")
                    values('c')

            @block.scalar
            def _(e):
                def X(i):
                    for k in (i, i + 1) if compress else ():
                        cp.copy_out(e, act, pe, k)

                def ex(a, o, n):
                    dve.wait(e, f"{a}s0")
                    ap = PB[:, o:o + n, :]
                    act.done(e, f"{a}e", nc.scalar.activation(ap, ap, ACT.Exp, scale=SCALE))

                def kt(j):
                    pe.wait(e, f"ks{j-1}" if j else "kt0")
                    act.done(e, f"kt{j}", nc.scalar.activation(PSg[:, 4 * j:4 * j + 4, 0:P], bk(3, 4), ACT.Copy))

                if attend:
                    kt(0)
                X(0)
                for j in range(8):
                    if attend and j < 7:
                        kt(j + 1)
                    if j < 7:
                        X(2 * j + 2)
                    if attend and j == 1:
                        pe.wait(e, "wt")
                        act.done(e, "wt", nc.scalar.activation(PW[:, :, 0:P], bk(4, 4), ACT.Copy))
                    if attend and j == 4:
                        ex('w', 2, 5)
                if compress:
                    cp.half_copy(e, act, pe, 0)
                if attend:
                    for q in range(4):
                        dve.wait(e, f"ss{q}")
                        ap = PB[:, SEL + 8 * q:SEL + 8 * q + (8 if q < 3 else 9), :]
                        act.done(e, f"se{q}", nc.scalar.activation(ap, ap, ACT.Exp, scale=SCALE))
                if compress:
                    cp.silu(e, act, pe, 0)
                    ex('c', 0, 2)
                    cp.half_copy(e, act, pe, 1)
                    cp.silu(e, act, pe, 1)

            @block.vector
            def _(e):
                def Rr(a, z):
                    for i in range(a, z) if compress else ():
                        for side in range(2):
                            e.wait_ge(pc_rows[side][i % SLOTS], 16 * (2 * (b + 1) + i // SLOTS + 1))
                        cp.side_by_side(e, dve, pe, i, i % SLOTS)

                def biggest(a, src):
                    dve.link(e, f"{a}x0", nc.vector.tensor_reduce(MX[:, CHAIN[a][2], :], src.rearrange("p n c -> p c n"), AX.X, ALU.max))

                def to_row(a):
                    M, _, s = CHAIN[a]
                    pe.wait(e, f"{a}mt")
                    dve.link(e, f"{a}m", nc.vector.tensor_reduce(m1[:, s:s + 1], M[0:COLS, 0:P], AX.X, ALU.max))
                    dve.link(e, f"{a}nd", nc.vector.tensor_scalar(nd[:, s, :], ident[0:COLS, 0:COLS], m1[:, s:s + 1], -1.0, ALU.mult, ALU.mult))

                def shift(a, src, o, n):
                    M, _, s = CHAIN[a]
                    pe.wait(e, f"{a}nb")
                    dve.link(e, f"{a}nm", nc.vector.tensor_copy(sm[:, s, 0, :], M[:, P:P + COLS]))
                    dve.done(e, f"{a}s0", nc.vector.tensor_tensor(PB[:, o:o + n, :], src, b_(sm[:, s, 0, :], 1, [P, n, COLS]), ALU.add))

                def keep_scores(j):
                    pe.wait(e, f"ks{2*j+1}")
                    ap = PB[:, SEL + 8 * j:SEL + 8 * j + 8, :]
                    dve.link(e, f"S{j}", nc.vector.tensor_copy(ap, bk(j % 2, 8)))
                    dve.done(e, f"xq{j}", nc.vector.tensor_reduce(MQ[:, j, :], ap.rearrange("p n c -> p c n"), AX.X, ALU.max))

                def sums(a, o, n):
                    act.wait(e, f"{a}e" if a != 's' else "se3")
                    dve.link(e, f"{a}ps", nc.vector.tensor_reduce(sm[:, CHAIN[a][2], 1, :], PB[:, o:o + n, :].rearrange("p n c -> p c n"), AX.X, ALU.add))

                def inverse(a):
                    M, _, s = CHAIN[a]
                    pe.wait(e, f"{a}sb")
                    dve.link(e, f"{a}cl", nc.vector.tensor_scalar(sm[:, s, 2, :], M[:, 192:256], 1e-30, None, ALU.max))
                    dve.link(e, f"{a}rc", nc.vector.reciprocal(sm[:, s, 3, :], sm[:, s, 2, :]))

                def outs(a, br, where):
                    pe.wait(e, f"{a}pv")
                    _, V, s = CHAIN[a]
                    for g in range(G):
                        o = g * HD
                        dve.link(e, f"{a}{'o'}{g}", nc.vector.tensor_tensor(OT[o:o + HD, br, :, where, :].rearrange("p r b t -> p r (b t)"),
                                                                         V[o:o + HD, 256 + g * 32:256 + (g + 1) * 32].rearrange("p (r t) -> p r t", r=R),
                                                                         sm[o:o + HD, s, 3, g * 32:(g + 1) * 32].rearrange("p (r t) -> p r t", r=R), ALU.mult))

                if compress:
                    dve.done(e, "qp", nc.vector.tensor_copy(QB[:, 0, :], QBD[:, 0, after(1), :].rearrange("p b c -> p (b c)")))
                if attend:
                    dve.done(e, "qb", nc.vector.tensor_copy(QB[:, 1, :], QBD[:, 1, here(1), :].rearrange("p b c -> p (b c)")))
                    dve.done(e, "kn", nc.vector.tensor_copy(KN[:, :, 0:NT], KNT[:, :, here(NT)]))
                Rr(0, 8)
                if attend:
                    keep_scores(0)
                Rr(8, 10)
                if attend:
                    pe.wait(e, "w4")
                    biggest('w', B4[:, 2:7, :])
                Rr(10, 12)
                if attend:
                    keep_scores(1)
                    to_row('w')
                Rr(12, 14)
                if attend:
                    shift('w', B4[:, 2:7, :], 2, 5)
                    dve.done(e, "S4", nc.vector.tensor_copy(PB[:, SEL + 2 * GT, :], B4[:, 7, :]))
                    keep_scores(2)
                Rr(14, 16)
                if attend:
                    sums('w', 2, 5)
                    inverse('w')
                    keep_scores(3)
                    outs('w', 2, here(1))
                    dve.link(e, "sx0", nc.vector.tensor_tensor(MX[:, 0, :], MQ[:, 0, :], PB[:, SEL + 2 * GT, :], ALU.max))
                    for q in range(1, 4):
                        dve.link(e, f"sx{q}", nc.vector.tensor_tensor(MX[:, 0, :], MX[:, 0, :], MQ[:, q, :], ALU.max))
                    to_row('s')
                    pe.wait(e, "snb")
                    dve.link(e, "snm", nc.vector.tensor_copy(sm[:, 0, 0, :], bk(5)[:, P:P + COLS]))
                    for q in range(4):
                        n = 8 if q < 3 else 9
                        ap = PB[:, SEL + 8 * q:SEL + 8 * q + n, :]
                        dve.done(e, f"ss{q}", nc.vector.tensor_tensor(ap, ap, b_(sm[:, 0, 0, :], 1, [P, n, COLS]), ALU.add))
                    sums('s', SEL, NKEYG)
                if compress:
                    cp.keep(e, dve, pe, 0)
                    pe.wait(e, "c4")
                    C = bk(0, 8)[:, 0:2, :]
                    biggest('c', C)
                    to_row('c')
                    shift('c', C, 0, 2)
                    sums('c', 0, 2)
                    inverse('c')
                    dve.link(e, "pn", nc.vector.tensor_tensor(PR[:, 0, :, :], PB[:, 0:2, :], b_(sm[:, 1, 3, :], 1, [P, 2, COLS]), ALU.mult))
                    for c in range(2):
                        dve.done(e, f"pr{c}", nc.vector.tensor_reduce(PR[:, 1, c, 0:16].rearrange("p (g t) -> p g t", g=G),
                                                                       PR[:, 0, c, :].rearrange("p (g r t) -> p g t r", g=G, r=R), AX.X, ALU.add))
                if attend:
                    inverse('s')
                if compress:
                    pe.wait(e, "sc")
                    dve.link(e, "sf", nc.vector.tensor_tensor(top[:, 0, 0:NBLK], bk(7)[0:16, 320:320 + NBLK], cf('force')[0:16, :], ALU.add))
                    dve.link(e, "t1", nc.vector.max(t8[:, 0, :], top[:, 0, 0:NBLK]))
                    dve.link(e, "r1", nc.vector.match_replace(top[:, 1, 0:NBLK], t8[:, 0, :], top[:, 0, 0:NBLK], -1.0))
                    dve.link(e, "t2", nc.vector.max(t8[:, 1, :], top[:, 1, 0:NBLK]))
                    dve.link(e, "r2", nc.vector.match_replace(top[:, 2, 0:NBLK], t8[:, 1, :], top[:, 1, 0:NBLK], -1.0))
                    dve.link(e, "bi", nc.vector.tensor_scalar(top[:, 1, 0:NBLK], top[:, 2, 0:NBLK], -0.5, NEG, ALU.is_gt, ALU.mult))
                if compress:
                    pe.wait(e, "scT")
                    dve.link(e, "bt", nc.vector.tensor_copy(BT[:, :].rearrange("p (g r t) -> p g r t", g=G, r=R),
                                                             bk(7)[0:HD, 400:416].rearrange("p (g t) -> p g t", g=G).unsqueeze(2).broadcast_to([HD, G, R, NT])))
                    cp.keep(e, dve, pe, 1)
                if attend:
                    outs('s', 1, here(1))
                if compress:
                    outs('c', 0, after(1))

    step(-1, False, True)
    with nc.Fori(0, NB - 1) as b:
        step(b, True, True)
    step(NB - 1, True, False)

    with stage([]) as (block, _):
        @block.sync
        def _(e):
            for s in pc_rows[0] + pc_rows[1]:
                e.wait_ge(s, 16 * (2 * NB + 1))
            for s in sel_rows[0] + sel_rows[1]:
                e.wait_ge(s, 32 * NB)
    nc.gpsimd.dma_reset()
    for s in pc_rows[0] + pc_rows[1] + sel_rows[0] + sel_rows[1]:
        nc.gpsimd.sem_clear(s)
    nc.all_engine_barrier()

    NO = sb(scope, "NOs", [64, 3, 512])
    with stage(["dve_s", "pe_s"]) as (block, (dve_s, pe_s)):
        dve = Steps(dve_s, ["m0", "m1", "a1", "m2", "a2", "mix"])
        pe = Steps(pe_s, ["t0", "t1", "t2"])

        @block.tensor
        def _(e):
            for i in range(3):
                for r in range(R):
                    mm = nc.tensor.transpose(bk(i, 4)[0:64, r, :], OT[:, i, r, :, :].rearrange("p b t -> p (b t)"), ident)
                pe.done(e, f"t{i}", mm)

        @block.vector
        def _(e):
            for i in range(3):
                pe.wait(e, f"t{i}")
                dve.link(e, f"m{i}", nc.vector.tensor_tensor(
                    NO[:, i, :].rearrange("p (g r d) -> p g r d", g=G, r=R), bk(i)[0:64, :].rearrange("p (r g d) -> p g r d", r=R, g=G),
                    US[0:64, NGATE + i * NH:NGATE + (i + 1) * NH].rearrange("p (g r) -> p g r", g=G).unsqueeze(3).broadcast_to([64, G, R, HD]), ALU.mult))
                if i:
                    dve.link(e, f"a{i}", nc.vector.tensor_tensor(NO[:, 0, :], NO[:, 0, :], NO[:, i, :], ALU.add))
            dve.link(e, "mix", nc.vector.tensor_tensor(MIX[0:64, 4, 256:768], NO[:, 0, :], US[0:64, NG:NG + 512], ALU.mult))


def out_project(nc, A, l, scope, sb, stage, v):
    X, MIX, ident, bk = v['X'], v['MIX'], v['ident'], v['bk']
    mT = sb(scope, "mT", [P, KD, 4 * P + 64])
    W = sb(scope, "Wo", [P, KD, D])
    YO = sb(scope, "YO", [P, 2, D])
    sq = sb(scope, "sq", [P, D])
    ss = sb(scope, "ss", [P, NTILE])
    gpost = sb(scope, "gpost", [P, D])
    with stage(["w_half", "gain", "act_s", "dve_s", "pe_s"]) as (block, (w_half, gain, act_s, dve_s, pe_s)):
        pe = Steps(pe_s, [f"T{t}" for t in range(NTILE)] + [f"{x}{t}" for t in range(NTILE) for x in ("y0", "y1")])
        dve = Steps(dve_s, [f"{x}{t}" for t in range(NTILE) for x in ("m0", "m1")] + [f"{x}{t}" for t in range(NTILE) for x in ("rc", "g", "x")])
        act = Steps(act_s, [f"{x}{t}" for t in range(NTILE) for x in ("c0", "c1", "sq", "rt")])

        @block.sync
        def _(e):
            e.dma_start(gpost[:, :], A['norm_post'][l].partition_broadcast(P)).then_inc(gain, 16)
            wv = A['w_out'][l].rearrange("(k p) c -> p k c", p=P)
            for h in range(2):
                e.dma_start(W[:, :, h * 512:(h + 1) * 512], wv[:, :, h * 512:(h + 1) * 512]).then_inc(w_half, 16)

        @block.tensor
        def _(e):
            for t in range(NTILE):
                n = ROWS[t]
                if t >= 2:
                    dve.wait(e, f"m1{t-2}")
                for k in range(KD):
                    mm = nc.tensor.transpose(bk(2 * (t % 2) + k // 4, 4)[:, k % 4, 0:n], MIX[0:n, t, k * P:(k + 1) * P], ident[0:n, 0:n])
                pe.done(e, f"T{t}", mm)
            e.wait_ge(w_half, 32)
            for t in range(NTILE):
                n = ROWS[t]
                dve.wait(e, f"m1{t}")
                if t >= 2:
                    act.wait(e, f"c1{t-2}")
                for h in range(2):
                    for k in range(KD):
                        mm = nc.tensor.matmul(bk(4 + 2 * (t % 2) + h)[0:n, :], mT[:, k, t * P:t * P + n], W[:, k, h * 512:(h + 1) * 512],
                                              start=(k == 0), stop=(k == KD - 1))
                    pe.done(e, f"y{h}{t}", mm)

        @block.scalar
        def _(e):
            for t in range(NTILE):
                n = ROWS[t]
                if t >= 2:
                    dve.wait(e, f"x{t-2}")
                for h in range(2):
                    pe.wait(e, f"y{h}{t}")
                    act.link(e, f"c{h}{t}", nc.scalar.activation(YO[0:n, t % 2, h * 512:(h + 1) * 512], bk(4 + 2 * (t % 2) + h)[0:n, :], ACT.Copy))
                act.link(e, f"sq{t}", nc.scalar.activation(sq[0:n, :], YO[0:n, t % 2, :], ACT.Square, accum_out=ss[0:n, t:t + 1]))
                act.link(e, f"rt{t}", nc.scalar.activation(ss[0:n, t:t + 1], ss[0:n, t:t + 1], ACT.Sqrt, scale=1.0 / D, bias=v['eps'][0:n, :]))

        @block.vector
        def _(e):
            for t in range(NTILE):
                n = ROWS[t]
                pe.wait(e, f"T{t}")
                for h in range(2):
                    dve.done(e, f"m{h}{t}", nc.vector.tensor_copy(mT[:, 4 * h:4 * h + 4, t * P:t * P + n], bk(2 * (t % 2) + h, 4)[:, :, 0:n]))
            e.wait_ge(gain, 16)
            for t in range(NTILE):
                n = ROWS[t]
                y = YO[0:n, t % 2, :]
                act.wait(e, f"rt{t}")
                dve.link(e, f"rc{t}", nc.vector.reciprocal(ss[0:n, t:t + 1], ss[0:n, t:t + 1]))
                dve.link(e, f"g{t}", nc.vector.scalar_tensor_tensor(y, y, ss[0:n, t:t + 1], gpost[0:n, :], ALU.mult, ALU.mult))
                dve.link(e, f"x{t}", nc.vector.tensor_tensor(X[0:n, t, :], X[0:n, t, :], y, ALU.add))



INPUTS = ['x_prompt', 'x_sample', 'cache_nsa_kv', 'page_table', 'state_nsa_win', 'state_ret', 'state_gdn', 'state_gdn_conv',
          'w_in', 'w_out', 'norm_pre', 'norm_post', 'ret_gn', 'gdn_norm', 'gdn_conv', 'gdn_a_log', 'gdn_dt_bias',
          'cmp_w1', 'cmp_b1', 'cmp_w2']
OUTPUTS = [('y_prompt', (1, SEQ, D)), ('y_sample', (NB, NT, D)),
           ('kv_prompt', (DEPTH, 1, SEQ, 4, G, HD)), ('kv_sample', (DEPTH, NB, NT, 4, G, HD)),
           ('win_prompt', (DEPTH, 1, WIN, 2, G, HD)), ('win_sample', (DEPTH, NB, WIN, 2, G, HD)),
           ('ret_prompt', (DEPTH, 1, H4, HD, HD)), ('ret_sample', (DEPTH, NB, H4, HD, HD)),
           ('gdn_prompt', (DEPTH, 1, H4, HD, HD)), ('gdn_sample', (DEPTH, NB, H4, HD, HD)),
           ('conv_prompt', (DEPTH, 1, CONV - 1, CW)), ('conv_sample', (DEPTH, NB, CONV - 1, CW))]
SCRATCH = [('conv_p', (SEQ + 3, CW)), ('conv_s', (NB, NT + 3, CW)), ('q_rot', (SEQ, 1024)), ('new_kv', (NB, NT, CW))]


def kernel(**inputs):
    import ml_dtypes
    import concourse.bacc as bacc
    from concourse.bass_utils import run_bass_kernel_spmd

    nc = bacc.Bacc("TRN2", target_bir_lowering=False, num_devices=1)
    arrays = {n: np.ascontiguousarray(inputs[n]) for n in INPUTS}
    c = constants()
    arrays['cf'] = np.concatenate([c[n] for n in KEPT], 1)
    arrays['ce'] = np.concatenate([a for n, a in c.items() if n not in KEPT], 1)
    arrays['cb'] = np.concatenate(list(bf_constants().values()), 1).astype(ml_dtypes.bfloat16)
    A = {n: nc.dram_tensor(f"in_{n}", a.shape, mybir.dt.from_np(a.dtype), kind="ExternalInput").ap() for n, a in arrays.items()}
    O = {n: nc.dram_tensor(f"out_{n}", s, F32, kind="ExternalOutput").ap() for n, s in OUTPUTS}
    for n, s in SCRATCH:
        A[n] = nc.dram_tensor(f"scratch_{n}", s, F32, kind="Internal").ap()
    build(nc, A, O)
    r = run_bass_kernel_spmd(nc, [{f"in_{n}": a for n, a in arrays.items()}], core_ids=[0])
    return tuple(r.results[0][f"out_{n}"] for n, _ in OUTPUTS)
```
